# Optimizing a Trainium2 kernel written in Bass

```python
import math
import jax, jax.numpy as jnp
from jax import lax
import numpy as np

D_MODEL = 1024
BATCH = 1
SEQ = 256
DEPTH = 1
DEC_BATCH = 8
DEC_SEQ = 8
PAST_LEN = 2048
PAGE_SIZE = 128

D_SSM = D_MODEL // 2
SSM_GROUP = 16
N_GROUPS = D_SSM // SSM_GROUP
SSM_STATE = 64
ML_HEADS = 4
ML_DK = 128
ML_DV = 128
D_ML = ML_HEADS * ML_DV
ML_CHUNK = 64
N_EXPERTS = 32
TOP_K = 4
D_EXPERT = D_MODEL
SWIGLU_LIMIT = 7.0
SWIGLU_ALPHA = 1.702
MOE_BLOCK = 128
D_PLE = 256
RMS_EPS = 1e-6
D_IN = D_SSM + 4 * D_ML + 2 * ML_HEADS + 2 * D_MODEL

kernel_name = 'hybrid_s5_mlstm_moe_step'

def rmsnorm(x, g):
    xf = x.astype(jnp.float32)
    y = xf * lax.rsqrt(jnp.mean(xf * xf, axis=-1, keepdims=True) + RMS_EPS)
    return (y * g.astype(jnp.float32)).astype(x.dtype)

def _cplx_affine(e1, e2):
    a1r, a1i, b1r, b1i = e1
    a2r, a2i, b2r, b2i = e2
    return (a2r * a1r - a2i * a1i, a2r * a1i + a2i * a1r,
            a2r * b1r - a2i * b1i + b2r, a2r * b1i + a2i * b1r + b2i)

def s5_mixer(u, h0_re, h0_im, a_re, a_im, log_dt, b_re, b_im, c_re, c_im, d_skip, w_glu, b_glu):
    f32 = jnp.float32
    a_re, a_im, log_dt = a_re.astype(f32), a_im.astype(f32), log_dt.astype(f32)
    b_re, b_im, c_re, c_im = b_re.astype(f32), b_im.astype(f32), c_re.astype(f32), c_im.astype(f32)
    bsz, L, _ = u.shape
    ug = u.reshape(bsz, L, N_GROUPS, SSM_GROUP)
    dt = jnp.exp(log_dt)[:, None]
    mag = jnp.exp(a_re * dt)
    abar_r, abar_i = mag * jnp.cos(a_im * dt), mag * jnp.sin(a_im * dt)
    den = a_re * a_re + a_im * a_im
    nr, ni = abar_r - 1.0, abar_i
    coef_r = (nr * a_re + ni * a_im) / den
    coef_i = (ni * a_re - nr * a_im) / den
    bbar_r = coef_r[..., None] * b_re - coef_i[..., None] * b_im
    bbar_i = coef_r[..., None] * b_im + coef_i[..., None] * b_re
    bu_r = jnp.einsum('blgh,gph->blgp', ug, bbar_r)
    bu_i = jnp.einsum('blgh,gph->blgp', ug, bbar_i)
    h0_re, h0_im = h0_re.astype(f32), h0_im.astype(f32)
    bu_r = bu_r.at[:, 0].add(abar_r * h0_re - abar_i * h0_im)
    bu_i = bu_i.at[:, 0].add(abar_r * h0_im + abar_i * h0_re)
    ar = jnp.broadcast_to(abar_r, bu_r.shape)
    ai = jnp.broadcast_to(abar_i, bu_i.shape)
    _, _, xr, xi = lax.associative_scan(_cplx_affine, (ar, ai, bu_r, bu_i), axis=1)
    y = (jnp.einsum('blgp,ghp->blgh', xr, c_re) - jnp.einsum('blgp,ghp->blgh', xi, c_im)
         + d_skip.astype(f32) * ug)
    y = jax.nn.gelu(y.reshape(bsz, L, D_SSM))
    y = y * jax.nn.sigmoid(y @ w_glu.astype(f32) + b_glu.astype(f32))
    return y, xr[:, -1], xi[:, -1]

def mlstm_mixer(q, k, v, ig, fg, o, c0, n0, m0):
    bsz, L = q.shape[0], q.shape[1]
    lc = math.gcd(L, ML_CHUNK)
    nc = L // lc
    logf = jax.nn.log_sigmoid(fg)
    k = k * (ML_DK ** -0.5)

    def to_chunks(t):
        t = t.reshape((bsz, nc, lc) + t.shape[2:])
        return jnp.moveaxis(t, (1, 3), (0, 2))

    causal = jnp.tril(jnp.ones((lc, lc), dtype=bool))

    def step(carry, xs):
        C, n, m = carry
        qc, kc, vc, ic, fc = xs
        b = jnp.cumsum(fc, axis=-1)
        dmat = b[..., :, None] - b[..., None, :] + ic[..., None, :]
        dmat = jnp.where(causal, dmat, -jnp.inf)
        inter = b + m[..., None]
        mt = jnp.maximum(inter, jnp.max(dmat, axis=-1))
        w_in = jnp.exp(dmat - mt[..., None])
        w_out = jnp.exp(inter - mt)
        s = jnp.einsum('bhtd,bhsd->bhts', qc, kc) * w_in
        num = (w_out[..., None] * jnp.einsum('bhtd,bhde->bhte', qc, C)
               + jnp.einsum('bhts,bhse->bhte', s, vc))
        qn = w_out * jnp.einsum('bhtd,bhd->bht', qc, n) + jnp.sum(s, axis=-1)
        h = num / jnp.maximum(jnp.abs(qn), jnp.exp(-mt))[..., None]
        m_end = mt[..., -1]
        decay = jnp.exp(b[..., -1] + m - m_end)
        ws = jnp.exp(b[..., -1:] - b + ic - m_end[..., None])
        C_new = decay[..., None, None] * C + jnp.einsum('bhs,bhsd,bhse->bhde', ws, kc, vc)
        n_new = decay[..., None] * n + jnp.einsum('bhs,bhsd->bhd', ws, kc)
        return (C_new, n_new, m_end), h

    xs = (to_chunks(q), to_chunks(k), to_chunks(v), to_chunks(ig), to_chunks(logf))
    carry0 = (c0.astype(jnp.float32), n0.astype(jnp.float32), m0.astype(jnp.float32))
    (C, n, m), hs = lax.scan(step, carry0, xs)
    hs = jnp.moveaxis(hs, (0, 2), (1, 3)).reshape(bsz, L, D_ML)
    return jax.nn.sigmoid(o) * hs, C, n, m

def moe_ffn(x, w_router, b_router, w_gate, b_gate, w_up, b_up, w_down, b_down):
    shape = x.shape
    xt = x.reshape(-1, shape[-1])
    n_tok = xt.shape[0]
    logits = (xt @ w_router + b_router).astype(jnp.float32)
    top_val, top_idx = lax.top_k(logits, TOP_K)
    top_w = jax.nn.softmax(top_val, axis=-1)
    n_assign = n_tok * TOP_K
    flat_e = top_idx.reshape(-1)
    flat_tok = jnp.repeat(jnp.arange(n_tok, dtype=jnp.int32), TOP_K)
    flat_w = top_w.reshape(-1)
    order = jnp.argsort(flat_e)
    sorted_e = flat_e[order]
    counts = jnp.zeros((N_EXPERTS,), jnp.int32).at[flat_e].add(1)
    padded = (counts + MOE_BLOCK - 1) // MOE_BLOCK * MOE_BLOCK
    pad_end = jnp.cumsum(padded)
    pad_start = pad_end - padded
    start = jnp.cumsum(counts) - counts
    rank = jnp.arange(n_assign, dtype=jnp.int32) - start[sorted_e]
    dest = pad_start[sorted_e] + rank
    n_blocks = -(-(n_assign + N_EXPERTS * (MOE_BLOCK - 1)) // MOE_BLOCK)
    n_rows = n_blocks * MOE_BLOCK
    row_tok = jnp.zeros((n_rows,), jnp.int32).at[dest].set(flat_tok[order])
    row_w = jnp.zeros((n_rows,), jnp.float32).at[dest].set(flat_w[order])
    block_e = jnp.minimum(
        jnp.searchsorted(pad_end, jnp.arange(n_blocks, dtype=jnp.int32) * MOE_BLOCK, side='right'),
        N_EXPERTS - 1)

    def expert_block(args):
        tok, e = args
        xb = xt[tok]
        g = xb @ w_gate[e] + b_gate[e]
        u = xb @ w_up[e] + b_up[e]
        g = jnp.minimum(g, SWIGLU_LIMIT)
        u = jnp.clip(u, -SWIGLU_LIMIT, SWIGLU_LIMIT)
        return (g * jax.nn.sigmoid(SWIGLU_ALPHA * g) * (u + 1.0)) @ w_down[e] + b_down[e]

    rows = lax.map(expert_block, (row_tok.reshape(n_blocks, MOE_BLOCK), block_e))
    rows = rows.reshape(n_rows, -1) * row_w[:, None].astype(rows.dtype)
    out = jnp.zeros_like(xt).at[row_tok].add(rows.astype(xt.dtype))
    return out.reshape(shape)

def trunk(x, p, s_re, s_im, s_c, s_n, s_m,
          g_mix, w_in, ssm_a_re, ssm_a_im, ssm_log_dt, ssm_b_re, ssm_b_im, ssm_c_re, ssm_c_im,
          ssm_d, ssm_w_glu, ssm_b_glu, ml_b_ig, ml_b_fg, w_ssm_up, w_ml_up, w_out,
          g_ffn, w_router, b_router, w_gate, b_gate, w_up, b_up, w_down, b_down,
          g_ple, w_ple_gate, w_ple_proj, g_final):
    h = x
    bsz, L = x.shape[0], x.shape[1]
    splits = list(np.cumsum([D_SSM, D_ML, D_ML, D_ML, D_ML, ML_HEADS, ML_HEADS, D_MODEL]))
    o_re, o_im, o_c, o_n, o_m = [], [], [], [], []
    for i in range(DEPTH):
        hn = rmsnorm(h, g_mix[i])
        z = (hn @ w_in[i]).astype(jnp.float32)
        u, q, k, v, o, ig, fg, gs, gm = jnp.split(z, splits, axis=-1)
        ys, nre, nim = s5_mixer(u, s_re[i], s_im[i], ssm_a_re[i], ssm_a_im[i], ssm_log_dt[i],
                                ssm_b_re[i], ssm_b_im[i], ssm_c_re[i], ssm_c_im[i], ssm_d[i],
                                ssm_w_glu[i], ssm_b_glu[i])
        heads = lambda t: t.reshape(bsz, L, ML_HEADS, -1)
        ym, nC, nN, nM = mlstm_mixer(heads(q), heads(k), heads(v),
                                     ig + ml_b_ig[i].astype(jnp.float32),
                                     fg + ml_b_fg[i].astype(jnp.float32),
                                     o, s_c[i], s_n[i], s_m[i])
        merged = (jax.nn.sigmoid(gs) * (ys @ w_ssm_up[i].astype(jnp.float32))
                  + jax.nn.sigmoid(gm) * (ym @ w_ml_up[i].astype(jnp.float32)))
        h = h + (merged @ w_out[i].astype(jnp.float32)).astype(h.dtype)
        h = h + moe_ffn(rmsnorm(h, g_ffn[i]), w_router[i], b_router[i], w_gate[i], b_gate[i],
                        w_up[i], b_up[i], w_down[i], b_down[i])
        gate = jax.nn.sigmoid(rmsnorm(h, g_ple[i]) @ w_ple_gate[i])
        h = h + gate * (p[i] @ w_ple_proj[i])
        o_re.append(nre); o_im.append(nim); o_c.append(nC); o_n.append(nN); o_m.append(nM)
    y = rmsnorm(h, g_final)
    return (y, jnp.stack(o_re), jnp.stack(o_im), jnp.stack(o_c), jnp.stack(o_n), jnp.stack(o_m))

def setup_inputs(seed: int = 0) -> dict:
    key = jax.random.key(seed)
    kit = iter(jax.random.split(key, 64))
    f32 = jnp.float32
    nrm = lambda shape, scale: scale * jax.random.normal(next(kit), shape, f32)
    P, G, H = SSM_STATE, N_GROUPS, ML_HEADS
    inp = {}
    inp['x_prompt'] = nrm((BATCH, SEQ, D_MODEL), 1.0)
    inp['x_sample'] = nrm((DEC_BATCH, DEC_SEQ, D_MODEL), 1.0)
    inp['p_prompt'] = nrm((DEPTH, BATCH, SEQ, D_PLE), 1.0)
    inp['p_sample'] = nrm((DEPTH, DEC_BATCH, DEC_SEQ, D_PLE), 1.0)
    inp['state_ssm_re'] = nrm((DEPTH, DEC_BATCH, G, P), 0.3)
    inp['state_ssm_im'] = nrm((DEPTH, DEC_BATCH, G, P), 0.3)
    inp['state_ml_c'] = nrm((DEPTH, DEC_BATCH, H, ML_DK, ML_DV), 0.1)
    inp['state_ml_n'] = nrm((DEPTH, DEC_BATCH, H, ML_DK), 0.1)
    inp['state_ml_m'] = nrm((DEPTH, DEC_BATCH, H), 1.0)
    inp['g_mix'] = 1.0 + nrm((DEPTH, D_MODEL), 0.02)
    inp['w_in'] = nrm((DEPTH, D_MODEL, D_IN), D_MODEL ** -0.5)
    inp['ssm_a_re'] = -0.5 + nrm((DEPTH, G, P), 0.01)
    inp['ssm_a_im'] = jnp.pi * jnp.arange(P, dtype=f32) + nrm((DEPTH, G, P), 0.01)
    inp['ssm_log_dt'] = jax.random.uniform(next(kit), (DEPTH, G), f32, math.log(1e-3), math.log(1e-1))
    inp['ssm_b_re'] = nrm((DEPTH, G, P, SSM_GROUP), (2 * SSM_GROUP) ** -0.5)
    inp['ssm_b_im'] = nrm((DEPTH, G, P, SSM_GROUP), (2 * SSM_GROUP) ** -0.5)
    inp['ssm_c_re'] = nrm((DEPTH, G, SSM_GROUP, P), (2 * P) ** -0.5)
    inp['ssm_c_im'] = nrm((DEPTH, G, SSM_GROUP, P), (2 * P) ** -0.5)
    inp['ssm_d'] = nrm((DEPTH, G, SSM_GROUP), 1.0)
    inp['ssm_w_glu'] = nrm((DEPTH, D_SSM, D_SSM), D_SSM ** -0.5)
    inp['ssm_b_glu'] = nrm((DEPTH, D_SSM), 0.01)
    inp['ml_b_ig'] = -1.0 + nrm((DEPTH, H), 0.1)
    inp['ml_b_fg'] = jnp.linspace(3.0, 6.0, H, dtype=f32) + nrm((DEPTH, H), 0.1)
    inp['w_ssm_up'] = nrm((DEPTH, D_SSM, D_MODEL), D_SSM ** -0.5)
    inp['w_ml_up'] = nrm((DEPTH, D_ML, D_MODEL), D_ML ** -0.5)
    inp['w_out'] = nrm((DEPTH, D_MODEL, D_MODEL), D_MODEL ** -0.5)
    inp['g_ffn'] = 1.0 + nrm((DEPTH, D_MODEL), 0.02)
    inp['w_router'] = nrm((DEPTH, D_MODEL, N_EXPERTS), D_MODEL ** -0.5)
    inp['b_router'] = nrm((DEPTH, N_EXPERTS), 0.01)
    inp['w_gate'] = nrm((DEPTH, N_EXPERTS, D_MODEL, D_EXPERT), D_MODEL ** -0.5)
    inp['b_gate'] = nrm((DEPTH, N_EXPERTS, D_EXPERT), 0.01)
    inp['w_up'] = nrm((DEPTH, N_EXPERTS, D_MODEL, D_EXPERT), D_MODEL ** -0.5)
    inp['b_up'] = nrm((DEPTH, N_EXPERTS, D_EXPERT), 0.01)
    inp['w_down'] = nrm((DEPTH, N_EXPERTS, D_EXPERT, D_MODEL), D_EXPERT ** -0.5)
    inp['b_down'] = nrm((DEPTH, N_EXPERTS, D_MODEL), 0.01)
    inp['g_ple'] = 1.0 + nrm((DEPTH, D_MODEL), 0.02)
    inp['w_ple_gate'] = nrm((DEPTH, D_MODEL, D_MODEL), D_MODEL ** -0.5)
    inp['w_ple_proj'] = nrm((DEPTH, D_PLE, D_MODEL), D_PLE ** -0.5)
    inp['g_final'] = 1.0 + nrm((D_MODEL,), 0.02)
    return inp

def reference(x_prompt, x_sample, p_prompt, p_sample, state_ssm_re, state_ssm_im, state_ml_c,
              state_ml_n, state_ml_m, g_mix, w_in, ssm_a_re, ssm_a_im, ssm_log_dt, ssm_b_re,
              ssm_b_im, ssm_c_re, ssm_c_im, ssm_d, ssm_w_glu, ssm_b_glu, ml_b_ig, ml_b_fg,
              w_ssm_up, w_ml_up, w_out, g_ffn, w_router, b_router, w_gate, b_gate, w_up, b_up,
              w_down, b_down, g_ple, w_ple_gate, w_ple_proj, g_final):
    f32 = jnp.float32
    weights = (g_mix, w_in, ssm_a_re, ssm_a_im, ssm_log_dt, ssm_b_re, ssm_b_im, ssm_c_re, ssm_c_im,
               ssm_d, ssm_w_glu, ssm_b_glu, ml_b_ig, ml_b_fg, w_ssm_up, w_ml_up, w_out,
               g_ffn, w_router, b_router, w_gate, b_gate, w_up, b_up, w_down, b_down,
               g_ple, w_ple_gate, w_ple_proj, g_final)
    bp = x_prompt.shape[0]
    z_re = jnp.zeros((DEPTH, bp, N_GROUPS, SSM_STATE), f32)
    z_c = jnp.zeros((DEPTH, bp, ML_HEADS, ML_DK, ML_DV), f32)
    z_n = jnp.zeros((DEPTH, bp, ML_HEADS, ML_DK), f32)
    z_m = jnp.zeros((DEPTH, bp, ML_HEADS), f32)
    y_prompt, re_p, im_p, c_p, n_p, m_p = trunk(x_prompt, p_prompt, z_re, z_re, z_c, z_n, z_m, *weights)
    y_sample, re_s, im_s, c_s, n_s, m_s = trunk(x_sample, p_sample, state_ssm_re, state_ssm_im,
                                                state_ml_c, state_ml_n, state_ml_m, *weights)
    return (y_prompt, y_sample, re_p, im_p, c_p, n_p, m_p, re_s, im_s, c_s, n_s, m_s)


_drawn_inputs = setup_inputs


def setup_inputs(seed=0):
    import zlib

    import numpy as np

    out = dict(_drawn_inputs(seed))
    spreads = {}
    factors = {'ssm_a_re': 18.293,
     'ssm_b_glu': 8.0,
     'ml_b_ig': 3.053,
     'b_router': 3.429,
     'b_gate': 8.0,
     'b_up': 8.0,
     'b_down': 8.0,
     'g_ple': 43.541,
     'g_final': 8.257}
    for name, (base, spread) in spreads.items():
        noise = np.random.default_rng([zlib.crc32(name.encode()), seed]).standard_normal(out[name].shape)
        drawn = base * np.exp(spread * noise) if base else spread * noise
        out[name] = __import__('jax').numpy.asarray(drawn.astype(out[name].dtype))
    for name, factor in factors.items():
        out[name] = (out[name] * factor).astype(out[name].dtype)
    return out
```

```python
from contextlib import ExitStack

import concourse.bass as bass
from concourse import mybir

F32 = mybir.dt.float32
I32 = mybir.dt.int32
ALU = mybir.AluOpType
ACT = mybir.ActivationFunctionType
AX = mybir.AxisListType

P = 128
D = 1024
KD = D // P
NP_TOK, NB, LB = 256, 8, 8
NT = NP_TOK + NB * LB
TT = 3
TW = [128, 128, 64]
G, ST, GW = 32, 64, 16
NJ, NI = 4, 4
NK = NJ * NI
H = 4
NE = 32
SLOTS = 64
EXTRA = 20
RING, SW = 12, 2048
ZT = 36
ZG = 6
ZU, ZQ, ZK, ZV, ZO, ZGS, ZGM = 0, 4, 8, 12, 16, 20, 28
EPS = 1e-6
KSCALE = float(P) ** -0.5
TWO_PI = 6.2831845
ROUND = 12582912.0
LIMIT, ALPHA = 7.0, 1.702

CONST = {}
_at = 0
for _name, _n in (("ident", P), ("ones", P), ("triu", P), ("slot", SLOTS), ("tloc", NT), ("amask", 448),
                  ("seqm", NB), ("half", 2), ("par", 2), ("npar", 2), ("imask", NI), ("start", NT),
                  ("sel", H * P), ("pidx", 1), ("halfpi", 1), ("eps", 1)):
    CONST[_name] = (_at, _at + _n)
    _at += _n
CONST_W = _at


def hybrid_step(nc, t, o):
    ctx = ExitStack()
    with ctx:
        def sb(name, shape, dt=F32):
            return ctx.enter_context(nc.sbuf_tensor(name, shape, dt))

        def sem(name):
            return ctx.enter_context(nc.semaphore(name))

        bank = [ctx.enter_context(nc.psum_tensor(f"bank{i}", [P, 512], F32)) for i in range(8)]

        ring = sb("ring", [P, RING * SW])
        zT = sb("zT", [P, ZT * NT])
        hnT = sb("hnT", [P, KD * NT])
        xkv = sb("xkv", [P, TT * D])
        cst = sb("cst", [P, CONST_W])
        BT = sb("BT", [P, 2, NJ, P])
        CT = sb("CT", [P, 2, NJ, P])
        rows = sb("rows", [P, 704])
        hrow = sb("hrow", [H, 7 * 384])
        att = sb("att", [P, 1664])
        small = sb("small", [P, 1280])
        cnt_i = sb("cnt_i", [1, 1 + EXTRA], I32)

        def slot(s, n=SW):
            return ring[:, s * SW:s * SW + n]

        def c(name, n=None):
            a, b = CONST[name]
            return cst[:, a:b]

        def Z(n, m=1):
            return zT[:, n * NT:(n + m) * NT]

        def zz(a, n):
            return zT[:, a:a + n]

        ident = c("ident")
        ones = c("ones")
        x3 = xkv[:, :].rearrange("p (t d) -> p t d", t=TT)
        hn3 = hnT[:, :].rearrange("p (k n) -> p k n", k=KD)

        s5 = 6 * SW
        JW = NI * NT

        def S(n, w=JW):
            return ring[:, s5 + n:s5 + n + w]

        bu_r, bu_i, t1, t2, XR, XI, rho4, um, fb = (S(n * JW) for n in range(9))
        vec_rows, h0_rows_r, h0_rows_i, n_rows = (S(9 * JW + n * P, P) for n in range(4))
        tabc, tabs = xkv[:, 0:JW], xkv[:, JW:2 * JW]
        pz = 24 * NT
        so = BT[:, 0].rearrange("p j q -> p (j q)")
        bn_r, bn_i, bb_r, bb_i, btmp = (zz(pz + 256 * n, 256) for n in range(5))
        Bx = zz(pz + 1280, 1024)
        cn = zz(pz + 2304, 512)
        Cx = zz(pz + 2816, 1024)

        at = [0]

        def sm(w):
            at[0] += w
            return small[:, at[0] - w:at[0]]

        vec = sm(80)
        V_LDT, V_ARE, V_AIM, V_GMIX, V_GFFN, V_GPLE, V_D, V_BGLU = 0, 16, 32, 48, 56, 64, 72, 76

        def v(off, n):
            return vec[:, off:off + n]

        ssq, rstd = sm(4), sm(4)
        dt_, adr, mag, fr, fr_r = sm(16), sm(16), sm(16), sm(32), sm(32)
        sc = sm(32)
        ab_r, ab_i, nr, den, co_r, co_i, tm = (sm(16) for _ in range(7))
        h0T = sm(256)
        ah = sm(256)
        n0T = sm(36)
        fin_s = sm(256)
        fin_p = sm(32)
        asT = sm(24)
        gb = sm(2)
        m09 = sm(9)
        brb = sm(32)
        assert at[0] <= 1280, at

        v_tok = xkv[:, 0:TT * 512].rearrange("p (t d) -> p t d", t=TT)
        ig, lf, bb, mm, arow, wrow, tmpr = (hrow[0:H, 384 * n:384 * n + 384] for n in range(7))
        et, den_a, bc, qw, qn, kw = (att[:, 0:448], att[:, 448:768], att[:, 768:1152], att[:, 1152:1216],
                                     att[:, 1216:1280], att[:, 1280:1664])
        C0 = ring[:, 8 * SW:10 * SW].rearrange("p (h b e) -> p h b e", h=H, b=NB)
        vx = xkv[:, TT * 512:TT * 512 + NB * P].rearrange("p (b e) -> p b e", b=NB)
        ysT2 = hnT[:, 0:4 * NT]
        sgl = hnT[:, 4 * NT:8 * NT]

        acc = zz(0, TT * D).rearrange("p (t d) -> p t d", t=TT)
        btab = zz(3072, 3 * D)
        wr_sb = zz(6144, 256)
        mg, ms, mu = (zz(6400 + 512 * n, 512) for n in range(3))
        m0_ = 28 * NT
        sel = zz(m0_, 192).rearrange("p (t s) -> p t s", t=TT)
        selw = zz(m0_ + 192, 384).rearrange("p (t a s) -> p t a s", t=TT, a=2)
        onehot = zz(m0_ + 576, 64)
        p_lo, p_hi = zz(m0_ + 640, 384), zz(m0_ + 1024, 384)
        rk = zz(m0_ + 1408, 99).rearrange("p (t e) -> p t e", t=TT)
        wt = zz(m0_ + 1507, 99).rearrange("p (t e) -> p t e", t=TT)
        lg, msk, gtm, eqm, exw = (zz(m0_ + 1606 + 96 * n, 96).rearrange("p (t e) -> p t e", t=TT)
                                  for n in range(5))
        mtop = zz(m0_ + 2086, 24).rearrange("p (t e) -> p t e", t=TT)
        mcol = zz(m0_ + 2110, 12)
        nov, cinc, ind = (zz(m0_ + 2122 + 32 * n, 32) for n in range(3))
        opass = zz(m0_ + 2218, 4)
        dtab = zz(m0_ + 2222, 2 * EXTRA)
        obase = zz(m0_ + 2262, EXTRA)
        islot = zz(m0_ + 2282, SLOTS)
        xs, xsT, hT, yb, hb = (hnT[:, 512 * n:512 * n + 512] for n in range(5))
        pproj = zz(3072, TT * D).rearrange("p (t d) -> p t d", t=TT)
        gfin = ring[:, 8 * SW:8 * SW + D]
        p_tok = ring[:, 9 * SW:9 * SW + TT * 256].rearrange("p (t d) -> p t d", t=TT)
        pT = ring[:, 10 * SW:10 * SW + 2 * 384].rearrange("p (k n) -> p k n", k=2)

        slot_full = [sem(f"slot_full{s}") for s in range(RING)]
        slot_free = [sem(f"slot_free{s}") for s in range(RING)]
        cst_full, x_full, vec_full, wif_full = sem("cst_full"), sem("x_full"), sem("vec_full"), sem("wif_full")
        bn_full, st_full, gb_full, c0_full = sem("bn_full"), sem("st_full"), sem("gb_full"), sem("c0_full")
        bt_full, wr_full, res_full, ple_full, gfin_full = (sem(n) for n in (
            "bt_full", "wr_full", "res_full", "ple_full", "gfin_full"))
        stored, stored_pool = sem("stored"), sem("stored_pool")
        zeroed = sem("zeroed")
        ssq_ready, sd_ready = sem("ssq_ready"), sem("sd_ready")
        xn_ready, xT_done, hnT_ready = sem("xn_ready"), sem("xT_done"), sem("hnT_ready")
        vecT_done, vec_ready = sem("vecT_done"), sem("vec_ready")
        ldt_ready = sem("ldt_ready")
        par_act, par_dve = sem("par_act"), sem("par_dve")
        bx_ready, bxT_done, bct_ready = sem("bx_ready"), sem("bxT_done"), sem("bct_ready")
        stT_done, stT_ready = sem("stT_done"), sem("stT_ready")
        z_done, z_ready = sem("z_done"), sem("z_ready")
        gate_done, gate_rows, gate_act, row_ready, R_ready = (sem(n) for n in (
            "gate_done", "gate_rows", "gate_act", "row_ready", "R_ready"))
        asT_done, asT_ready = sem("asT_done"), sem("asT_ready")
        fb_ready, fb_red, tab_ready, um_ready = (sem(n) for n in (
            "fb_ready", "fb_red", "tab_ready", "um_ready"))
        bu_done, bu_ready, rotin_done, rotout_done, s5d = (sem(n) for n in (
            "bu_done", "bu_ready", "rotin_done", "rotout_done", "s5d"))
        fin_ready, finT_done, finT_ready = sem("fin_ready"), sem("finT_done"), sem("finT_ready")
        y_done, yd_ready, gelu_ready, glu_done, sgl_ready, ys_ready = (sem(n) for n in (
            "y_done", "yd_ready", "gelu_ready", "glu_done", "sgl_ready", "ys_ready"))
        g_sig = sem("g_sig")
        vT_done, v_ready = sem("vT_done"), sem("v_ready")
        E_done, bc_done, bc_ready, em_ready, ex_ready, S_done, P_ready = (sem(n) for n in (
            "E_done", "bc_done", "bc_ready", "em_ready", "ex_ready", "S_done", "P_ready"))
        qw_ready, qn_ready, N_done, den_done, ym_ready = (sem(n) for n in (
            "qw_ready", "qn_ready", "N_done", "den_done", "ym_ready"))
        kT_done, kw_ready, vx_ready, C_done, C_ready, att_d = (sem(n) for n in (
            "kT_done", "kw_ready", "vx_ready", "C_done", "C_ready", "att_d"))
        abs_ready = sem("abs_ready")
        cp_ready, nT_done, nT_ready = sem("cp_ready"), sem("nT_done"), sem("nT_ready")
        up_done, up_dve, merged = sem("up_done"), sem("up_dve"), sem("merged")
        out_done, h_ready = sem("out_done"), sem("h_ready")
        ch = sem("dve_chain")
        ach = sem("act_chain")
        rl_done, rl_ready, mask_ready, rank_done, tab_made = (sem(n) for n in (
            "rl_done", "rl_ready", "mask_ready", "rank_done", "tab_made"))
        wtT_done, wtT_ready, bd_done, acc_ready = (sem(n) for n in (
            "wtT_done", "wtT_ready", "bd_done", "acc_ready"))
        ob_done, cnt_ready = sem("ob_done"), sem("cnt_ready")
        sel_ready, selw_ready, oh_ready = sem("sel_ready"), sem("selw_ready"), sem("oh_ready")
        gath_done, xs_ready, xsT_done, xsT_ready = (sem(n) for n in (
            "gath_done", "xs_ready", "xsT_done", "xsT_ready"))
        g_done, u_done, g_ready, s_ready, u_ready, gu_ready, hb_ready = (sem(n) for n in (
            "g_done", "u_done", "g_ready", "s_ready", "u_ready", "gu_ready", "hb_ready"))
        hTt_done, hT_ready, pw_done, pw_ready, dn_done, y_ready, sc_done, acc_add = (sem(n) for n in (
            "hTt_done", "hT_ready", "pw_done", "pw_ready", "dn_done", "y_ready", "sc_done", "acc_add"))
        pj_done, pj_ready, pTt_done, pT_ready = (sem(n) for n in (
            "pj_done", "pj_ready", "pTt_done", "pT_ready"))
        gt_done, gt_sig, fin_h, out_ready = sem("gt_done"), sem("gt_sig"), sem("fin_h"), sem("out_ready")

        block = ctx.enter_context(nc.Block())

        w_in = t["w_in"][0].rearrange("(k p) n -> p k n", p=P)

        def zcol(ch_):
            return 256 * ch_ if ch_ < 10 else 2568 + 256 * (ch_ - 10)

        def w3(s, k, n):
            return ring[:, s * SW:s * SW + k * n].rearrange("p (k n) -> p k n", k=k)

        wexp = [t[n][0].rearrange("e (k p) n -> e p k n", p=P) for n in ("w_gate", "w_up", "w_down")]
        FREE0 = [4, 4, 4, 4, 4, 3, 1, 1, 1, 1, 1, 1]

        @block.sync
        def _(sp):
            sp.dma_start(cst[:, :], t["cst"]).then_inc(cst_full, 16)
            xp = t["x_prompt"][0].rearrange("(t p) d -> p t d", p=P)
            xd = t["x_sample"].rearrange("b l d -> (b l) d")
            sp.dma_start(x3[:, 0:2, :], xp).then_inc(x_full, 16)
            sp.dma_start(x3[0:64, 2, :], xd).then_inc(x_full, 16)

            def load_z(ch_):
                s = ch_ % ZG
                if ch_ >= ZG:
                    sp.wait_ge(slot_free[s], ch_ // ZG)
                sp.dma_start(w3(s, KD, 256), w_in[:, :, zcol(ch_):zcol(ch_) + 256]).then_inc(slot_full[s], 16)

            for ch_ in range(18):
                load_z(ch_)
            sp.wait_ge(y_done, NJ)
            sp.wait_ge(fin_ready, 4 * NJ)
            for h in range(H):
                sp.dma_start(C0[:, h], t["state_ml_c"][0, :, h].rearrange("b d e -> d b e")).then_inc(c0_full, 16)
            sp.dma_start(w3(6, 2, D), t["w_ssm_up"][0, 0:256].rearrange("(k p) n -> p k n", p=P)).then_inc(slot_full[6], 16)
            sp.dma_start(w3(7, 2, D), t["w_ssm_up"][0, 256:512].rearrange("(k p) n -> p k n", p=P)).then_inc(slot_full[7], 16)
            sp.dma_start(w3(10, 2, D), t["w_ml_up"][0, 0:256].rearrange("(k p) n -> p k n", p=P)).then_inc(slot_full[10], 16)
            sp.dma_start(w3(11, 2, D), t["w_ml_up"][0, 256:512].rearrange("(k p) n -> p k n", p=P)).then_inc(slot_full[11], 16)
            sp.wait_ge(slot_free[4], 3)
            sp.dma_start(w3(4, 4, 512), t["ssm_w_glu"][0].rearrange("(k p) n -> p k n", p=P)).then_inc(slot_full[4], 16)
            for s in range(4):
                sp.wait_ge(slot_free[s], 3)
                sp.dma_start(w3(s, 2, D), t["w_out"][0, 256 * s:256 * s + 256].rearrange("(k p) n -> p k n", p=P)).then_inc(slot_full[s], 16)
            for h in range(H):
                sp.wait_ge(C_ready, h + 1)
                sp.dma_start(o["cs"][0, :, h].rearrange("b d e -> d b e"), C0[:, h]).then_inc(stored, 16)
            sp.wait_ge(ym_ready, H)
            sp.wait_ge(ys_ready, 4)
            sp.wait_ge(kT_done, H)
            sp.wait_ge(up_done, 2 * KD)
            sp.dma_start(acc[:, 0:2, :], xp).then_inc(res_full, 16)
            sp.dma_start(acc[0:64, 2, :], xd).then_inc(res_full, 16)
            sp.wait_ge(zeroed, 5)
            for n, name in enumerate(("b_gate", "b_up", "b_down")):
                sp.dma_start(btab[0:NE, n * D:(n + 1) * D], t[name][0]).then_inc(bt_full, 16)
            sp.dma_start(wr_sb.rearrange("p (k e) -> p k e", k=KD), t["w_router"][0].rearrange("(k p) e -> p k e", p=P)).then_inc(wr_full, 16)
            sp.wait_ge(stored, 16 * H)

            def load_pass(e, n, first=()):
                for s in range(RING):
                    sp.wait_ge(slot_free[s], n + FREE0[s])
                    k = 2 * (s % 4)
                    sp.dma_start(w3(s, 2, D), wexp[s // 4][bass.ds(e, 1), :, k:k + 2, :].rearrange("a p k n -> (a p) k n")).then_inc(slot_full[s], 16)

            with sp.Fori(0, NE) as p:
                load_pass(p, p)
            sp.wait_ge(cnt_ready, 1)
            extra = sp.value_load(cnt_i[0:1, 0:1], min_val=0, max_val=EXTRA)
            with sp.If(extra > 0):
                with sp.Fori(0, extra) as q:
                    e = sp.value_load(cnt_i[0:1, bass.ds(q + 1, 1)], min_val=0, max_val=NE - 1)
                    load_pass(e, q + NE)
            for s in range(4):
                sp.wait_ge(slot_free[s], extra + (NE + FREE0[s]))
                sp.dma_start(w3(s, 2, D), t["w_ple_gate"][0, 256 * s:256 * s + 256].rearrange("(k p) n -> p k n", p=P)).then_inc(slot_full[s], 16)
            sp.wait_ge(slot_free[4], extra + (NE + FREE0[4]))
            sp.dma_start(w3(4, 2, D), t["w_ple_proj"][0].rearrange("(k p) n -> p k n", p=P)).then_inc(slot_full[4], 16)
            for s in (8, 9, 10):
                sp.wait_ge(slot_free[s], extra + (NE + FREE0[s]))
            sp.dma_start(gfin, t["g_final"].rearrange("(a n) -> a n", a=1).to_broadcast([P, D])).then_inc(gfin_full, 16)
            sp.dma_start(p_tok[:, 0:2, :], t["p_prompt"][0, 0].rearrange("(t p) d -> p t d", p=P)).then_inc(ple_full, 16)
            sp.dma_start(p_tok[0:64, 2, :], t["p_sample"][0].rearrange("b l d -> (b l) d")).then_inc(ple_full, 16)
            yp = o["yp"][0].rearrange("(t p) d -> t p d", p=P)
            for tt in range(TT):
                sp.wait_ge(out_ready, tt + 1)
                if tt < 2:
                    sp.dma_start(yp[tt], acc[:, tt, :]).then_inc(stored, 16)
                else:
                    sp.dma_start(o["ys"].rearrange("b l d -> (b l) d"), acc[0:64, 2, :]).then_inc(stored, 16)
            sp.wait_ge(stored, 16 * (H + TT))
            sp.wait_ge(stored_pool, 16 * 9)

        @block.gpsimd
        def _(pool):
            ms_ = nc.gpsimd.memset
            ms_(xkv[64:128, 2 * D:3 * D], 0.0).then_inc(zeroed, 1)
            pool.wait_ge(zeroed, 1)
            ms_(rows[:, :], 0.0).then_inc(zeroed, 1)
            pool.wait_ge(zeroed, 2)
            ms_(hrow[0:H, 4 * 384:6 * 384], 0.0).then_inc(zeroed, 1)
            pool.wait_ge(zeroed, 3)
            fl = "(a b) -> a b"
            for r0, name, n in ((V_ARE, "ssm_a_re", 16), (V_AIM, "ssm_a_im", 16)):
                pool.dma_start(vec_rows[r0:r0 + n, :], t[name][0].rearrange("(k g) s -> k (g s)", g=2)).then_inc(vec_full, 16)
            for r0, name in ((V_GMIX, "g_mix"), (V_GFFN, "g_ffn"), (V_GPLE, "g_ple")):
                pool.dma_start(vec_rows[r0:r0 + 8, :], t[name][0].rearrange(fl, b=P)).then_inc(vec_full, 16)
            pool.dma_start(vec_rows[V_D:V_D + 4, :], t["ssm_d"][0].rearrange("(j g) h -> j (g h)", g=8)).then_inc(vec_full, 16)
            pool.dma_start(vec_rows[V_BGLU:V_BGLU + 4, :], t["ssm_b_glu"][0].rearrange(fl, b=P)).then_inc(vec_full, 16)
            pool.dma_start(ssq[0:16, 0:2], t["ssm_log_dt"][0].rearrange("(k g) -> k g", g=2)).then_inc(vec_full, 16)
            for n, name in enumerate(("ssm_b_re", "ssm_b_im")):
                src = t[name][0].rearrange("g s h -> (g s) h").rearrange("(k q) h -> q k h", q=P)
                pool.dma_start((bn_r, bn_i)[n].rearrange("p (k h) -> p k h", k=NK), src).then_inc(bn_full, 16)
            for n, name in enumerate(("ssm_c_re", "ssm_c_im")):
                src = t[name][0].rearrange("g h s -> (g h) s").rearrange("(j q) s -> q j s", q=P)
                pool.dma_start(cn[:, 256 * n:256 * n + 256].rearrange("p (j s) -> p j s", j=NJ), src).then_inc(bn_full, 16)
            pool.dma_start(h0_rows_r, t["state_ssm_re"][0].rearrange("b g s -> b (g s)").rearrange("b (k q) -> b k q", q=P).rearrange("b k q -> (b k) q")).then_inc(st_full, 16)
            pool.dma_start(h0_rows_i, t["state_ssm_im"][0].rearrange("b g s -> b (g s)").rearrange("b (k q) -> b k q", q=P).rearrange("b k q -> (b k) q")).then_inc(st_full, 16)
            pool.dma_start(n_rows[0:32, :], t["state_ml_n"][0].rearrange("b h d -> (b h) d")).then_inc(st_full, 16)
            pool.dma_start(gb[0:H, 0:1], t["ml_b_ig"][0].rearrange("(a b) -> a b", b=1)).then_inc(gb_full, 16)
            pool.dma_start(gb[0:H, 1:2], t["ml_b_fg"][0].rearrange("(a b) -> a b", b=1)).then_inc(gb_full, 16)
            pool.dma_start(m09[0:H, 1:9], t["state_ml_m"][0].rearrange("b h -> h b"), allow_slow_non_contiguous=True).then_inc(gb_full, 16)
            pool.dma_start(brb, t["b_router"].to_broadcast([P, NE])).then_inc(gb_full, 16)
            wif = att[:, 0:KD * 36].rearrange("p (k n) -> p k n", k=KD)
            ms_(att[:, 0:KD * 36], 0.0).then_inc(zeroed, 1)
            pool.wait_ge(zeroed, 4)
            pool.dma_start(wif[:, :, 0:4], w_in[:, :, 2560:2564]).then_inc(wif_full, 16)
            pool.dma_start(wif[:, :, 32:36], w_in[:, :, 2564:2568]).then_inc(wif_full, 16)

            for j in range(NJ):
                for n, X in enumerate((XR, XI)):
                    X3 = X.rearrange("p (i n) -> p i n", i=NI)
                    pool.wait_ge(rotout_done, 2 * j + n + 1)
                    f4 = fin_s[:, 128 * n:128 * n + 128].rearrange("p (b k) -> p k b", b=NB)
                    nc.gpsimd.tensor_copy(f4[:, NI * j:NI * j + NI, :],
                                          X3[:, :, NP_TOK + LB - 1:NT:LB]).then_inc(fin_ready, 1)
                    pool.wait_ge(fin_ready, 4 * j + 2 * n + 1)
                    nc.gpsimd.tensor_copy(fin_p[:, 16 * n + NI * j:16 * n + NI * j + NI],
                                          X3[:, :, NP_TOK - 1:NP_TOK].rearrange("p i a -> p (i a)")).then_inc(fin_ready, 1)
                    pool.wait_ge(fin_ready, 4 * j + 2 * n + 2)
            pool.wait_ge(finT_ready, 3)
            
            pool.dma_start(o["rs"][0].rearrange("b g s -> b (g s)").rearrange("b (k q) -> (b k) q", q=P), so[:, 0:128]).then_inc(stored_pool, 16)
            pool.dma_start(o["is"][0].rearrange("b g s -> b (g s)").rearrange("b (k q) -> (b k) q", q=P), so[:, 128:256]).then_inc(stored_pool, 16)
            pool.dma_start(o["rp"][0, 0].rearrange("(k g) s -> k (g s)", g=2), so[0:16, 256:384]).then_inc(stored_pool, 16)
            pool.dma_start(o["ip"][0, 0].rearrange("(k g) s -> k (g s)", g=2), so[16:32, 256:384]).then_inc(stored_pool, 16)
            pool.wait_ge(row_ready, 1)
            pool.dma_start(o["mp"][0].rearrange("b h -> h b"), mm[:, NP_TOK - 1:NP_TOK], allow_slow_non_contiguous=True).then_inc(stored_pool, 16)
            pool.dma_start(o["ms"][0].rearrange("b h -> h b"), mm[:, NP_TOK + LB - 1:NT:LB], allow_slow_non_contiguous=True).then_inc(stored_pool, 16)
            pool.wait_ge(cp_ready, 1)
            pool.dma_start(o["cp"][0, 0].rearrange("h d e -> d h e"), sgl[:, 0:512].rearrange("p (h e) -> p h e", h=H)).then_inc(stored_pool, 16)
            pool.wait_ge(nT_ready, 1)
            pool.dma_start(o["ns"][0].rearrange("b h d -> (b h) d"), sgl[0:32, 512:640]).then_inc(stored_pool, 16)
            pool.dma_start(o["np"][0, 0], sgl[32:36, 512:640]).then_inc(stored_pool, 16)
            pool.wait_ge(up_done, 2 * KD)
            ms_(btab, 0.0).then_inc(zeroed, 1)
            pool.wait_ge(merged, KD)
            pool.wait_ge(zeroed, 5)
            ms_(zz(m0_ + 640, 768), 0.0).then_inc(zeroed, 1)
            pool.wait_ge(zeroed, 6)
            ms_(acc[64:128, 2, :], 0.0).then_inc(zeroed, 1)
            pool.wait_ge(zeroed, 7)
            ms_(lg.rearrange("p t e -> p (t e)"), 0.0).then_inc(zeroed, 1)

        @block.scalar
        def _(act):
            a = nc.scalar.activation
            cnt = [0]

            def link(ins):
                cnt[0] += 1
                ins.then_inc(ach, 1)
                act.wait_ge(ach, cnt[0])

            act.wait_ge(x_full, 32)
            act.wait_ge(zeroed, 1)
            for tt in range(TT):
                a(S(tt * D, D), x3[:, tt, :], ACT.Square, accum_out=rstd[:, tt:tt + 1]).then_inc(ssq_ready, 1)
            act.wait_ge(sd_ready, 1)
            link(a(rstd[:, 0:3], rstd[:, 0:3], ACT.Sqrt))
            act.sem_inc(sd_ready, 1)
            act.wait_ge(vec_ready, 1)
            a(dt_, v(V_LDT, 16), ACT.Exp).then_inc(par_act, 1)
            act.wait_ge(par_dve, 1)
            a(mag, adr, ACT.Exp).then_inc(par_act, 1)
            act.wait_ge(par_dve, 2)
            act.wait_ge(cst_full, 16)
            a(sc, fr_r, ACT.Sin, scale=TWO_PI).then_inc(par_act, 1)
            def z_evac(n):
                act.wait_ge(z_done, n + 1)
                a(Z(n), bank[n % 4][:, 0:NT], ACT.Copy).then_inc(z_ready, 1)

            for n in range(8):
                z_evac(n)
            for n in range(4):
                act.wait_ge(bxT_done, n + 1)
                dst = (BT, CT)[n // 2][:, n % 2]
                a(dst.rearrange("p j q -> p (j q)"), bank[4 + n][:, :], ACT.Copy).then_inc(bct_ready, 1)
            act.wait_ge(stT_done, 1)
            a(h0T, bank[4][:, 0:256], ACT.Copy).then_inc(stT_ready, 1)
            a(n0T[:, 0:32], bank[4][:, 256:288], ACT.Copy).then_inc(stT_ready, 1)

            for n in range(8, 12):
                z_evac(n)
            act.wait_ge(xT_done, KD)
            for j in range(NJ):
                if j:
                    act.wait_ge(rotout_done, 2 * j)
                for i in range(NI):
                    a(fb[:, i * NT:i * NT + NT], c("tloc"), ACT.Copy, scale=fr[:, NI * j + i:NI * j + i + 1]).then_inc(fb_ready, 1)
                for i in range(NI):
                    a(rho4[:, i * NT:i * NT + NT], c("start"), ACT.Copy, scale=mag[:, NI * j + i:NI * j + i + 1]).then_inc(tab_ready, 1)
                if j:
                    act.wait_ge(bu_done, 8 * j)
                for i in range(NI):
                    a(um[:, i * NT:i * NT + NT], Z(ZU + j), ACT.Copy, scale=c("imask")[:, i:i + 1]).then_inc(um_ready, 1)
                act.wait_ge(fb_red, j + 1)
                a(tabs, fb, ACT.Sin, scale=TWO_PI).then_inc(tab_ready, 1)
                link(a(tabc, fb, ACT.Abs))
                a(tabc, tabc, ACT.Sin, scale=-TWO_PI, bias=c("halfpi")).then_inc(tab_ready, 1)
                if j:
                    act.wait_ge(rotin_done, j)
                for q in range(8):
                    act.wait_ge(bu_done, 8 * j + q + 1)
                    dst = (bu_r, bu_i)[q % 2][:, (q // 2) * NT:(q // 2 + 1) * NT]
                    a(dst, bank[4 + q % 3][:, 0:NT], ACT.Copy).then_inc(bu_ready, 1)
                for n in range(12 + 6 * j, 18 + 6 * j):
                    z_evac(n)
                if j == 0:
                    act.wait_ge(gate_rows, 3)
                    link(a(tmpr[:, 0:NT], tmpr[:, 0:NT], ACT.Abs))
                    link(a(tmpr[:, 0:NT], tmpr[:, 0:NT], ACT.Exp, scale=-1.0))
                    a(tmpr[:, 0:NT], tmpr[:, 0:NT], ACT.Ln, bias=1.0).then_inc(gate_act, 1)
                if j == 1:
                    act.wait_ge(row_ready, 1)
                    a(rows[0:H, NT:2 * NT], mm[:, 0:NT], ACT.Exp, scale=-1.0).then_inc(R_ready, 1)
                    a(rows[0:H, 2 * NT:2 * NT + 64], rows[0:H, 2 * NT:2 * NT + 64], ACT.Exp).then_inc(R_ready, 1)
                    a(wrow[:, 0:NT], wrow[:, 0:NT], ACT.Exp).then_inc(R_ready, 1)
                if j:
                    act.wait_ge(yd_ready, j)
                    a(Z(ZU + j - 1), Z(ZU + j - 1), ACT.Gelu_apprx_tanh).then_inc(gelu_ready, 1)
            act.wait_ge(yd_ready, NJ)
            a(Z(ZU + NJ - 1), Z(ZU + NJ - 1), ACT.Gelu_apprx_tanh).then_inc(gelu_ready, 1)
            act.wait_ge(finT_done, 3)
            for n in range(3):
                rr = 128 if n < 2 else 32
                a(so[0:rr, 128 * n:128 * n + 128], bank[4][0:rr, 128 * n:128 * n + 128], ACT.Copy).then_inc(finT_ready, 1)
            act.wait_ge(z_ready, ZT)
            a(Z(ZO, 4), Z(ZO, 4), ACT.Sigmoid).then_inc(g_sig, 1)
            a(Z(ZGS, 16), Z(ZGS, 16), ACT.Sigmoid).then_inc(g_sig, 1)
            for n in range(4):
                act.wait_ge(glu_done, n + 1)
                a(sgl[:, n * NT:n * NT + NT], bank[n][:, 0:NT], ACT.Sigmoid, bias=v(V_BGLU + n, 1)).then_inc(sgl_ready, 1)
            act.wait_ge(asT_done, 1)
            a(asT, bank[7][:, 0:24], ACT.Copy).then_inc(asT_ready, 1)
            for h in range(H):
                act.wait_ge(vT_done, h + 1)
                for tt in range(TT):
                    w = TW[tt]
                    a(v_tok[0:w, tt, h * P:h * P + P], bank[4 + h % 2][0:w, tt * P:tt * P + P], ACT.Copy).then_inc(v_ready, 1)
            for h in range(H):
                act.wait_ge(bc_done, h + 1)
                if h:
                    act.wait_ge(ym_ready, h)
                    act.wait_ge(C_ready, h)
                a(bc, bank[1][:, 0:384], ACT.Copy).then_inc(bc_ready, 1)
                act.wait_ge(em_ready, h + 1)
                for n, (c0, c1) in enumerate(((0, 256), (256, 384), (384, 448))):
                    a(et[:, c0:c1], et[:, c0:c1], ACT.Exp, bias=asT[:, n * H + h:n * H + h + 1]).then_inc(ex_ready, 1)
                act.wait_ge(den_done, h + 1)
                a(den_a, bank[5][:, 0:NT], ACT.Abs).then_inc(abs_ready, 1)
            act.wait_ge(C_done, H)
            act.wait_ge(C_ready, H)
            a(sgl[:, 0:512], bank[6][:, :], ACT.Copy).then_inc(cp_ready, 1)
            act.wait_ge(nT_done, 1)
            a(sgl[0:36, 512:640], bank[4][0:36, 0:P], ACT.Copy).then_inc(nT_ready, 1)

            for tt in range(TT):
                act.wait_ge(h_ready, 2 * tt + 2)
                a(x3[:, tt, :], acc[:, tt, :], ACT.Square, accum_out=rstd[:, tt:tt + 1]).then_inc(ssq_ready, 1)
            act.wait_ge(sd_ready, 3)
            link(a(rstd[:, 0:3], rstd[:, 0:3], ACT.Sqrt))
            act.sem_inc(sd_ready, 1)
            act.wait_ge(rl_ready, 1)
            a(exw.rearrange("p t e -> p (t e)"), exw.rearrange("p t e -> p (t e)"), ACT.Exp).then_inc(rl_ready, 1)
            act.wait_ge(wtT_done, 1)
            a(p_lo[0:NE, :], bank[4][0:NE, 0:384], ACT.Copy).then_inc(wtT_ready, 1)

            def experts_act(n, prologue=False):
                if not prologue:
                    act.wait_ge(g_ready, n + 1)
                    a(ms, mg, ACT.Sigmoid, scale=ALPHA).then_inc(s_ready, 1)

            def gather_act(n):
                act.wait_ge(gath_done, n + 1)
                a(xs, bank[2][:, :], ACT.Copy).then_inc(xs_ready, 1)

            def down_act(n):
                act.wait_ge(hTt_done, n + 1)
                a(hT, bank[3][:, :], ACT.Copy).then_inc(hT_ready, 1)

            def y_act(n):
                act.wait_ge(dn_done, n + 1)
                a(yb, bank[5][:, :], ACT.Copy).then_inc(y_ready, 1)

            gather_act(0)
            with act.Fori(0, NE) as p:
                experts_act(p)
                gather_act(p + 1)
                down_act(p)
                y_act(p)
            act.wait_ge(cnt_ready, 1)
            extra = act.value_load(cnt_i[0:1, 0:1], min_val=0, max_val=EXTRA)
            with act.If(extra > 0):
                with act.Fori(0, extra) as q:
                    gather_act(q + (NE + 1))
                    experts_act(q + NE)
                    down_act(q + NE)
                    y_act(q + NE)

            for tt in range(TT):
                if tt == 0:
                    act.wait_ge(acc_add, extra * 6 + (6 * (NE + 1) + 2))
                a(x3[:, tt, :], acc[:, tt, :], ACT.Square, accum_out=rstd[:, tt:tt + 1]).then_inc(ssq_ready, 1)
            act.wait_ge(sd_ready, 5)
            cnt[0] += 1
            a(rstd[:, 0:3], rstd[:, 0:3], ACT.Sqrt).then_inc(ach, 1)
            act.wait_ge(ach, cnt[0])
            act.sem_inc(sd_ready, 1)
            for k in range(2):
                act.wait_ge(pTt_done, k + 1)
                a(pT[:, k, :], bank[4 + k][:, 0:384], ACT.Copy).then_inc(pT_ready, 1)
            for n in range(6):
                act.wait_ge(pj_done, n + 1)
                a(pproj[:, n // 2, (n % 2) * 512:(n % 2) * 512 + 512], bank[4 + n % 4][:, :], ACT.Copy).then_inc(pj_ready, 1)
            for n in range(6):
                act.wait_ge(gt_done, n + 1)
                a(x3[:, n // 2, (n % 2) * 512:(n % 2) * 512 + 512], bank[n % 2][:, :], ACT.Sigmoid).then_inc(gt_sig, 1)
            for tt in range(TT):
                act.wait_ge(fin_h, 2 * tt + 2)
                a(x3[:, tt, :], acc[:, tt, :], ACT.Square, accum_out=rstd[:, tt:tt + 1]).then_inc(ssq_ready, 1)
            act.wait_ge(sd_ready, 7)
            link(a(rstd[:, 0:3], rstd[:, 0:3], ACT.Sqrt))
            act.sem_inc(sd_ready, 1)

        @block.vector
        def _(dve):
            V = nc.vector
            cnt = [0]

            def link(ins):
                cnt[0] += 1
                ins.then_inc(ch, 1)
                dve.wait_ge(ch, cnt[0])

            def rms(r, src, dst):
                dve.wait_ge(ssq_ready, 3 * (r + 1))
                V.tensor_scalar(rstd[:, 0:3], rstd[:, 0:3], 1.0 / D, EPS, ALU.mult, ALU.add).then_inc(sd_ready, 1)
                dve.wait_ge(sd_ready, 2 * r + 2)
                link(V.reciprocal(rstd[:, 0:3], rstd[:, 0:3]))
                for tt in range(TT):
                    V.tensor_scalar(dst[:, tt, :], src[:, tt, :], rstd[:, tt:tt + 1], None, ALU.mult).then_inc(xn_ready, 1)

            def hnT_evac(r, g, banks):
                for k in range(KD):
                    dve.wait_ge(xT_done, KD * r + k + 1)
                    V.tensor_scalar(hn3[:, k, :], bank[banks[k % len(banks)]][:, 0:NT], v(g + k, 1), None, ALU.mult).then_inc(hnT_ready, 1)

            dve.wait_ge(cst_full, 16)
            dve.wait_ge(vec_full, 16 * 8)
            V.tensor_copy(vec_rows[0:16, :].rearrange("p (g s) -> p g s", g=2),
                          ssq[0:16, 0:2].unsqueeze(2).to_broadcast([16, 2, ST])).then_inc(ldt_ready, 1)
            rms(0, x3, x3)
            dve.wait_ge(vecT_done, 1)
            V.tensor_copy(vec, bank[4][:, 0:80]).then_inc(vec_ready, 1)
            dve.wait_ge(vec_ready, 1)
            hnT_evac(0, V_GMIX, (0, 1, 2, 3))

            dve.wait_ge(par_act, 1)
            V.tensor_tensor(adr, v(V_ARE, 16), dt_, ALU.mult).then_inc(par_dve, 1)
            link(V.tensor_tensor(fr[:, 0:16], v(V_AIM, 16), dt_, ALU.mult))
            link(V.tensor_scalar(fr[:, 0:16], fr[:, 0:16], 1.0 / 6.283185307179586, None, ALU.mult))
            link(V.tensor_scalar(fr_r[:, 0:16], fr[:, 0:16], ROUND, ROUND, ALU.add, ALU.subtract))
            link(V.tensor_tensor(fr[:, 0:16], fr[:, 0:16], fr_r[:, 0:16], ALU.subtract))
            link(V.tensor_scalar(fr[:, 16:32], fr[:, 0:16], 0.25, None, ALU.add))
            link(V.tensor_scalar(fr_r, fr, ROUND, ROUND, ALU.add, ALU.subtract))
            V.tensor_tensor(fr_r, fr, fr_r, ALU.subtract).then_inc(par_dve, 1)
            dve.wait_ge(par_act, 3)
            link(V.tensor_tensor(ab_i, mag, sc[:, 0:16], ALU.mult))
            link(V.tensor_tensor(ab_r, mag, sc[:, 16:32], ALU.mult))
            ar, ai = v(V_ARE, 16), v(V_AIM, 16)
            link(V.tensor_scalar(nr, ab_r, -1.0, None, ALU.add))
            link(V.tensor_tensor(den, ar, ar, ALU.mult))
            link(V.tensor_tensor(tm, ai, ai, ALU.mult))
            link(V.tensor_tensor(den, den, tm, ALU.add))
            link(V.reciprocal(den, den))
            link(V.tensor_tensor(co_r, nr, ar, ALU.mult))
            link(V.tensor_tensor(tm, ab_i, ai, ALU.mult))
            link(V.tensor_tensor(co_r, co_r, tm, ALU.add))
            link(V.tensor_tensor(co_r, co_r, den, ALU.mult))
            link(V.tensor_tensor(co_i, ab_i, ar, ALU.mult))
            link(V.tensor_tensor(tm, nr, ai, ALU.mult))
            link(V.tensor_tensor(co_i, co_i, tm, ALU.subtract))
            link(V.tensor_tensor(co_i, co_i, den, ALU.mult))

            def k3(x_):
                return x_.rearrange("p (k h) -> p k h", k=NK)

            def bck(x_):
                return x_.unsqueeze(2).to_broadcast([P, NK, GW])

            dve.wait_ge(bn_full, 64)
            link(V.tensor_tensor(k3(bb_r), k3(bn_r), bck(co_r), ALU.mult))
            link(V.tensor_tensor(k3(btmp), k3(bn_i), bck(co_i), ALU.mult))
            link(V.tensor_tensor(bb_r, bb_r, btmp, ALU.subtract))
            link(V.tensor_tensor(k3(bb_i), k3(bn_i), bck(co_r), ALU.mult))
            link(V.tensor_tensor(k3(btmp), k3(bn_r), bck(co_i), ALU.mult))
            link(V.tensor_tensor(bb_i, bb_i, btmp, ALU.add))
            for n, src in enumerate((bb_r, bb_i)):
                V.tensor_tensor(Bx[:, 512 * n:512 * n + 512].rearrange("p (k a h) -> p k a h", k=NK, a=2),
                                k3(src).unsqueeze(2).to_broadcast([P, NK, 2, GW]),
                                c("half").unsqueeze(1).unsqueeze(3).to_broadcast([P, NK, 2, GW]), ALU.mult).then_inc(bx_ready, 1)
            for n, m_ in enumerate(("par", "npar")):
                V.tensor_tensor(Cx[:, 512 * n:512 * n + 512].rearrange("p (j a s) -> p j a s", j=NJ, a=2),
                                cn[:, 256 * n:256 * n + 256].rearrange("p (j s) -> p j s", j=NJ).unsqueeze(2).to_broadcast([P, NJ, 2, ST]),
                                c(m_).unsqueeze(1).unsqueeze(3).to_broadcast([P, NJ, 2, ST]), ALU.mult).then_inc(bx_ready, 1)
            dve.wait_ge(stT_ready, 2)
            h0v = h0T.rearrange("p (n b k) -> p n b k", n=2, b=NB)
            ahv = ah.rearrange("p (n b k) -> p n b k", n=2, b=NB)
            tv = bn_r[:, 0:128].rearrange("p (b k) -> p b k", b=NB)

            def bcb(x_):
                return x_.unsqueeze(1).to_broadcast([P, NB, NK])

            link(V.tensor_tensor(ahv[:, 0], h0v[:, 0], bcb(ab_r), ALU.mult))
            link(V.tensor_tensor(tv, h0v[:, 1], bcb(ab_i), ALU.mult))
            link(V.tensor_tensor(ahv[:, 0], ahv[:, 0], tv, ALU.subtract))
            link(V.tensor_tensor(ahv[:, 1], h0v[:, 1], bcb(ab_r), ALU.mult))
            link(V.tensor_tensor(tv, h0v[:, 0], bcb(ab_i), ALU.mult))
            link(V.tensor_tensor(ahv[:, 1], ahv[:, 1], tv, ALU.add))

            def i3(x_):
                return x_.rearrange("p (i n) -> p i n", i=NI)

            s5n = [0]

            def s5link(ins):
                s5n[0] += 1
                ins.then_inc(s5d, 1)
                dve.wait_ge(s5d, s5n[0])

            for j in range(NJ):
                dve.wait_ge(fb_ready, 4 * (j + 1))
                s5link(V.tensor_scalar(tabs, fb, ROUND, ROUND, ALU.add, ALU.subtract))
                V.tensor_tensor(fb, fb, tabs, ALU.subtract).then_inc(fb_red, 1)
                dve.wait_ge(bu_ready, 8 * (j + 1))
                dve.wait_ge(tab_ready, 6 * (j + 1))
                for n, b_ in enumerate((bu_r, bu_i)):
                    first = i3(b_)[:, :, NP_TOK:NT:LB]
                    s5link(V.tensor_tensor(first, first, ahv[:, n, :, NI * j:NI * j + NI].rearrange("p b i -> p i b"), ALU.add))
                s5link(V.tensor_tensor(t1, bu_r, tabc, ALU.mult))
                s5link(V.tensor_tensor(t2, bu_i, tabs, ALU.mult))
                s5link(V.tensor_tensor(t1, t1, t2, ALU.add))
                s5link(V.tensor_tensor(t2, bu_i, tabc, ALU.mult))
                s5link(V.tensor_tensor(bu_r, bu_r, tabs, ALU.mult))
                s5link(V.tensor_tensor(t2, t2, bu_r, ALU.subtract))
                s5link(V.tensor_tensor_scan(bu_r, rho4, t1, 0.0, ALU.mult, ALU.add))
                s5link(V.tensor_tensor_scan(bu_i, rho4, t2, 0.0, ALU.mult, ALU.add))
                s5link(V.tensor_tensor(t1, bu_r, tabc, ALU.mult))
                s5link(V.tensor_tensor(t2, bu_i, tabs, ALU.mult))
                if j:
                    dve.wait_ge(y_done, j)
                    dve.wait_ge(fin_ready, 4 * j)
                V.tensor_tensor(XR, t1, t2, ALU.subtract).then_inc(rotout_done, 1)
                dve.wait_ge(rotout_done, 2 * j + 1)
                s5link(V.tensor_tensor(t1, bu_r, tabs, ALU.mult))
                s5link(V.tensor_tensor(t2, bu_i, tabc, ALU.mult))
                dve.sem_inc(rotin_done, 1)
                V.tensor_tensor(XI, t1, t2, ALU.add).then_inc(rotout_done, 1)
                if j:
                    V.scalar_tensor_tensor(Z(ZU + j - 1), Z(ZU + j - 1), v(V_D + j - 1, 1), bank[7][:, 0:NT], ALU.mult, ALU.add).then_inc(yd_ready, 1)
                if j == 0:
                    dve.wait_ge(gate_done, 1)
                    dve.wait_ge(gb_full, 64)
                    V.tensor_scalar(ig[:, 0:NT], bank[3 + 4][0:H, 0:NT], gb[0:H, 0:1], None, ALU.add).then_inc(gate_rows, 1)
                    V.tensor_scalar(lf[:, 0:NT], bank[7][32:32 + H, 0:NT], gb[0:H, 1:2], 0.0, ALU.add, ALU.min).then_inc(gate_rows, 1)
                    V.tensor_scalar(tmpr[:, 0:NT], bank[7][32:32 + H, 0:NT], gb[0:H, 1:2], None, ALU.add).then_inc(gate_rows, 1)
                    dve.wait_ge(gate_rows, 3)
                    link(V.memset(m09[0:H, 0:1], 0.0))
                if j == 1:
                    dve.wait_ge(gate_act, 1)
                    st = c("start")[0:H, :]
                    link(V.tensor_tensor(lf[:, 0:NT], lf[:, 0:NT], tmpr[:, 0:NT], ALU.subtract))
                    link(V.tensor_tensor_scan(bb[:, 0:NT], st, lf[:, 0:NT], 0.0, ALU.mult, ALU.add))
                    link(V.tensor_copy(arow[:, 0:NT], ig[:, 0:NT]))
                    f0 = wrow[:, 0:9]
                    link(V.tensor_copy(f0[:, 0:1], lf[:, 0:1]))
                    link(V.tensor_copy(f0[:, 1:9], lf[:, NP_TOK:NT:LB]))
                    link(V.tensor_tensor(f0, f0, m09[0:H, :], ALU.add))
                    link(V.tensor_tensor(arow[:, 0:1], arow[:, 0:1], f0[:, 0:1], ALU.max))
                    link(V.tensor_tensor(arow[:, NP_TOK:NT:LB], arow[:, NP_TOK:NT:LB], f0[:, 1:9], ALU.max))
                    link(V.tensor_scalar(tmpr[:, 0:NT], st, -1.0, 3.0e38, ALU.add, ALU.mult))
                    link(V.tensor_tensor(lf[:, 0:NT], lf[:, 0:NT], tmpr[:, 0:NT], ALU.add))
                    link(V.tensor_tensor_scan(mm[:, 0:NT], lf[:, 0:NT], arow[:, 0:NT], 0.0, ALU.add, ALU.max))
                    link(V.tensor_tensor(rows[0:H, 0:NT], bb[:, 0:NT], mm[:, 0:NT], ALU.subtract))
                    link(V.tensor_tensor(arow[:, 0:NT], ig[:, 0:NT], bb[:, 0:NT], ALU.subtract))
                    r1 = rows[0:H, 0:NT]
                    r1s = r1[:, NP_TOK:NT].rearrange("p (b l) -> p b l", b=NB)
                    ars = arow[:, NP_TOK:NT].rearrange("p (b l) -> p b l", b=NB)
                    link(V.tensor_tensor(rows[0:H, 2 * NT:2 * NT + 64].rearrange("p (b l) -> p b l", b=NB), r1s,
                                         m09[0:H, 1:9].unsqueeze(2).to_broadcast([H, NB, LB]), ALU.add))
                    link(V.tensor_scalar(wrow[:, 0:NP_TOK], arow[:, 0:NP_TOK], r1[:, NP_TOK - 1:NP_TOK], None, ALU.add))
                    V.tensor_tensor(wrow[:, NP_TOK:NT].rearrange("p (b l) -> p b l", b=NB), ars,
                                    r1s[:, :, LB - 1:LB].to_broadcast([H, NB, LB]), ALU.add).then_inc(row_ready, 1)
            dve.wait_ge(y_done, NJ)
            V.scalar_tensor_tensor(Z(ZU + 3), Z(ZU + 3), v(V_D + 3, 1), bank[7][:, 0:NT], ALU.mult, ALU.add).then_inc(yd_ready, 1)
            for n in range(4):
                dve.wait_ge(sgl_ready, n + 1)
                V.tensor_tensor(ysT2[:, n * NT:n * NT + NT], Z(ZU + n), sgl[:, n * NT:n * NT + NT], ALU.mult).then_inc(ys_ready, 1)

            dve.wait_ge(asT_ready, 1)
            dve.wait_ge(R_ready, 3)
            link(V.memset(kw[:, 256:384], 0.0))
            link(V.memset(v_tok[64:128, 2, :], 0.0))
            dve.wait_ge(v_ready, TT * H)
            a_n = [0]

            def alink(ins):
                a_n[0] += 1
                ins.then_inc(att_d, 1)
                dve.wait_ge(att_d, a_n[0])

            for h in range(H):
                dve.wait_ge(E_done, h + 1)
                if h:
                    dve.wait_ge(N_done, h)
                V.tensor_tensor(et, bank[0][:, 0:448], c("amask"), ALU.add).then_inc(em_ready, 1)
                dve.wait_ge(kT_done, h + 1)
                if h:
                    dve.wait_ge(C_done, h)
                for tt in range(TT):
                    w = TW[tt]
                    V.tensor_scalar(kw[0:w, tt * P:tt * P + P], bank[3][0:w, tt * P:tt * P + P], asT[0:w, 12 + tt * H + h:13 + tt * H + h],
                                    KSCALE, ALU.mult, ALU.mult).then_inc(kw_ready, 1)
                V.tensor_tensor(vx, v_tok[:, 2, h * P:h * P + P].unsqueeze(1).to_broadcast([P, NB, P]),
                                c("seqm").unsqueeze(2).to_broadcast([P, NB, P]), ALU.mult).then_inc(vx_ready, 1)
                dve.wait_ge(bc_ready, h + 1)
                V.tensor_tensor(qw, Z(ZQ + h)[:, NP_TOK:NT], bc[:, NT:NT + 64], ALU.mult).then_inc(qw_ready, 1)
                dve.wait_ge(qw_ready, h + 1)
                n0h = n0T[:, 0:32].rearrange("p (b h) -> p b h", b=NB)[:, :, h:h + 1]
                V.tensor_tensor(qn.rearrange("p (b l) -> p b l", b=NB), qw.rearrange("p (b l) -> p b l", b=NB),
                                n0h.to_broadcast([P, NB, LB]), ALU.mult).then_inc(qn_ready, 1)
                dve.wait_ge(ex_ready, 3 * (h + 1))
                dve.wait_ge(S_done, h + 1)
                V.scalar_tensor_tensor(et, bank[2][:, 0:448], KSCALE, et, ALU.mult, ALU.mult).then_inc(P_ready, 1)
                dve.wait_ge(abs_ready, h + 1)
                alink(V.tensor_tensor(den_a, den_a, bc[:, 0:NT], ALU.max))
                alink(V.reciprocal(den_a, den_a))
                dve.wait_ge(N_done, h + 1)
                alink(V.tensor_tensor(den_a, bank[4][:, 0:NT], den_a, ALU.mult))
                V.tensor_tensor(Z(ZQ + h), den_a, Z(ZO + h), ALU.mult).then_inc(ym_ready, 1)
                dec = bc[:, NT:NT + 64].rearrange("p (b l) -> p b l", b=NB)[:, :, LB - 1:LB]
                dve.wait_ge(qn_ready, h + 1)
                alink(V.tensor_tensor(C0[:, h], C0[:, h], dec.to_broadcast([P, NB, P]), ALU.mult))
                alink(V.tensor_tensor(n0h, n0h, dec, ALU.mult))
                dve.wait_ge(C_done, h + 1)
                alink(V.tensor_tensor(C0[:, h, 0:4], C0[:, h, 0:4], bank[0][:, :].rearrange("p (b e) -> p b e", b=4), ALU.add))
                alink(V.tensor_tensor(n0h, n0h, bank[3][:, 384:392].unsqueeze(2), ALU.add))
                alink(V.tensor_copy(n0T[:, 32 + h:33 + h], bank[3][:, 392:393]))
                V.tensor_tensor(C0[:, h, 4:8], C0[:, h, 4:8], bank[7][:, :].rearrange("p (b e) -> p b e", b=4), ALU.add).then_inc(C_ready, 1)

            dve.wait_ge(g_sig, 2)
            for n in range(KD):
                dve.wait_ge(up_done, 2 * n + 1)
                b0, b1 = bank[(2 * n) % 4], bank[(2 * n) % 4 + 1]
                V.tensor_tensor(Z(ZGS + n), Z(ZGS + n), b0[:, 0:NT], ALU.mult).then_inc(up_dve, 1)
                dve.wait_ge(up_done, 2 * n + 2)
                V.tensor_tensor(Z(ZGM + n), Z(ZGM + n), b1[:, 0:NT], ALU.mult).then_inc(up_dve, 1)
                dve.wait_ge(up_dve, 2 * n + 2)
                V.tensor_tensor(Z(ZGS + n), Z(ZGS + n), Z(ZGM + n), ALU.add).then_inc(merged, 1)
            dve.wait_ge(res_full, 32)
            dve.wait_ge(zeroed, 8)
            for n in range(6):
                tt, hf = n // 2, n % 2
                w = TW[tt]
                dve.wait_ge(out_done, n + 1)
                A = acc[0:w, tt, 512 * hf:512 * hf + 512]
                V.tensor_tensor(A, A, bank[4 + n % 4][0:w, :], ALU.add).then_inc(h_ready, 1)
            rms(1, acc, x3)
            dve.wait_ge(stored_pool, 16 * 9)
            hnT_evac(1, V_GFFN, (0, 1, 2, 3))

            dve.wait_ge(rl_done, TT)
            for tt in range(TT):
                w = TW[tt]
                link(V.tensor_tensor(lg[0:w, tt, :], bank[4][0:w, 32 * tt:32 * tt + 32], brb[0:w, :], ALU.add))
            for tt in range(TT):
                link(V.max(mtop[:, tt, :], lg[:, tt, :]))

            def bce(x_):
                return x_.to_broadcast([P, TT, NE])

            link(V.tensor_tensor(gtm, lg, bce(mtop[:, :, 3:4]), ALU.is_gt))
            link(V.tensor_tensor(eqm, lg, bce(mtop[:, :, 3:4]), ALU.is_equal))
            link(V.reduce_sum(mcol[:, 0:3].unsqueeze(2), gtm, AX.X))
            link(V.tensor_scalar(mcol[:, 0:3], mcol[:, 0:3], -1.0, 4.5, ALU.mult, ALU.add))
            for tt in range(TT):
                link(V.tensor_tensor_scan(msk[:, tt, :], ones[:, 0:NE], eqm[:, tt, :], 0.0, ALU.mult, ALU.add))
            link(V.tensor_tensor(msk, msk, bce(mcol[:, 0:3].unsqueeze(2)), ALU.is_lt))
            link(V.tensor_tensor(msk, msk, eqm, ALU.mult))
            link(V.tensor_tensor(msk, msk, gtm, ALU.add))
            link(V.memset(msk[64:128, 2, :], 0.0))
            V.tensor_tensor(exw, lg, bce(mtop[:, :, 0:1]), ALU.subtract).then_inc(rl_ready, 1)
            dve.sem_inc(mask_ready, 1)
            dve.wait_ge(rl_ready, 2)
            link(V.tensor_tensor(exw, exw, msk, ALU.mult))
            link(V.reduce_sum(mcol[:, 4:7].unsqueeze(2), exw, AX.X))
            link(V.tensor_scalar(mcol[:, 4:7], mcol[:, 4:7], 1e-30, None, ALU.max))
            link(V.reciprocal(mcol[:, 4:7], mcol[:, 4:7]))
            link(V.memset(wt[:, :, NE:NE + 1], 0.0))
            link(V.tensor_tensor(wt[:, :, 0:NE], exw, bce(mcol[:, 4:7].unsqueeze(2)), ALU.mult))
            dve.sem_inc(mask_ready, 1)
            dve.wait_ge(rank_done, 1)
            link(V.memset(rk[:, :, NE:NE + 1], -1.0))
            link(V.tensor_scalar(rk[:, :, 0:NE], bank[5][:, 0:96].rearrange("p (t e) -> p t e", t=TT), 1.0, None, ALU.add))
            link(V.tensor_tensor(rk[:, :, 0:NE], rk[:, :, 0:NE], msk, ALU.mult))
            link(V.tensor_scalar(rk[:, :, 0:NE], rk[:, :, 0:NE], -1.0, None, ALU.add))
            cntb = bank[5][:, 96:128]
            link(V.tensor_scalar(nov, cntb, float(SLOTS), None, ALU.is_gt))
            for r in range(2, 5):
                link(V.tensor_scalar(ind, cntb, float(SLOTS * r), None, ALU.is_gt))
                link(V.tensor_tensor(nov, nov, ind, ALU.add))
            link(V.tensor_tensor_scan(cinc, ones[:, 0:NE], nov, 0.0, ALU.mult, ALU.add))
            link(V.tensor_scalar(ind, cinc, c("pidx"), None, ALU.is_le))
            link(V.reduce_sum(opass[:, 0:1], ind, AX.X))
            link(V.tensor_scalar(opass[:, 0:1], opass[:, 0:1], float(NE - 1), None, ALU.min))
            link(V.tensor_tensor(ind, ind, nov, ALU.mult))
            link(V.reduce_sum(opass[:, 1:2], ind, AX.X))
            link(V.tensor_tensor(opass[:, 1:2], c("pidx"), opass[:, 1:2], ALU.subtract))
            link(V.tensor_scalar(opass[:, 1:2], opass[:, 1:2], 1.0, float(SLOTS), ALU.add, ALU.mult))
            link(V.tensor_scalar(dtab[:, 0:EXTRA], ident[:, 0:EXTRA], opass[:, 0:1], None, ALU.mult))
            V.tensor_scalar(dtab[:, EXTRA:2 * EXTRA], ident[:, 0:EXTRA], opass[:, 1:2], None, ALU.mult).then_inc(tab_made, 1)
            dve.wait_ge(ob_done, 1)
            link(V.tensor_copy(cnt_i[0:1, 0:1], cinc[0:1, NE - 1:NE]))
            link(V.tensor_copy(cnt_i[0:1, 1:1 + EXTRA], bank[6][0:1, 0:EXTRA]))
            link(V.tensor_copy(obase, bank[6][:, EXTRA:2 * EXTRA]))
            dve.sem_inc(cnt_ready, 1)
            for n in range(6):
                tt, hf = n // 2, n % 2
                w = TW[tt]
                dve.wait_ge(bd_done, n + 1)
                A = acc[0:w, tt, 512 * hf:512 * hf + 512]
                V.tensor_tensor(A, A, bank[n % 2][0:w, :], ALU.add).then_inc(acc_ready, 1)
            link(V.memset(p_lo, 0.0))
            link(V.memset(yb, 0.0))
            dve.sem_inc(y_ready, 1)
            dve.sem_inc(acc_add, 2)

            gffn = v(V_GFFN, 8)

            def select(e, base=None):
                V.tensor_tensor(sel, (c("slot") if base is None else base).unsqueeze(1).to_broadcast([P, TT, SLOTS]),
                                rk[:, :, bass.ds(e, 1)].to_broadcast([P, TT, SLOTS]), ALU.is_equal).then_inc(sel_ready, 1)

            def hot(e):
                V.tensor_copy(onehot, ident[:, bass.ds(e, 1)].to_broadcast([P, SLOTS])).then_inc(oh_ready, 1)

            def weigh(e, n):
                dve.wait_ge(sel_ready, n + 1)
                V.tensor_tensor(selw, sel.unsqueeze(2).to_broadcast([P, TT, 2, SLOTS]),
                                wt[:, :, bass.ds(e, 1)].unsqueeze(3).to_broadcast([P, TT, 2, SLOTS]), ALU.mult).then_inc(selw_ready, 1)

            def x_evac(n):
                dve.wait_ge(xsT_done, n + 1)
                V.tensor_tensor(xsT.rearrange("p (j a s) -> p a j s", j=4, a=2),
                                bank[2][:, :].rearrange("p (j a s) -> p a j s", j=4, a=2),
                                gffn.rearrange("p (a j) -> p a j", a=2).unsqueeze(3).to_broadcast([P, 2, 4, SLOTS]),
                                ALU.mult).then_inc(xsT_ready, 1)

            def swiglu(n):
                dve.wait_ge(g_done, n + 1)
                V.tensor_scalar(mg, bank[0][:, :], LIMIT, None, ALU.min).then_inc(g_ready, 1)
                dve.wait_ge(u_done, n + 1)
                V.tensor_scalar(mu, bank[1][:, :], LIMIT, -LIMIT, ALU.min, ALU.max).then_inc(u_ready, 1)
                dve.wait_ge(u_ready, n + 1)
                V.scalar_tensor_tensor(mu, mu, 1.0, mg, ALU.add, ALU.mult).then_inc(gu_ready, 1)
                dve.wait_ge(gu_ready, n + 1)
                dve.wait_ge(s_ready, n + 1)
                V.tensor_tensor(hb, mu, ms, ALU.mult).then_inc(hb_ready, 1)

            def accumulate(n):
                for m in range(6):
                    tt, hf = m // 2, m % 2
                    w = TW[tt]
                    dve.wait_ge(sc_done, n * 6 + m + 1)
                    A = acc[0:w, tt, 512 * hf:512 * hf + 512]
                    V.tensor_tensor(A, A, bank[6 + m % 2][0:w, :], ALU.add).then_inc(acc_add, 1)

            def p_evac(n):
                dve.wait_ge(pw_done, n + 1)
                V.tensor_copy(p_lo[0:64, :], bank[4][0:64, 0:384]).then_inc(pw_ready, 1)
                V.tensor_copy(p_hi[64:128, :], bank[4][64:128, 0:384]).then_inc(pw_ready, 1)

            dve.wait_ge(acc_ready, 6)
            select(0)
            hot(0)
            x_evac(0)
            with dve.Fori(0, NE) as p:
                dve.wait_ge(gath_done, p + 1)
                weigh(p, p)
                dve.wait_ge(selw_ready, p + 1)
                select(p + 1)
                swiglu(p)
                hot(p + 1)
                accumulate(p)
                p_evac(p)
                x_evac(p + 1)
            accumulate(NE)
            extra = dve.value_load(cnt_i[0:1, 0:1], min_val=0, max_val=EXTRA)
            with dve.If(extra > 0):
                with dve.Fori(0, extra) as q:
                    e = dve.value_load(cnt_i[0:1, bass.ds(q + 1, 1)], min_val=0, max_val=NE - 1)
                    V.tensor_scalar(islot, c("slot"), obase[:, bass.ds(q, 1)], None, ALU.add).then_inc(tab_made, 1)
                    dve.wait_ge(tab_made, q + 2)
                    select(e, islot)
                    hot(e)
                    weigh(e, q + (NE + 1))
                    x_evac(q + (NE + 1))
                    swiglu(q + NE)
                    p_evac(q + NE)
                    accumulate(q + (NE + 1))

            dve.wait_ge(acc_add, extra * 6 + (6 * (NE + 1) + 2))
            rms(2, acc, x3)
            hnT_evac(2, V_GPLE, (0, 1, 2, 3))
            dve.wait_ge(pj_ready, 6)
            for n in range(6):
                tt, hf = n // 2, n % 2
                cs = slice(512 * hf, 512 * hf + 512)
                dve.wait_ge(gt_sig, n + 1)
                link(V.tensor_tensor(x3[:, tt, cs], x3[:, tt, cs], pproj[:, tt, cs], ALU.mult))
                V.tensor_tensor(acc[:, tt, cs], acc[:, tt, cs], x3[:, tt, cs], ALU.add).then_inc(fin_h, 1)
            dve.wait_ge(ssq_ready, 12)
            V.tensor_scalar(rstd[:, 0:3], rstd[:, 0:3], 1.0 / D, EPS, ALU.mult, ALU.add).then_inc(sd_ready, 1)
            dve.wait_ge(sd_ready, 8)
            link(V.reciprocal(rstd[:, 0:3], rstd[:, 0:3]))
            dve.wait_ge(gfin_full, 16)
            for tt in range(TT):
                V.scalar_tensor_tensor(acc[:, tt, :], acc[:, tt, :], rstd[:, tt:tt + 1], gfin, ALU.mult, ALU.mult).then_inc(out_ready, 1)

        @block.tensor
        def _(pe):
            mm_, tr = nc.tensor.matmul, nc.tensor.transpose

            def transposes(r, src):
                pe.wait_ge(xn_ready, TT * (r + 1))
                for k in range(KD):
                    if k >= 4:
                        pe.wait_ge(hnT_ready, KD * r + k - 3)
                    for tt in range(TT):
                        last = tr(bank[k % 4][:, tt * P:tt * P + P], src[:, tt, k * P:k * P + P], ident)
                    last.then_inc(xT_done, 1)

            pe.wait_ge(cst_full, 16)
            pe.wait_ge(ldt_ready, 1)
            tr(bank[4][:, 0:80], vec_rows[0:80, :], ident[0:80, 0:80]).then_inc(vecT_done, 1)
            transposes(0, x3)

            def z_tile(n):
                s, half = (n // 2) % ZG, n % 2
                if half == 0:
                    pe.wait_ge(slot_full[s], 16 * (n // 2 // ZG + 1))
                if n >= 4:
                    pe.wait_ge(z_ready, n - 3)
                wz = w3(s, KD, 256)
                for k in range(KD):
                    last = mm_(bank[n % 4][:, 0:NT], wz[:, k, half * P:half * P + P], hn3[:, k, :], start=k == 0, stop=k == KD - 1)
                last.then_inc(z_done, 1)
                if half:
                    pe.wait_ge(z_done, n + 1)
                    pe.sem_inc(slot_free[s], 1)

            pe.wait_ge(hnT_ready, KD)
            for n in range(8):
                z_tile(n)
            for n in range(4):
                pe.wait_ge(bx_ready, n + 1)
                if n == 0:
                    pe.wait_ge(vec_ready, 1)
                src = (Bx, Cx)[n // 2][:, 512 * (n % 2):512 * (n % 2) + 512]
                for j in range(NJ):
                    last = tr(bank[4 + n][:, j * P:j * P + P], src[:, j * P:j * P + P], ident)
                last.then_inc(bxT_done, 1)
            pe.wait_ge(bct_ready, 4)
            pe.wait_ge(st_full, 48)
            tr(bank[4][:, 0:P], h0_rows_r, ident)
            tr(bank[4][:, P:2 * P], h0_rows_i, ident)
            tr(bank[4][:, 256:288], n_rows[0:32, :], ident[0:32, 0:32]).then_inc(stT_done, 1)
            for n in range(8, 12):
                z_tile(n)
            pe.wait_ge(stT_ready, 2)

            def bu(j):
                for q in range(8):
                    m = 8 * j + q
                    if q % 2 == 0:
                        pe.wait_ge(um_ready, 4 * j + q // 2 + 1)
                    if m >= 3:
                        pe.wait_ge(bu_ready, 8 * j + q - 2 if q >= 3 else 8 * j)
                    mm_(bank[4 + q % 3][:, 0:NT], BT[:, q % 2, j, :], um[:, (q // 2) * NT:(q // 2 + 1) * NT],
                        start=True, stop=True).then_inc(bu_done, 1)

            def y(j):
                pe.wait_ge(rotout_done, 2 * j + 2)
                if j:
                    pe.wait_ge(yd_ready, j)
                for i in range(NI):
                    out = bank[7][32 * i:32 * i + 32, 0:NT]
                    mm_(out, CT[:, 0, j, 32 * i:32 * i + 32], XR[:, i * NT:(i + 1) * NT], start=True, stop=False)
                    last = mm_(out, CT[:, 1, j, 32 * i:32 * i + 32], XI[:, i * NT:(i + 1) * NT], start=False, stop=True)
                last.then_inc(y_done, 1)

            bu(0)
            pe.wait_ge(wif_full, 32)
            wif = att[:, 0:KD * 36].rearrange("p (k n) -> p k n", k=KD)
            for k in range(KD):
                last = mm_(bank[7][0:36, 0:NT], wif[:, k, :], hn3[:, k, :], start=k == 0, stop=k == KD - 1)
            last.then_inc(gate_done, 1)
            for n in range(12, 18):
                z_tile(n)
            for j in range(1, NJ):
                bu(j)
                if j == 1:
                    pe.wait_ge(gate_rows, 3)
                y(j - 1)
                for n in range(12 + 6 * j, 18 + 6 * j):
                    z_tile(n)
            y(NJ - 1)
            pe.wait_ge(fin_ready, 4 * NJ)
            pe.wait_ge(bu_ready, 8 * NJ)
            for n in range(2):
                tr(bank[4][:, n * P:n * P + P], fin_s[:, n * P:n * P + P], ident).then_inc(finT_done, 1)
            tr(bank[4][0:32, 2 * P:3 * P], fin_p, ident).then_inc(finT_done, 1)
            pe.wait_ge(gelu_ready, 4)
            pe.wait_ge(z_ready, ZT)
            pe.wait_ge(slot_full[4], 16 * 4)
            wg = w3(4, 4, 512)
            for n in range(4):
                for k in range(4):
                    last = mm_(bank[n][:, 0:NT], wg[:, k, n * P:n * P + P], Z(ZU + k), start=k == 0, stop=k == 3)
                last.then_inc(glu_done, 1)
            pe.wait_ge(glu_done, 4)
            pe.sem_inc(slot_free[4], 1)

            pe.wait_ge(R_ready, 3)
            pe.wait_ge(yd_ready, NJ)
            for n, src in enumerate((arow, wrow)):
                for tt in range(TT):
                    last = tr(bank[7][:, 12 * n + H * tt:12 * n + H * tt + H], src[:, tt * P:tt * P + P], ident[0:H, 0:H])
            last.then_inc(asT_done, 1)
            pe.wait_ge(finT_ready, 3)
            for h in range(H):
                if h >= 2:
                    pe.wait_ge(v_ready, TT * (h - 1))
                for tt in range(TT):
                    w = TW[tt]
                    last = tr(bank[4 + h % 2][0:w, tt * P:tt * P + P], Z(ZV + h)[:, tt * P:tt * P + w], ident)
                last.then_inc(vT_done, 1)
            pe.wait_ge(sgl_ready, 4)
            pe.wait_ge(v_ready, TT * H)
            pe.wait_ge(asT_ready, 1)
            pe.wait_ge(c0_full, 16 * H)
            selh = c("sel")
            blocks = ((0, 256, 0, 256), (256, 384, 128, 256), (384, 448, 256, 320))
            for h in range(H):
                if h:
                    pe.wait_ge(C_ready, h)
                sh = selh[:, h * P:h * P + P]
                for c0, c1, a0, a1 in blocks:
                    last = mm_(bank[0][:, c0:c1], sh, rows[:, a0:a1], start=True, stop=True)
                last.then_inc(E_done, 1)
                mm_(bank[1][:, 0:384], sh, rows[:, NT:2 * NT + 64], start=True, stop=True).then_inc(bc_done, 1)
                qT_, kT_ = Z(ZQ + h), Z(ZK + h)
                mm_(bank[2][:, 0:256], kT_[:, 0:128], qT_[:, 0:256], start=True, stop=True)
                mm_(bank[2][:, 256:384], kT_[:, 128:256], qT_[:, 128:256], start=True, stop=True)
                mm_(bank[2][:, 384:448], zT[:, (ZK + h) * NT + 256:(ZK + h) * NT + 384], qT_[:, 256:320], start=True, stop=True).then_inc(S_done, 1)
                for tt in range(TT):
                    w = TW[tt]
                    last = tr(bank[3][0:w, tt * P:tt * P + P], kT_[:, tt * P:tt * P + w], ident)
                last.then_inc(kT_done, 1)
                vh = [v_tok[:, tt, h * P:h * P + P] for tt in range(TT)]
                pe.wait_ge(P_ready, h + 1)
                pe.wait_ge(qn_ready, h + 1)
                bN, bD = bank[4], bank[5]
                mm_(bD[:, 0:256], ones, et[:, 0:256], start=True, stop=False)
                mm_(bD[:, 128:256], ones, et[:, 256:384], start=False, stop=True)
                mm_(bD[:, 256:320], ones, et[:, 384:448], start=True, stop=False)
                mm_(bD[:, 256:320], ones, qn, start=False, stop=True).then_inc(den_done, 1)
                mm_(bN[:, 0:256], vh[0], et[:, 0:256], start=True, stop=False)
                mm_(bN[:, 128:256], vh[1], et[:, 256:384], start=False, stop=True)
                mm_(bN[:, 256:320], vh[2], et[:, 384:448], start=True, stop=False)
                for b in range(NB):
                    last = mm_(bN[:, 256 + LB * b:264 + LB * b], C0[:, h, b], qw[:, LB * b:LB * b + LB], start=False, stop=b == NB - 1)
                last.then_inc(N_done, 1)
                pe.wait_ge(kw_ready, TT * (h + 1))
                pe.wait_ge(vx_ready, h + 1)
                k2 = [kw[:, tt * P:tt * P + P] for tt in range(TT)]
                pe.wait_ge(em_ready, h + 1)
                mm_(bank[0][:, :], k2[2], vx[:, 0:4].rearrange("p b e -> p (b e)"), start=True, stop=True)
                mm_(bank[7][:, :], k2[2], vx[:, 4:8].rearrange("p b e -> p (b e)"), start=True, stop=True)
                mm_(bank[3][:, 384:392], k2[2], c("seqm"), start=True, stop=True)
                mm_(bank[3][:, 392:393], k2[0], ones[:, 0:1], start=True, stop=False)
                mm_(bank[3][:, 392:393], k2[1], ones[:, 0:1], start=False, stop=True)
                mm_(bank[6][:, h * P:h * P + P], k2[0], vh[0], start=True, stop=False)
                mm_(bank[6][:, h * P:h * P + P], k2[1], vh[1], start=False, stop=True).then_inc(C_done, 1)
            pe.wait_ge(C_ready, H)
            tr(bank[4][0:36, 0:P], n0T, ident).then_inc(nT_done, 1)
            for s in (8, 9):
                pe.sem_inc(slot_free[s], 1)

            pe.wait_ge(ys_ready, 4)
            pe.wait_ge(ym_ready, H)
            for s in (6, 7, 10, 11):
                pe.wait_ge(slot_full[s], 16)
            for n in range(KD):
                if n >= 2:
                    pe.wait_ge(up_dve, 2 * n - 2)
                for b, (s0, src) in enumerate(((6, ysT2), (10, None))):
                    for k in range(4):
                        w = w3(s0 + k // 2, 2, D)[:, k % 2, n * P:n * P + P]
                        rhs = src[:, k * NT:(k + 1) * NT] if b == 0 else Z(ZQ + k)
                        last = mm_(bank[(2 * n) % 4 + b][:, 0:NT], w, rhs, start=k == 0, stop=k == 3)
                    last.then_inc(up_done, 1)
            pe.wait_ge(up_done, 2 * KD)
            for s in (6, 7, 10, 11):
                pe.sem_inc(slot_free[s], 1)
            pe.wait_ge(merged, KD)
            pe.wait_ge(nT_ready, 1)
            pe.wait_ge(cp_ready, 1)
            for n in range(6):
                tt, hf = n // 2, n % 2
                w = TW[tt]
                if n >= 4:
                    pe.wait_ge(h_ready, n - 3)
                for k in range(KD):
                    if n == 0 and k % 2 == 0:
                        pe.wait_ge(slot_full[k // 2], 16 * 4)
                    last = mm_(bank[4 + n % 4][0:w, :], Z(ZGS + k)[:, tt * P:tt * P + w],
                               w3(k // 2, 2, D)[:, k % 2, 512 * hf:512 * hf + 512], start=k == 0, stop=k == KD - 1)
                last.then_inc(out_done, 1)
            pe.wait_ge(out_done, 6)
            for s in range(4):
                pe.sem_inc(slot_free[s], 1)

            transposes(1, x3)
            pe.wait_ge(hnT_ready, 2 * KD)
            pe.wait_ge(wr_full, 16)
            pe.wait_ge(h_ready, 6)
            wr3 = wr_sb.rearrange("p (k e) -> p k e", k=KD)
            for tt in range(TT):
                w = TW[tt]
                for k in range(KD):
                    last = mm_(bank[4][0:w, 32 * tt:32 * tt + 32], hn3[:, k, tt * P:tt * P + w], wr3[:, k, :], start=k == 0, stop=k == KD - 1)
                last.then_inc(rl_done, 1)
            pe.wait_ge(mask_ready, 1)
            tri = c("triu")
            for tt in range(TT):
                for s in range(tt + 1):
                    mm_(bank[5][:, 32 * tt:32 * tt + 32], tri if s == tt else ones, msk[:, s, :], start=s == 0, stop=s == tt)
            for s in range(TT):
                last = mm_(bank[5][:, 96:128], ones, msk[:, s, :], start=s == 0, stop=s == TT - 1)
            last.then_inc(rank_done, 1)
            pe.wait_ge(mask_ready, 2)
            for tt in range(TT):
                last = tr(bank[4][0:NE, tt * P:tt * P + P], wt[:, tt, 0:NE], ident)
            last.then_inc(wtT_done, 1)
            pe.wait_ge(tab_made, 1)
            mm_(bank[6][:, 0:2 * EXTRA], ones, dtab, start=True, stop=True).then_inc(ob_done, 1)
            pe.wait_ge(wtT_ready, 1)
            pe.wait_ge(bt_full, 48)
            for n in range(6):
                tt, hf = n // 2, n % 2
                w = TW[tt]
                if n >= 2:
                    pe.wait_ge(acc_ready, n - 1)
                mm_(bank[n % 2][0:w, :], p_lo[:, tt * P:tt * P + w], btab[:, 2 * D + 512 * hf:2 * D + 512 * hf + 512],
                    start=True, stop=True).then_inc(bd_done, 1)
            pe.wait_ge(y_ready, 1)

            def gather(n):
                pe.wait_ge(sel_ready, n + 1)
                for tt in range(TT):
                    for hf in range(2):
                        last = mm_(bank[2][64 * hf:64 * hf + 64, :], sel[:, tt, :], x3[:, tt, 512 * hf:512 * hf + 512],
                                   start=tt == 0, stop=tt == TT - 1)
                last.then_inc(gath_done, 1)

            def gather_T(n):
                pe.wait_ge(xs_ready, n + 1)
                for j in range(4):
                    last = tr(bank[2][:, j * P:j * P + P], xs[:, j * P:j * P + P], ident)
                last.then_inc(xsT_done, 1)

            def project(n, s0, srcT, dst, done, bias=None):
                for hf in range(2 if bias is not None else 0):
                    mm_(dst[64 * hf:64 * hf + 64, :], onehot, btab[:, bias * D + 512 * hf:bias * D + 512 * hf + 512], start=True, stop=False)
                for k in range(KD):
                    s = s0 + k // 2
                    if k % 2 == 0:
                        pe.wait_ge(slot_full[s], n * 16 + 16 * (FREE_FULL[s] + 1))
                    for hf in range(2):
                        last = mm_(dst[64 * hf:64 * hf + 64, :], srcT[:, (k % 4) * P + 64 * (k // 4):(k % 4) * P + 64 * (k // 4) + 64],
                                   w3(s, 2, D)[:, k % 2, 512 * hf:512 * hf + 512], start=bias is None and k == 0, stop=k == KD - 1)
                    if k % 2:
                        last.then_inc(slot_free[s] if k < KD - 1 else done, 1)
                pe.wait_ge(done, n + 1)
                pe.sem_inc(slot_free[s0 + 3], 1)

            def scatter(n):
                pe.wait_ge(y_ready, n + 1)
                for m in range(6):
                    tt, hf = m // 2, m % 2
                    w = TW[tt]
                    pe.wait_ge(acc_add, n * 6 + (m + 1))
                    mm_(bank[6 + m % 2][0:w, :], (p_lo, p_hi)[hf][:, tt * P:tt * P + w], yb, start=True, stop=True).then_inc(sc_done, 1)

            def weights_T(n):
                pe.wait_ge(selw_ready, n + 1)
                for tt in range(TT):
                    last = tr(bank[4][:, tt * P:tt * P + P], selw[:, tt].rearrange("p a s -> p (a s)"), ident)
                last.then_inc(pw_done, 1)

            def gate_up(n):
                pe.wait_ge(xsT_ready, n + 1)
                pe.wait_ge(oh_ready, n + 1)
                project(n, 0, xsT, bank[0], g_done, bias=0)
                project(n, 4, xsT, bank[1], u_done, bias=1)

            def hidden_T(n):
                pe.wait_ge(hb_ready, n + 1)
                for j in range(4):
                    last = tr(bank[3][:, j * P:j * P + P], hb[:, j * P:j * P + P], ident)
                last.then_inc(hTt_done, 1)

            def down(n):
                pe.wait_ge(hT_ready, n + 1)
                project(n, 8, hT, bank[5], dn_done)

            FREE_FULL = [f if s not in (5, 8, 9) else (3 if s == 5 else 0) for s, f in enumerate(FREE0)]
            pe.wait_ge(cnt_ready, 1)
            gather(0)
            gather_T(0)
            with pe.Fori(0, NE) as p:
                gate_up(p)
                gather(p + 1)
                scatter(p)
                weights_T(p)
                hidden_T(p)
                gather_T(p + 1)
                down(p)
            pe.wait_ge(pw_ready, 2 * NE)
            scatter(NE)
            extra = pe.value_load(cnt_i[0:1, 0:1], min_val=0, max_val=EXTRA)
            with pe.If(extra > 0):
                with pe.Fori(0, extra) as q:
                    gather(q + (NE + 1))
                    gather_T(q + (NE + 1))
                    gate_up(q + NE)
                    weights_T(q + NE)
                    hidden_T(q + NE)
                    down(q + NE)
                    pe.wait_ge(pw_ready, q * 2 + 2 * (NE + 1))
                    scatter(q + (NE + 1))

            pe.wait_ge(ple_full, 32)
            pe.wait_ge(acc_add, extra * 6 + (6 * (NE + 1) + 2))
            for k in range(2):
                for tt in range(TT):
                    w = TW[tt]
                    last = tr(bank[4 + k][:, tt * P:tt * P + w], p_tok[0:w, tt, k * P:k * P + P], ident[0:w, 0:w])
                last.then_inc(pTt_done, 1)
            pe.wait_ge(pT_ready, 2)
            pe.wait_ge(slot_full[4], extra * 16 + 16 * (4 + NE + 1))
            for n in range(6):
                tt, hf = n // 2, n % 2
                if n >= 4:
                    pe.wait_ge(pj_ready, n - 3)
                for k in range(2):
                    last = mm_(bank[4 + n % 4][:, :], pT[:, k, tt * P:tt * P + P], w3(4, 2, D)[:, k, 512 * hf:512 * hf + 512], start=k == 0, stop=k == 1)
                last.then_inc(pj_done, 1)
            transposes(2, x3)
            pe.wait_ge(hnT_ready, 3 * KD)
            for n in range(6):
                tt, hf = n // 2, n % 2
                w = TW[tt]
                if n >= 2:
                    pe.wait_ge(gt_sig, n - 1)
                for k in range(KD):
                    if n == 0 and k % 2 == 0:
                        pe.wait_ge(slot_full[k // 2], extra * 16 + 16 * (4 + NE + 1))
                    last = mm_(bank[n % 2][0:w, :], hn3[:, k, tt * P:tt * P + w], w3(k // 2, 2, D)[:, k % 2, 512 * hf:512 * hf + 512],
                               start=k == 0, stop=k == KD - 1)
                last.then_inc(gt_done, 1)


def constants():
    import numpy as np
    c = np.zeros((P, CONST_W), np.float32)

    def put(name, a):
        c[:, CONST[name][0]:CONST[name][1]] = a

    p = np.arange(P)
    n = np.arange(NT)
    put("ident", np.eye(P))
    put("ones", 1.0)
    put("triu", p[:, None] < p[None, :])
    put("slot", np.arange(SLOTS)[None])
    put("tloc", np.where(n < NP_TOK, n, (n - NP_TOK) % LB)[None])
    m = np.full((P, 448), -1.0e30, np.float32)
    m[:, 0:256][p[:, None] <= np.arange(256)[None]] = 0.0
    m[:, 256:384][p[:, None] <= p[None]] = 0.0
    q = np.arange(64)
    ok = (q[:, None] // LB == q[None] // LB) & (q[:, None] <= q[None])
    m[0:64, 384:448][ok] = 0.0
    put("amask", m)
    put("seqm", (p[:, None] // LB == np.arange(NB)[None]))
    put("half", (p[:, None] // 64 == np.arange(2)[None]))
    put("par", (p[:, None] // GW % 2 == np.arange(2)[None]))
    put("npar", -1.0 * (p[:, None] // GW % 2 == np.arange(2)[None]))
    put("imask", (p[:, None] // 32 == np.arange(NI)[None]))
    put("start", np.where((n == 0) | ((n >= NP_TOK) & ((n - NP_TOK) % LB == 0)), 0.0, 1.0)[None])
    put("sel", (p[:, None] == np.arange(H * P)[None] // P))
    put("pidx", p[:, None])
    put("halfpi", np.float32(1.5707963))
    put("eps", EPS)
    return c


_INS = ["x_prompt", "x_sample", "p_prompt", "p_sample", "state_ssm_re", "state_ssm_im", "state_ml_c", "state_ml_n",
        "state_ml_m", "g_mix", "w_in", "ssm_a_re", "ssm_a_im", "ssm_log_dt", "ssm_b_re", "ssm_b_im", "ssm_c_re",
        "ssm_c_im", "ssm_d", "ssm_w_glu", "ssm_b_glu", "ml_b_ig", "ml_b_fg", "w_ssm_up", "w_ml_up", "w_out", "g_ffn",
        "w_router", "b_router", "w_gate", "b_gate", "w_up", "b_up", "w_down", "b_down", "g_ple", "w_ple_gate",
        "w_ple_proj", "g_final"]
_OUTS = [("yp", (1, 256, 1024)), ("ys", (8, 8, 1024)), ("rp", (1, 1, 32, 64)), ("ip", (1, 1, 32, 64)),
         ("cp", (1, 1, 4, 128, 128)), ("np", (1, 1, 4, 128)), ("mp", (1, 1, 4)), ("rs", (1, 8, 32, 64)),
         ("is", (1, 8, 32, 64)), ("cs", (1, 8, 4, 128, 128)), ("ns", (1, 8, 4, 128)), ("ms", (1, 8, 4))]


def kernel(**inputs):
    import numpy as np
    import concourse.bacc as bacc
    from concourse.bass_utils import run_bass_kernel_spmd

    nc = bacc.Bacc("TRN2", target_bir_lowering=False, num_devices=1)
    arrays, t, o = {}, {}, {}
    for name in _INS:
        arrays[name] = np.ascontiguousarray(inputs[name])
    arrays["cst"] = constants()
    for name, a in arrays.items():
        t[name] = nc.dram_tensor("in_" + name, a.shape, mybir.dt.from_np(a.dtype), kind="ExternalInput").ap()
    for name, shape in _OUTS:
        o[name] = nc.dram_tensor("out_" + name, shape, F32, kind="ExternalOutput").ap()
    hybrid_step(nc, t, o)
    r = run_bass_kernel_spmd(nc, [{"in_" + k: a for k, a in arrays.items()}], core_ids=[0])
    return tuple(r.results[0]["out_" + name] for name, _ in _OUTS)
```

```python
from contextlib import ExitStack

import concourse.bass as bass
from concourse import mybir

F32 = mybir.dt.float32
I32 = mybir.dt.int32
ALU = mybir.AluOpType
ACT = mybir.ActivationFunctionType
AX = mybir.AxisListType

P = 128
D = 1024
KD = D // P
NP_TOK, NB, LB = 256, 8, 8
NT = NP_TOK + NB * LB
TT = 3
TW = [128, 128, 64]
G, ST, GW = 32, 64, 16
NJ, NI = 4, 4
NK = NJ * NI
H = 4
NE = 32
SLOTS = 64
EXTRA = 20
RING, SW = 12, 2048
ZT = 36
ZG = 6
ZU, ZQ, ZK, ZV, ZO, ZGS, ZGM = 0, 4, 8, 12, 16, 20, 28
EPS = 1e-6
KSCALE = float(P) ** -0.5
TWO_PI = 6.2831845
ROUND = 12582912.0
LIMIT, ALPHA = 7.0, 1.702

CONST = {}
_at = 0
for _name, _n in (("ident", P), ("ones", P), ("triu", P), ("slot", SLOTS), ("tloc", NT), ("amask", 448),
                  ("seqm", NB), ("half", 2), ("par", 2), ("npar", 2), ("imask", NI), ("start", NT),
                  ("sel", H * P), ("pidx", 1), ("halfpi", 1), ("eps", 1)):
    CONST[_name] = (_at, _at + _n)
    _at += _n
CONST_W = _at


def hybrid_step(nc, t, o):
    ctx = ExitStack()
    with ctx:
        def sb(name, shape, dt=F32):
            return ctx.enter_context(nc.sbuf_tensor(name, shape, dt))

        def sem(name):
            return ctx.enter_context(nc.semaphore(name))

        bank = [ctx.enter_context(nc.psum_tensor(f"bank{i}", [P, 512], F32)) for i in range(8)]

        ring = sb("ring", [P, RING * SW])
        zT = sb("zT", [P, ZT * NT])
        hnT = sb("hnT", [P, KD * NT])
        xkv = sb("xkv", [P, TT * D])
        cst = sb("cst", [P, CONST_W])
        BT = sb("BT", [P, 2, NJ, P])
        CT = sb("CT", [P, 2, NJ, P])
        rows = sb("rows", [P, 704])
        hrow = sb("hrow", [H, 7 * 384])
        att = sb("att", [P, 1664])
        small = sb("small", [P, 1280])
        cnt_i = sb("cnt_i", [1, 1 + EXTRA], I32)

        def slot(s, n=SW):
            return ring[:, s * SW:s * SW + n]

        def c(name, n=None):
            a, b = CONST[name]
            return cst[:, a:b]

        def Z(n, m=1):
            return zT[:, n * NT:(n + m) * NT]

        def zz(a, n):
            return zT[:, a:a + n]

        ident = c("ident")
        ones = c("ones")
        x3 = xkv[:, :].rearrange("p (t d) -> p t d", t=TT)
        hn3 = hnT[:, :].rearrange("p (k n) -> p k n", k=KD)

        s5 = 6 * SW
        JW = NI * NT

        def S(n, w=JW):
            return ring[:, s5 + n:s5 + n + w]

        bu_r, bu_i, t1, t2, XR, XI, rho4 = (S(n * JW) for n in range(7))
        vec_rows, h0_rows_r, h0_rows_i, n_rows = (S(9 * JW + n * P, P) for n in range(4))
        um = Z(32, NI)
        tab = [(xkv[:, 0:JW], xkv[:, JW:2 * JW]), (S(7 * JW), S(8 * JW))]
        pz = 24 * NT
        so = BT[:, 0].rearrange("p j q -> p (j q)")
        bn_r, bn_i, bb_r, bb_i, btmp = (zz(pz + 256 * n, 256) for n in range(5))
        Bx = zz(pz + 1280, 1024)
        cn = zz(pz + 2304, 512)
        Cx = zz(pz + 2816, 1024)

        at = [0]

        def sm(w):
            at[0] += w
            return small[:, at[0] - w:at[0]]

        vec = sm(80)
        V_LDT, V_ARE, V_AIM, V_GMIX, V_GFFN, V_GPLE, V_D, V_BGLU = 0, 16, 32, 48, 56, 64, 72, 76

        def v(off, n):
            return vec[:, off:off + n]

        ssq, rstd = sm(4), sm(4)
        dt_, adr, mag, fr, fr_r = sm(16), sm(16), sm(16), sm(32), sm(32)
        sc = sm(32)
        ab_r, ab_i, nr, den, co_r, co_i, tm = (sm(16) for _ in range(7))
        h0T = sm(256)
        ah = sm(256)
        n0T = sm(36)
        fin_s = sm(256)
        fin_p = sm(32)
        asT = sm(24)
        gb = sm(2)
        m09 = sm(9)
        brb = sm(32)
        assert at[0] <= 1280, at

        v_tok = xkv[:, 0:TT * 512].rearrange("p (t d) -> p t d", t=TT)
        qw2, qn2 = ([xkv[:, a:a + 64] for a in (a0, a0 + 64)] for a0 in (1536, 1664))
        sgl = xkv[:, 1792:1792 + 4 * NT]
        cp_rows, nT_rows = sgl[:, 0:512], sgl[:, 512:640]
        ig, lf, bb, mm, arow, wrow, tmpr = (hrow[0:H, 384 * n:384 * n + 384] for n in range(7))
        kw_all = att[:, 0:H * 384]
        ml = 6 * SW

        def M(a, n):
            return ring[:, ml + a:ml + a + n]

        et2, bc2 = (M(0, 448), M(448, 448)), (M(896, 384), M(1280, 384))
        den_a = M(1664, NT)
        vx2 = [M(2048 + 1024 * n, 1024).rearrange("p (b e) -> p b e", b=NB) for n in range(2)]
        C0 = ring[:, 8 * SW:10 * SW].rearrange("p (h b e) -> p h b e", h=H, b=NB)

        acc = zz(ZK * NT, TT * D).rearrange("p (t d) -> p t d", t=TT)
        btab = [zz(ZU * NT, D), zz(ZQ * NT, D), att[:, 0:D]]
        wr_sb = zz(6144, 256)
        mg, ms, mu = (zz(6400 + 512 * n, 512) for n in range(3))
        m0_ = 28 * NT
        sel = zz(m0_, 192).rearrange("p (t s) -> p t s", t=TT)
        selw = zz(m0_ + 192, 384).rearrange("p (t a s) -> p t a s", t=TT, a=2)
        onehot = zz(m0_ + 576, 64)
        p_lo, p_hi = zz(m0_ + 640, 384), zz(m0_ + 1024, 384)
        rk = zz(m0_ + 1408, 99).rearrange("p (t e) -> p t e", t=TT)
        wt = zz(m0_ + 1507, 99).rearrange("p (t e) -> p t e", t=TT)
        lg, msk, gtm, eqm, exw = (zz(m0_ + 1606 + 96 * n, 96).rearrange("p (t e) -> p t e", t=TT)
                                  for n in range(5))
        mtop = zz(m0_ + 2086, 24).rearrange("p (t e) -> p t e", t=TT)
        mcol = zz(m0_ + 2110, 12)
        nov, cinc, ind = (zz(m0_ + 2122 + 32 * n, 32) for n in range(3))
        opass = zz(m0_ + 2218, 4)
        dtab = zz(m0_ + 2222, 2 * EXTRA)
        obase = zz(m0_ + 2262, EXTRA)
        islot = zz(m0_ + 2282, SLOTS)
        xs, xsT, hT, yb, hb = (hnT[:, 512 * n:512 * n + 512] for n in range(5))
        pproj = zz(5632, TT * D).rearrange("p (t d) -> p t d", t=TT)
        gfin = ring[:, 8 * SW:8 * SW + D]
        p_tok = ring[:, 9 * SW:9 * SW + TT * 256].rearrange("p (t d) -> p t d", t=TT)
        pT = ring[:, 10 * SW:10 * SW + 2 * 384].rearrange("p (k n) -> p k n", k=2)

        slot_full = [sem(f"slot_full{s}") for s in range(RING)]
        slot_free = [sem(f"slot_free{s}") for s in range(RING)]
        cst_full, x_full, vec_full, wif_full = sem("cst_full"), sem("x_full"), sem("vec_full"), sem("wif_full")
        bn_full, st_full, gb_full, c0_full = sem("bn_full"), sem("st_full"), sem("gb_full"), sem("c0_full")
        bt_full, wr_full, res_full, ple_full, gfin_full = (sem(n) for n in (
            "bt_full", "wr_full", "res_full", "ple_full", "gfin_full"))
        stored, stored_pool = sem("stored"), sem("stored_pool")
        zeroed = sem("zeroed")
        ssq_ready, sd_ready = sem("ssq_ready"), sem("sd_ready")
        xn_ready, xT_done, hnT_ready = sem("xn_ready"), sem("xT_done"), sem("hnT_ready")
        vecT_done, vec_ready = sem("vecT_done"), sem("vec_ready")
        ldt_ready = sem("ldt_ready")
        par_act, par_dve = sem("par_act"), sem("par_dve")
        bx_ready, bxT_done, bct_ready = sem("bx_ready"), sem("bxT_done"), sem("bct_ready")
        stT_done, stT_ready = sem("stT_done"), sem("stT_ready")
        z_done, z_ready = sem("z_done"), sem("z_ready")
        gate_done, gate_rows, gate_act, row_ready, R_ready = (sem(n) for n in (
            "gate_done", "gate_rows", "gate_act", "row_ready", "R_ready"))
        asT_done, asT_ready = sem("asT_done"), sem("asT_ready")
        fb_ready, fb_red, tab_ready, um_ready = (sem(n) for n in (
            "fb_ready", "fb_red", "tab_ready", "um_ready"))
        bu_done, bu_ready, rotin_done, rotout_done, s5d = (sem(n) for n in (
            "bu_done", "bu_ready", "rotin_done", "rotout_done", "s5d"))
        fin_ready, finT_done, finT_ready = sem("fin_ready"), sem("finT_done"), sem("finT_ready")
        y_done, yd_ready, gelu_ready, glu_done, sgl_ready, ys_ready = (sem(n) for n in (
            "y_done", "yd_ready", "gelu_ready", "glu_done", "sgl_ready", "ys_ready"))
        g_sig = sem("g_sig")
        kvT_done, kv_ready, rho_ready = sem("kvT_done"), sem("kv_ready"), sem("rho_ready")
        E_done, bc_done, bc_ready, em_ready, ex_ready, S_done, P_ready = (sem(n) for n in (
            "E_done", "bc_done", "bc_ready", "em_ready", "ex_ready", "S_done", "P_ready"))
        qw_ready, qn_ready, N_done, den_done, ym_ready = (sem(n) for n in (
            "qw_ready", "qn_ready", "N_done", "den_done", "ym_ready"))
        vx_ready, C_done, C_half, C_ready, att_d = (sem(n) for n in (
            "vx_ready", "C_done", "C_half", "C_ready", "att_d"))
        abs_ready = sem("abs_ready")
        cp_ready, nT_done, nT_ready = sem("cp_ready"), sem("nT_done"), sem("nT_ready")
        up_done, up_dve, merged = sem("up_done"), sem("up_dve"), sem("merged")
        out_done, h_ready = sem("out_done"), sem("h_ready")
        ch = sem("dve_chain")
        ach = sem("act_chain")
        rl_done, rl_ready, mask_ready, rank_done, tab_made = (sem(n) for n in (
            "rl_done", "rl_ready", "mask_ready", "rank_done", "tab_made"))
        wtT_done, wtT_ready, bd_done, acc_ready = (sem(n) for n in (
            "wtT_done", "wtT_ready", "bd_done", "acc_ready"))
        ob_done, cnt_ready = sem("ob_done"), sem("cnt_ready")
        sel_ready, selw_ready, oh_ready = sem("sel_ready"), sem("selw_ready"), sem("oh_ready")
        gath_done, xs_ready, xsT_done, xsT_ready = (sem(n) for n in (
            "gath_done", "xs_ready", "xsT_done", "xsT_ready"))
        g_done, u_done, g_ready, s_ready, u_ready, gu_ready, hb_ready = (sem(n) for n in (
            "g_done", "u_done", "g_ready", "s_ready", "u_ready", "gu_ready", "hb_ready"))
        hTt_done, hT_ready, pw_done, pw_ready, dn_done, y_ready, sc_done, acc_add = (sem(n) for n in (
            "hTt_done", "hT_ready", "pw_done", "pw_ready", "dn_done", "y_ready", "sc_done", "acc_add"))
        pj_done, pj_ready, pTt_done, pT_ready = (sem(n) for n in (
            "pj_done", "pj_ready", "pTt_done", "pT_ready"))
        gt_done, gt_sig, fin_h, out_ready = sem("gt_done"), sem("gt_sig"), sem("fin_h"), sem("out_ready")

        block = ctx.enter_context(nc.Block())

        w_in = t["w_in"][0].rearrange("(k p) n -> p k n", p=P)

        def zcol(ch_):
            return 256 * ch_ if ch_ < 10 else 2568 + 256 * (ch_ - 10)

        def z_slot(ch_):
            i = ch_ if ch_ < 15 else ch_ + 3
            return i % ZG, i // ZG

        def w3(s, k, n):
            return ring[:, s * SW:s * SW + k * n].rearrange("p (k n) -> p k n", k=k)

        wexp = [t[n][0].rearrange("e (k p) n -> e p k n", p=P) for n in ("w_gate", "w_up", "w_down")]
        USED0 = [5, 4, 4, 4, 3, 3, 0, 0, 1, 1, 1, 1]
        ZSTAGE = [range(10, 15), range(15, 20), range(20, 24), range(24, 28)]
        ZHEAD = [(29, 30), (31, 32), (33, 34), (35,)]
        GLU_BANK = [1, 5, 6, 0]

        def z_bank(n):
            return n % 4 if n < ZGM else 0

        WOUT = [10, 11, 8, 9]

        def rows256(name, i):
            return t[name][0, 256 * i:256 * i + 256].rearrange("(k p) n -> p k n", p=P)

        @block.sync
        def _(sp):
            xp = t["x_prompt"][0].rearrange("(t p) d -> p t d", p=P)
            xd = t["x_sample"].rearrange("b l d -> (b l) d")
            for tt in range(2):
                sp.dma_start(x3[:, tt, :], xp[:, tt, :]).then_inc(x_full, 16)
            sp.dma_start(x3[0:64, 2, :], xd).then_inc(x_full, 16)
            sp.dma_start(cst[:, :], t["cst"]).then_inc(cst_full, 16)

            def load(s, src, k=2, n=D):
                sp.dma_start(w3(s, k, n), src).then_inc(slot_full[s], 16)

            def load_z(ch_):
                s, use = z_slot(ch_)
                if use:
                    sp.wait_ge(slot_free[s], use)
                load(s, w_in[:, :, zcol(ch_):zcol(ch_) + 256], KD, 256)

            sp.wait_ge(vec_full, 16 * 8)
            for ch_ in range(15):
                load_z(ch_)
            sp.wait_ge(slot_free[3], 2)
            load(3, t["ssm_w_glu"][0].rearrange("(k p) n -> p k n", p=P), 4, 512)
            for i in range(2):
                sp.wait_ge(slot_free[4 + i], 2)
                load(4 + i, rows256("w_ssm_up", i))
            load_z(15)
            load_z(16)
            sp.wait_ge(y_done, NJ)
            sp.wait_ge(fin_ready, 4 * NJ)
            for h in range(H):
                sp.dma_start(C0[:, h], t["state_ml_c"][0, :, h].rearrange("b d e -> d b e")).then_inc(c0_full, 16)
            sp.wait_ge(slot_free[3], 3)
            load(3, rows256("w_ml_up", 0))
            load_z(17)
            for i in range(2):
                load(WOUT[i], rows256("w_out", i))
            sp.wait_ge(slot_free[0], 4)
            load(0, rows256("w_ml_up", 1))

            def load_first(s, e=0):
                if USED0[s]:
                    sp.wait_ge(slot_free[s], USED0[s])
                load(s, wexp[s // 4][e, :, 2 * (s % 4):2 * (s % 4) + 2, :])

            for h in range(H):
                sp.wait_ge(C_ready, h + 1)
                sp.dma_start(o["cs"][0, :, h].rearrange("b d e -> d b e"), C0[:, h]).then_inc(stored, 16)
            sp.wait_ge(ym_ready, H)
            sp.dma_start(acc[:, 0:2, :], xp).then_inc(res_full, 16)
            sp.dma_start(acc[0:64, 2, :], xd).then_inc(res_full, 16)
            sp.dma_start(wr_sb.rearrange("p (k e) -> p k e", k=KD), t["w_router"][0].rearrange("(k p) e -> p k e", p=P)).then_inc(wr_full, 16)
            sp.wait_ge(stored, 16 * H)
            for i in range(2, 4):
                load(WOUT[i], rows256("w_out", i))
            sp.wait_ge(zeroed, 7)
            sp.dma_start(btab[2][0:NE, :], t["b_down"][0]).then_inc(bt_full, 16)
            for s in (1, 2, 4, 5, 6, 7):
                load_first(s)
            sp.wait_ge(zeroed, 8)
            sp.dma_start(btab[0][0:NE, :], t["b_gate"][0]).then_inc(bt_full, 16)
            for s in (0, 3):
                load_first(s)
            sp.wait_ge(zeroed, 10)
            sp.dma_start(btab[1][0:NE, :], t["b_up"][0]).then_inc(bt_full, 16)
            for s in range(8, RING):
                load_first(s)

            def load_pass(e, n):
                for s in range(RING):
                    sp.wait_ge(slot_free[s], n + USED0[s])
                    k = 2 * (s % 4)
                    sp.dma_start(w3(s, 2, D), wexp[s // 4][bass.ds(e, 1), :, k:k + 2, :].rearrange("a p k n -> (a p) k n")).then_inc(slot_full[s], 16)

            with sp.Fori(1, NE) as p:
                load_pass(p, p)
            sp.wait_ge(cnt_ready, 1)
            extra = sp.value_load(cnt_i[0:1, 0:1], min_val=0, max_val=EXTRA)
            with sp.If(extra > 0):
                with sp.Fori(0, extra) as q:
                    e = sp.value_load(cnt_i[0:1, bass.ds(q + 1, 1)], min_val=0, max_val=NE - 1)
                    load_pass(e, q + NE)
            for s in range(4):
                sp.wait_ge(slot_free[s], extra + (NE + USED0[s]))
                sp.dma_start(w3(s, 2, D), t["w_ple_gate"][0, 256 * s:256 * s + 256].rearrange("(k p) n -> p k n", p=P)).then_inc(slot_full[s], 16)
            sp.wait_ge(slot_free[4], extra + (NE + USED0[4]))
            sp.dma_start(w3(4, 2, D), t["w_ple_proj"][0].rearrange("(k p) n -> p k n", p=P)).then_inc(slot_full[4], 16)
            for s in (8, 9, 10):
                sp.wait_ge(slot_free[s], extra + (NE + USED0[s]))
            sp.dma_start(gfin, t["g_final"].rearrange("(a n) -> a n", a=1).to_broadcast([P, D])).then_inc(gfin_full, 16)
            sp.dma_start(p_tok[:, 0:2, :], t["p_prompt"][0, 0].rearrange("(t p) d -> p t d", p=P)).then_inc(ple_full, 16)
            sp.dma_start(p_tok[0:64, 2, :], t["p_sample"][0].rearrange("b l d -> (b l) d")).then_inc(ple_full, 16)
            yp = o["yp"][0].rearrange("(t p) d -> t p d", p=P)
            for tt in range(TT):
                sp.wait_ge(out_ready, tt + 1)
                if tt < 2:
                    sp.dma_start(yp[tt], acc[:, tt, :]).then_inc(stored, 16)
                else:
                    sp.dma_start(o["ys"].rearrange("b l d -> (b l) d"), acc[0:64, 2, :]).then_inc(stored, 16)
            sp.wait_ge(stored, 16 * (H + TT))
            sp.wait_ge(stored_pool, 16 * 9)

        @block.gpsimd
        def _(pool):
            ms_ = nc.gpsimd.memset
            ms_(xkv[64:128, 2 * D:3 * D], 0.0).then_inc(zeroed, 1)
            pool.wait_ge(zeroed, 1)
            ms_(rows[:, :], 0.0).then_inc(zeroed, 1)
            pool.wait_ge(zeroed, 2)
            ms_(hrow[0:H, 4 * 384:6 * 384], 0.0).then_inc(zeroed, 1)
            pool.wait_ge(zeroed, 3)
            pool.wait_ge(slot_full[1], 16)
            for n, name in enumerate(("ssm_b_re", "ssm_b_im")):
                src = t[name][0].rearrange("g s h -> (g s) h").rearrange("(k q) h -> q k h", q=P)
                pool.dma_start((bn_r, bn_i)[n].rearrange("p (k h) -> p k h", k=NK), src).then_inc(bn_full, 16)
            for n, name in enumerate(("ssm_c_re", "ssm_c_im")):
                src = t[name][0].rearrange("g h s -> (g h) s").rearrange("(j q) s -> q j s", q=P)
                pool.dma_start(cn[:, 256 * n:256 * n + 256].rearrange("p (j s) -> p j s", j=NJ), src).then_inc(bn_full, 16)
            pool.dma_start(h0_rows_r, t["state_ssm_re"][0].rearrange("b g s -> b (g s)").rearrange("b (k q) -> b k q", q=P).rearrange("b k q -> (b k) q")).then_inc(st_full, 16)
            pool.dma_start(h0_rows_i, t["state_ssm_im"][0].rearrange("b g s -> b (g s)").rearrange("b (k q) -> b k q", q=P).rearrange("b k q -> (b k) q")).then_inc(st_full, 16)
            pool.dma_start(n_rows[0:32, :], t["state_ml_n"][0].rearrange("b h d -> (b h) d")).then_inc(st_full, 16)
            pool.dma_start(gb[0:H, 0:1], t["ml_b_ig"][0].rearrange("(a b) -> a b", b=1)).then_inc(gb_full, 16)
            pool.dma_start(gb[0:H, 1:2], t["ml_b_fg"][0].rearrange("(a b) -> a b", b=1)).then_inc(gb_full, 16)
            pool.dma_start(m09[0:H, 1:9], t["state_ml_m"][0].rearrange("b h -> h b"), allow_slow_non_contiguous=True).then_inc(gb_full, 16)
            pool.dma_start(brb, t["b_router"].to_broadcast([P, NE])).then_inc(gb_full, 16)
            wif = att[:, 0:KD * 36].rearrange("p (k n) -> p k n", k=KD)
            ms_(att[:, 0:KD * 36], 0.0).then_inc(zeroed, 1)
            pool.wait_ge(zeroed, 4)
            pool.dma_start(wif[:, :, 0:4], w_in[:, :, 2560:2564]).then_inc(wif_full, 16)
            pool.dma_start(wif[:, :, 32:36], w_in[:, :, 2564:2568]).then_inc(wif_full, 16)

            pool.wait_ge(gate_done, 1)
            ms_(kw_all.rearrange("p (h t) -> p h t", h=H)[64:128, :, 256:384], 0.0).then_inc(zeroed, 1)
            pool.wait_ge(zeroed, 5)

            for j in range(NJ):
                if j == NJ - 1:
                    pool.wait_ge(rotout_done, 2 * j)
                    ms_(v_tok[64:128, 2, :], 0.0).then_inc(zeroed, 1)
                    pool.wait_ge(zeroed, 6)
                for n, X in enumerate((XR, XI)):
                    X3 = X.rearrange("p (i n) -> p i n", i=NI)
                    pool.wait_ge(rotout_done, 2 * j + n + 1)
                    f4 = fin_s[:, 128 * n:128 * n + 128].rearrange("p (b k) -> p k b", b=NB)
                    nc.gpsimd.tensor_copy(f4[:, NI * j:NI * j + NI, :],
                                          X3[:, :, NP_TOK + LB - 1:NT:LB]).then_inc(fin_ready, 1)
                    pool.wait_ge(fin_ready, 4 * j + 2 * n + 1)
                    nc.gpsimd.tensor_copy(fin_p[:, 16 * n + NI * j:16 * n + NI * j + NI],
                                          X3[:, :, NP_TOK - 1:NP_TOK].rearrange("p i a -> p (i a)")).then_inc(fin_ready, 1)
                    pool.wait_ge(fin_ready, 4 * j + 2 * n + 2)
            pool.wait_ge(finT_ready, 3)
            
            pool.dma_start(o["rs"][0].rearrange("b g s -> b (g s)").rearrange("b (k q) -> (b k) q", q=P), so[:, 0:128]).then_inc(stored_pool, 16)
            pool.dma_start(o["is"][0].rearrange("b g s -> b (g s)").rearrange("b (k q) -> (b k) q", q=P), so[:, 128:256]).then_inc(stored_pool, 16)
            pool.dma_start(o["rp"][0, 0].rearrange("(k g) s -> k (g s)", g=2), so[0:16, 256:384]).then_inc(stored_pool, 16)
            pool.dma_start(o["ip"][0, 0].rearrange("(k g) s -> k (g s)", g=2), so[16:32, 256:384]).then_inc(stored_pool, 16)
            pool.wait_ge(row_ready, 1)
            pool.dma_start(o["mp"][0].rearrange("b h -> h b"), mm[:, NP_TOK - 1:NP_TOK], allow_slow_non_contiguous=True).then_inc(stored_pool, 16)
            pool.dma_start(o["ms"][0].rearrange("b h -> h b"), mm[:, NP_TOK + LB - 1:NT:LB], allow_slow_non_contiguous=True).then_inc(stored_pool, 16)
            pool.wait_ge(cp_ready, H)
            pool.dma_start(o["cp"][0, 0].rearrange("h d e -> d h e"), cp_rows.rearrange("p (h e) -> p h e", h=H)).then_inc(stored_pool, 16)
            pool.wait_ge(nT_ready, 1)
            pool.dma_start(o["ns"][0].rearrange("b h d -> (b h) d"), nT_rows[0:32, :]).then_inc(stored_pool, 16)
            pool.dma_start(o["np"][0, 0], nT_rows[32:36, :]).then_inc(stored_pool, 16)
            pool.wait_ge(C_ready, H)
            pool.wait_ge(ym_ready, H)
            ms_(btab[2], 0.0).then_inc(zeroed, 1)
            pool.wait_ge(up_done, KD)
            pool.wait_ge(zeroed, 7)
            ms_(btab[0], 0.0).then_inc(zeroed, 1)
            pool.wait_ge(zeroed, 8)
            ms_(acc[64:128, 2, :], 0.0).then_inc(zeroed, 1)
            pool.wait_ge(up_done, 2 * KD)
            pool.wait_ge(zeroed, 9)
            ms_(btab[1], 0.0).then_inc(zeroed, 1)
            pool.wait_ge(merged, KD)
            pool.wait_ge(zeroed, 10)
            ms_(zz(m0_ + 640, 768), 0.0).then_inc(zeroed, 1)
            pool.wait_ge(zeroed, 11)
            ms_(lg.rearrange("p t e -> p (t e)"), 0.0).then_inc(zeroed, 1)

        @block.scalar
        def _(act):
            a = nc.scalar.activation
            cnt = [0]

            def link(ins):
                cnt[0] += 1
                ins.then_inc(ach, 1)
                act.wait_ge(ach, cnt[0])

            fl = "(a b) -> a b"
            for r0, name, n in ((V_ARE, "ssm_a_re", 16), (V_AIM, "ssm_a_im", 16)):
                act.dma_start(vec_rows[r0:r0 + n, :], t[name][0].rearrange("(k g) s -> k (g s)", g=2)).then_inc(vec_full, 16)
            for r0, name in ((V_GMIX, "g_mix"), (V_GFFN, "g_ffn"), (V_GPLE, "g_ple")):
                act.dma_start(vec_rows[r0:r0 + 8, :], t[name][0].rearrange(fl, b=P)).then_inc(vec_full, 16)
            act.dma_start(vec_rows[V_D:V_D + 4, :], t["ssm_d"][0].rearrange("(j g) h -> j (g h)", g=8)).then_inc(vec_full, 16)
            act.dma_start(vec_rows[V_BGLU:V_BGLU + 4, :], t["ssm_b_glu"][0].rearrange(fl, b=P)).then_inc(vec_full, 16)
            act.dma_start(ssq[0:16, 0:2], t["ssm_log_dt"][0].rearrange("(k g) -> k g", g=2)).then_inc(vec_full, 16)
            for tt in range(TT):
                act.wait_ge(x_full, 48)
                if tt == 2:
                    act.wait_ge(zeroed, 1)
                a(S(tt * D, D), x3[:, tt, :], ACT.Square, accum_out=rstd[:, tt:tt + 1]).then_inc(ssq_ready, 1)
            act.wait_ge(sd_ready, 1)
            link(a(rstd[:, 0:3], rstd[:, 0:3], ACT.Sqrt))
            act.sem_inc(sd_ready, 1)
            act.wait_ge(vec_ready, 1)
            a(dt_, v(V_LDT, 16), ACT.Exp).then_inc(par_act, 1)
            act.wait_ge(par_dve, 1)
            a(mag, adr, ACT.Exp).then_inc(par_act, 1)
            act.wait_ge(par_dve, 2)
            act.wait_ge(cst_full, 16)
            a(sc, fr_r, ACT.Sin, scale=TWO_PI).then_inc(par_act, 1)
            def z_evac(n):
                act.wait_ge(z_done, n + 1)
                a(Z(n), bank[z_bank(n)][:, 0:NT], ACT.Copy).then_inc(z_ready, 1)

            for n in range(8):
                z_evac(n)
            for n in range(4):
                act.wait_ge(bxT_done, n + 1)
                dst = (BT, CT)[n // 2][:, n % 2]
                a(dst.rearrange("p j q -> p (j q)"), bank[4 + n][:, :], ACT.Copy).then_inc(bct_ready, 1)
            act.wait_ge(stT_done, 1)
            a(h0T, bank[4][:, 0:256], ACT.Copy).then_inc(stT_ready, 1)
            a(n0T[:, 0:32], bank[4][:, 256:288], ACT.Copy).then_inc(stT_ready, 1)

            def masked_u(j):
                for i in range(NI):
                    a(um[:, i * NT:i * NT + NT], Z(ZU + j), ACT.Copy, scale=c("imask")[:, i:i + 1]).then_inc(um_ready, 1)

            def turns(j):
                F = tab[j % 2][1]
                for i in range(NI):
                    a(F[:, i * NT:i * NT + NT], c("tloc"), ACT.Copy, scale=fr[:, NI * j + i:NI * j + i + 1]).then_inc(fb_ready, 1)

            def sines(j):
                cos_, sin_ = tab[j % 2]
                act.wait_ge(fb_red, j + 1)
                a(cos_, sin_, ACT.Abs).then_inc(tab_ready, 1)
                a(sin_, sin_, ACT.Sin, scale=TWO_PI).then_inc(tab_ready, 1)
                act.wait_ge(tab_ready, 3 * j + 1)
                a(cos_, cos_, ACT.Sin, scale=-TWO_PI, bias=c("halfpi")).then_inc(tab_ready, 1)

            def gelu(j):
                act.wait_ge(yd_ready, j + 1)
                a(Z(ZU + j), Z(ZU + j), ACT.Gelu_apprx_tanh).then_inc(gelu_ready, 1)

            masked_u(0)
            act.wait_ge(xT_done, KD)
            turns(0)
            for n in range(8, 10):
                z_evac(n)
            sines(0)
            for j in range(NJ):
                if j:
                    act.wait_ge(rotin_done, j)
                for q in range(8):
                    act.wait_ge(bu_done, 8 * j + q + 1)
                    dst = (bu_r, bu_i)[q % 2][:, (q // 2) * NT:(q // 2 + 1) * NT]
                    a(dst, bank[4 + q % 3][:, 0:NT], ACT.Copy).then_inc(bu_ready, 1)
                if j:
                    act.wait_ge(rotout_done, 2 * j)
                for i in range(NI):
                    a(rho4[:, i * NT:i * NT + NT], c("start"), ACT.Copy, scale=mag[:, NI * j + i:NI * j + i + 1]).then_inc(rho_ready, 1)
                if j < NJ - 1:
                    turns(j + 1)
                    masked_u(j + 1)
                if j == 1:
                    act.wait_ge(gate_rows, 3)
                    link(a(tmpr[:, 0:NT], tmpr[:, 0:NT], ACT.Abs))
                    link(a(tmpr[:, 0:NT], tmpr[:, 0:NT], ACT.Exp, scale=-1.0))
                    a(tmpr[:, 0:NT], tmpr[:, 0:NT], ACT.Ln, bias=1.0).then_inc(gate_act, 1)
                if j == 2:
                    act.wait_ge(row_ready, 1)
                    a(rows[0:H, NT:2 * NT], mm[:, 0:NT], ACT.Exp, scale=-1.0).then_inc(R_ready, 1)
                    a(rows[0:H, 2 * NT:2 * NT + 64], rows[0:H, 2 * NT:2 * NT + 64], ACT.Exp).then_inc(R_ready, 1)
                    a(wrow[:, 0:NT], wrow[:, 0:NT], ACT.Exp).then_inc(R_ready, 1)
                zn = ZSTAGE[j]
                for n in zn[:2]:
                    z_evac(n)
                if j == 2:
                    act.wait_ge(asT_done, 1)
                    a(asT[:, 0:12], bank[4][:, 0:12], ACT.Copy).then_inc(asT_ready, 1)
                    a(asT[:, 12:24], bank[4][:, 12:24], ACT.Copy, scale=KSCALE).then_inc(asT_ready, 1)
                if j < NJ - 1:
                    sines(j + 1)
                else:
                    act.wait_ge(asT_ready, 2)
                    act.wait_ge(zeroed, 6)
                    for g in range(2 * H):
                        h = g % H
                        act.wait_ge(kvT_done, g + 1)
                        for tt in range(TT):
                            w = TW[tt]
                            src = bank[4 + g % 3][0:w, tt * P:tt * P + P]
                            if g < H:
                                a(kw_all[0:w, h * 384 + tt * P:h * 384 + tt * P + P], src, ACT.Copy,
                                  scale=asT[0:w, 12 + tt * H + h:13 + tt * H + h]).then_inc(kv_ready, 1)
                            else:
                                a(v_tok[0:w, tt, h * P:h * P + P], src, ACT.Copy).then_inc(kv_ready, 1)
                for n in zn[2:]:
                    z_evac(n)
                if j:
                    gelu(j - 1)

            def bc_copy(h):
                act.wait_ge(bc_done, h + 1)
                if h >= 2:
                    act.wait_ge(C_ready, h - 1)
                a(bc2[h % 2], bank[4][:, 0:384], ACT.Copy).then_inc(bc_ready, 1)

            def decay_exp(h):
                act.wait_ge(em_ready, h + 1)
                et = et2[h % 2]
                for n, (c0, c1) in enumerate(((0, 256), (256, 384), (384, 448))):
                    a(et[:, c0:c1], et[:, c0:c1], ACT.Exp, bias=asT[:, n * H + h:n * H + h + 1]).then_inc(ex_ready, 1)

            act.wait_ge(rotout_done, 2 * NJ)
            bc_copy(0)
            decay_exp(0)
            gelu(NJ - 1)
            z_evac(ZGM)
            act.wait_ge(finT_done, 3)
            for n in range(3):
                rr = 128 if n < 2 else 32
                a(so[0:rr, 128 * n:128 * n + 128], bank[7][0:rr, 128 * n:128 * n + 128], ACT.Copy).then_inc(finT_ready, 1)
            for n in range(4):
                act.wait_ge(glu_done, n + 1)
                a(sgl[:, n * NT:n * NT + NT], bank[GLU_BANK[n]][:, 0:NT], ACT.Sigmoid, bias=v(V_BGLU + n, 1)).then_inc(sgl_ready, 1)
            act.wait_ge(z_ready, ZGM)
            a(Z(ZO, 4), Z(ZO, 4), ACT.Sigmoid).then_inc(g_sig, 1)
            a(Z(ZGS, 8), Z(ZGS, 8), ACT.Sigmoid).then_inc(g_sig, 1)
            for h in range(H):
                act.wait_ge(den_done, h + 1)
                if h:
                    act.wait_ge(ym_ready, h)
                a(den_a, bank[6][:, 0:NT], ACT.Abs).then_inc(abs_ready, 1)
                if h < H - 1:
                    bc_copy(h + 1)
                    decay_exp(h + 1)
                for n in ZHEAD[h]:
                    z_evac(n)
            act.wait_ge(z_ready, ZT)
            a(Z(ZGM, 8), Z(ZGM, 8), ACT.Sigmoid).then_inc(g_sig, 1)
            act.wait_ge(nT_done, 1)
            a(nT_rows[0:36, :], bank[4][0:36, 0:P], ACT.Copy).then_inc(nT_ready, 1)

            act.wait_ge(stored_pool, 16 * 9)
            for tt in range(TT):
                act.wait_ge(h_ready, 2 * tt + 2)
                a(x3[:, tt, :], acc[:, tt, :], ACT.Square, accum_out=rstd[:, tt:tt + 1]).then_inc(ssq_ready, 1)
            act.wait_ge(sd_ready, 3)
            link(a(rstd[:, 0:3], rstd[:, 0:3], ACT.Sqrt))
            act.sem_inc(sd_ready, 1)
            act.wait_ge(rl_ready, 1)
            a(exw.rearrange("p t e -> p (t e)"), exw.rearrange("p t e -> p (t e)"), ACT.Exp).then_inc(rl_ready, 1)
            act.wait_ge(wtT_done, 1)
            a(p_lo[0:NE, :], bank[4][0:NE, 0:384], ACT.Copy).then_inc(wtT_ready, 1)

            def experts_act(n, prologue=False):
                if not prologue:
                    act.wait_ge(g_ready, n + 1)
                    a(ms, mg, ACT.Sigmoid, scale=ALPHA).then_inc(s_ready, 1)

            def gather_act(n):
                act.wait_ge(gath_done, n + 1)
                a(xs, bank[2][:, :], ACT.Copy).then_inc(xs_ready, 1)

            def down_act(n):
                act.wait_ge(hTt_done, n + 1)
                a(hT, bank[3][:, :], ACT.Copy).then_inc(hT_ready, 1)

            def y_act(n):
                act.wait_ge(dn_done, n + 1)
                a(yb, bank[5][:, :], ACT.Copy).then_inc(y_ready, 1)

            gather_act(0)
            with act.Fori(0, NE) as p:
                experts_act(p)
                gather_act(p + 1)
                down_act(p)
                y_act(p)
            act.wait_ge(cnt_ready, 1)
            extra = act.value_load(cnt_i[0:1, 0:1], min_val=0, max_val=EXTRA)
            with act.If(extra > 0):
                with act.Fori(0, extra) as q:
                    gather_act(q + (NE + 1))
                    experts_act(q + NE)
                    down_act(q + NE)
                    y_act(q + NE)

            for tt in range(TT):
                if tt == 0:
                    act.wait_ge(acc_add, extra * 6 + (6 * (NE + 1) + 2))
                a(x3[:, tt, :], acc[:, tt, :], ACT.Square, accum_out=rstd[:, tt:tt + 1]).then_inc(ssq_ready, 1)
            act.wait_ge(sd_ready, 5)
            cnt[0] += 1
            a(rstd[:, 0:3], rstd[:, 0:3], ACT.Sqrt).then_inc(ach, 1)
            act.wait_ge(ach, cnt[0])
            act.sem_inc(sd_ready, 1)
            for k in range(2):
                act.wait_ge(pTt_done, k + 1)
                a(pT[:, k, :], bank[4 + k][:, 0:384], ACT.Copy).then_inc(pT_ready, 1)
            for n in range(6):
                act.wait_ge(pj_done, n + 1)
                a(pproj[:, n // 2, (n % 2) * 512:(n % 2) * 512 + 512], bank[4 + n % 4][:, :], ACT.Copy).then_inc(pj_ready, 1)
            for n in range(6):
                act.wait_ge(gt_done, n + 1)
                a(x3[:, n // 2, (n % 2) * 512:(n % 2) * 512 + 512], bank[n % 2][:, :], ACT.Sigmoid).then_inc(gt_sig, 1)
            for tt in range(TT):
                act.wait_ge(fin_h, 2 * tt + 2)
                a(x3[:, tt, :], acc[:, tt, :], ACT.Square, accum_out=rstd[:, tt:tt + 1]).then_inc(ssq_ready, 1)
            act.wait_ge(sd_ready, 7)
            link(a(rstd[:, 0:3], rstd[:, 0:3], ACT.Sqrt))
            act.sem_inc(sd_ready, 1)

        @block.vector
        def _(dve):
            V = nc.vector
            cnt = [0]

            def link(ins):
                cnt[0] += 1
                ins.then_inc(ch, 1)
                dve.wait_ge(ch, cnt[0])

            def rms(r, src, dst):
                dve.wait_ge(ssq_ready, 3 * (r + 1))
                V.tensor_scalar(rstd[:, 0:3], rstd[:, 0:3], 1.0 / D, EPS, ALU.mult, ALU.add).then_inc(sd_ready, 1)
                dve.wait_ge(sd_ready, 2 * r + 2)
                link(V.reciprocal(rstd[:, 0:3], rstd[:, 0:3]))
                for tt in range(TT):
                    V.tensor_scalar(dst[:, tt, :], src[:, tt, :], rstd[:, tt:tt + 1], None, ALU.mult).then_inc(xn_ready, 1)

            def hnT_evac(r, g, banks):
                for k in range(KD):
                    dve.wait_ge(xT_done, KD * r + k + 1)
                    V.tensor_scalar(hn3[:, k, :], bank[banks[k % len(banks)]][:, 0:NT], v(g + k, 1), None, ALU.mult).then_inc(hnT_ready, 1)

            dve.wait_ge(vec_full, 16 * 8)
            V.tensor_copy(vec_rows[0:16, :].rearrange("p (g s) -> p g s", g=2),
                          ssq[0:16, 0:2].unsqueeze(2).to_broadcast([16, 2, ST])).then_inc(ldt_ready, 1)
            rms(0, x3, x3)
            dve.wait_ge(vecT_done, 1)
            V.tensor_copy(vec, bank[4][:, 0:80]).then_inc(vec_ready, 1)
            dve.wait_ge(vec_ready, 1)
            hnT_evac(0, V_GMIX, (0, 1, 2, 3))

            dve.wait_ge(par_act, 1)
            V.tensor_tensor(adr, v(V_ARE, 16), dt_, ALU.mult).then_inc(par_dve, 1)
            link(V.tensor_tensor(fr[:, 0:16], v(V_AIM, 16), dt_, ALU.mult))
            link(V.tensor_scalar(fr[:, 0:16], fr[:, 0:16], 1.0 / 6.283185307179586, None, ALU.mult))
            link(V.tensor_scalar(fr_r[:, 0:16], fr[:, 0:16], ROUND, ROUND, ALU.add, ALU.subtract))
            link(V.tensor_tensor(fr[:, 0:16], fr[:, 0:16], fr_r[:, 0:16], ALU.subtract))
            link(V.tensor_scalar(fr[:, 16:32], fr[:, 0:16], 0.25, None, ALU.add))
            link(V.tensor_scalar(fr_r, fr, ROUND, ROUND, ALU.add, ALU.subtract))
            V.tensor_tensor(fr_r, fr, fr_r, ALU.subtract).then_inc(par_dve, 1)
            dve.wait_ge(par_act, 3)
            link(V.tensor_tensor(ab_i, mag, sc[:, 0:16], ALU.mult))
            link(V.tensor_tensor(ab_r, mag, sc[:, 16:32], ALU.mult))
            ar, ai = v(V_ARE, 16), v(V_AIM, 16)
            link(V.tensor_scalar(nr, ab_r, -1.0, None, ALU.add))
            link(V.tensor_tensor(den, ar, ar, ALU.mult))
            link(V.tensor_tensor(tm, ai, ai, ALU.mult))
            link(V.tensor_tensor(den, den, tm, ALU.add))
            link(V.reciprocal(den, den))
            link(V.tensor_tensor(co_r, nr, ar, ALU.mult))
            link(V.tensor_tensor(tm, ab_i, ai, ALU.mult))
            link(V.tensor_tensor(co_r, co_r, tm, ALU.add))
            link(V.tensor_tensor(co_r, co_r, den, ALU.mult))
            link(V.tensor_tensor(co_i, ab_i, ar, ALU.mult))
            link(V.tensor_tensor(tm, nr, ai, ALU.mult))
            link(V.tensor_tensor(co_i, co_i, tm, ALU.subtract))
            link(V.tensor_tensor(co_i, co_i, den, ALU.mult))

            def k3(x_):
                return x_.rearrange("p (k h) -> p k h", k=NK)

            def bck(x_):
                return x_.unsqueeze(2).to_broadcast([P, NK, GW])

            dve.wait_ge(bn_full, 64)
            link(V.tensor_tensor(k3(bb_r), k3(bn_r), bck(co_r), ALU.mult))
            link(V.tensor_tensor(k3(btmp), k3(bn_i), bck(co_i), ALU.mult))
            link(V.tensor_tensor(bb_r, bb_r, btmp, ALU.subtract))
            link(V.tensor_tensor(k3(bb_i), k3(bn_i), bck(co_r), ALU.mult))
            link(V.tensor_tensor(k3(btmp), k3(bn_r), bck(co_i), ALU.mult))
            link(V.tensor_tensor(bb_i, bb_i, btmp, ALU.add))
            for n, src in enumerate((bb_r, bb_i)):
                V.tensor_tensor(Bx[:, 512 * n:512 * n + 512].rearrange("p (k a h) -> p k a h", k=NK, a=2),
                                k3(src).unsqueeze(2).to_broadcast([P, NK, 2, GW]),
                                c("half").unsqueeze(1).unsqueeze(3).to_broadcast([P, NK, 2, GW]), ALU.mult).then_inc(bx_ready, 1)
            for n, m_ in enumerate(("par", "npar")):
                V.tensor_tensor(Cx[:, 512 * n:512 * n + 512].rearrange("p (j a s) -> p j a s", j=NJ, a=2),
                                cn[:, 256 * n:256 * n + 256].rearrange("p (j s) -> p j s", j=NJ).unsqueeze(2).to_broadcast([P, NJ, 2, ST]),
                                c(m_).unsqueeze(1).unsqueeze(3).to_broadcast([P, NJ, 2, ST]), ALU.mult).then_inc(bx_ready, 1)
            dve.wait_ge(stT_ready, 2)
            h0v = h0T.rearrange("p (n b k) -> p n b k", n=2, b=NB)
            ahv = ah.rearrange("p (n b k) -> p n b k", n=2, b=NB)
            tv = bn_r[:, 0:128].rearrange("p (b k) -> p b k", b=NB)

            def bcb(x_):
                return x_.unsqueeze(1).to_broadcast([P, NB, NK])

            link(V.tensor_tensor(ahv[:, 0], h0v[:, 0], bcb(ab_r), ALU.mult))
            link(V.tensor_tensor(tv, h0v[:, 1], bcb(ab_i), ALU.mult))
            link(V.tensor_tensor(ahv[:, 0], ahv[:, 0], tv, ALU.subtract))
            link(V.tensor_tensor(ahv[:, 1], h0v[:, 1], bcb(ab_r), ALU.mult))
            link(V.tensor_tensor(tv, h0v[:, 0], bcb(ab_i), ALU.mult))
            link(V.tensor_tensor(ahv[:, 1], ahv[:, 1], tv, ALU.add))

            def i3(x_):
                return x_.rearrange("p (i n) -> p i n", i=NI)

            s5n = [0]

            def s5link(ins):
                s5n[0] += 1
                ins.then_inc(s5d, 1)
                dve.wait_ge(s5d, s5n[0])

            def reduce_turns(j):
                tmp, F = tab[j % 2]
                dve.wait_ge(fb_ready, 4 * (j + 1))
                s5link(V.tensor_scalar(tmp, F, ROUND, ROUND, ALU.add, ALU.subtract))
                V.tensor_tensor(F, F, tmp, ALU.subtract).then_inc(fb_red, 1)

            reduce_turns(0)
            for j in range(NJ):
                tabc, tabs = tab[j % 2]
                dve.wait_ge(bu_ready, 8 * (j + 1))
                dve.wait_ge(tab_ready, 3 * (j + 1))
                for n, b_ in enumerate((bu_r, bu_i)):
                    first = i3(b_)[:, :, NP_TOK:NT:LB]
                    s5link(V.tensor_tensor(first, first, ahv[:, n, :, NI * j:NI * j + NI].rearrange("p b i -> p i b"), ALU.add))
                s5link(V.tensor_tensor(t1, bu_r, tabc, ALU.mult))
                s5link(V.tensor_tensor(t2, bu_i, tabs, ALU.mult))
                s5link(V.tensor_tensor(t1, t1, t2, ALU.add))
                s5link(V.tensor_tensor(t2, bu_i, tabc, ALU.mult))
                s5link(V.tensor_tensor(bu_r, bu_r, tabs, ALU.mult))
                V.tensor_tensor(t2, t2, bu_r, ALU.subtract).then_inc(rotin_done, 1)
                if j < NJ - 1:
                    reduce_turns(j + 1)
                dve.wait_ge(rotin_done, j + 1)
                dve.wait_ge(rho_ready, 4 * (j + 1))
                s5link(V.tensor_tensor_scan(t1, rho4, t1, 0.0, ALU.mult, ALU.add))
                s5link(V.tensor_tensor_scan(t2, rho4, t2, 0.0, ALU.mult, ALU.add))
                if j:
                    dve.wait_ge(y_done, j)
                    dve.wait_ge(fin_ready, 4 * j)
                s5link(V.tensor_tensor(rho4, t2, tabs, ALU.mult))
                s5link(V.tensor_tensor(XR, t1, tabc, ALU.mult))
                V.tensor_tensor(XR, XR, rho4, ALU.subtract).then_inc(rotout_done, 1)
                dve.wait_ge(rotout_done, 2 * j + 1)
                s5link(V.tensor_tensor(rho4, t2, tabc, ALU.mult))
                s5link(V.tensor_tensor(XI, t1, tabs, ALU.mult))
                V.tensor_tensor(XI, XI, rho4, ALU.add).then_inc(rotout_done, 1)
                dve.wait_ge(rotout_done, 2 * j + 2)
                if j:
                    V.scalar_tensor_tensor(Z(ZU + j - 1), Z(ZU + j - 1), v(V_D + j - 1, 1), bank[7][:, 0:NT], ALU.mult, ALU.add).then_inc(yd_ready, 1)
                if j == 0:
                    dve.wait_ge(gate_done, 1)
                    dve.wait_ge(gb_full, 64)
                    V.tensor_scalar(ig[:, 0:NT], bank[7][0:H, 0:NT], gb[0:H, 0:1], None, ALU.add).then_inc(gate_rows, 1)
                    V.tensor_scalar(lf[:, 0:NT], bank[7][32:32 + H, 0:NT], gb[0:H, 1:2], 0.0, ALU.add, ALU.min).then_inc(gate_rows, 1)
                    V.tensor_scalar(tmpr[:, 0:NT], bank[7][32:32 + H, 0:NT], gb[0:H, 1:2], None, ALU.add).then_inc(gate_rows, 1)
                    dve.wait_ge(gate_rows, 3)
                    link(V.memset(m09[0:H, 0:1], 0.0))
                if j == 1:
                    dve.wait_ge(gate_act, 1)
                    st = c("start")[0:H, :]
                    link(V.tensor_tensor(lf[:, 0:NT], lf[:, 0:NT], tmpr[:, 0:NT], ALU.subtract))
                    link(V.tensor_tensor_scan(bb[:, 0:NT], st, lf[:, 0:NT], 0.0, ALU.mult, ALU.add))
                    link(V.tensor_copy(arow[:, 0:NT], ig[:, 0:NT]))
                    f0 = wrow[:, 0:9]
                    link(V.tensor_copy(f0[:, 0:1], lf[:, 0:1]))
                    link(V.tensor_copy(f0[:, 1:9], lf[:, NP_TOK:NT:LB]))
                    link(V.tensor_tensor(f0, f0, m09[0:H, :], ALU.add))
                    link(V.tensor_tensor(arow[:, 0:1], arow[:, 0:1], f0[:, 0:1], ALU.max))
                    link(V.tensor_tensor(arow[:, NP_TOK:NT:LB], arow[:, NP_TOK:NT:LB], f0[:, 1:9], ALU.max))
                    link(V.tensor_scalar(tmpr[:, 0:NT], st, -1.0, 3.0e38, ALU.add, ALU.mult))
                    link(V.tensor_tensor(lf[:, 0:NT], lf[:, 0:NT], tmpr[:, 0:NT], ALU.add))
                    link(V.tensor_tensor_scan(mm[:, 0:NT], lf[:, 0:NT], arow[:, 0:NT], 0.0, ALU.add, ALU.max))
                    link(V.tensor_tensor(rows[0:H, 0:NT], bb[:, 0:NT], mm[:, 0:NT], ALU.subtract))
                    link(V.tensor_tensor(arow[:, 0:NT], ig[:, 0:NT], bb[:, 0:NT], ALU.subtract))
                    r1 = rows[0:H, 0:NT]
                    r1s = r1[:, NP_TOK:NT].rearrange("p (b l) -> p b l", b=NB)
                    ars = arow[:, NP_TOK:NT].rearrange("p (b l) -> p b l", b=NB)
                    link(V.tensor_tensor(rows[0:H, 2 * NT:2 * NT + 64].rearrange("p (b l) -> p b l", b=NB), r1s,
                                         m09[0:H, 1:9].unsqueeze(2).to_broadcast([H, NB, LB]), ALU.add))
                    link(V.tensor_scalar(wrow[:, 0:NP_TOK], arow[:, 0:NP_TOK], r1[:, NP_TOK - 1:NP_TOK], None, ALU.add))
                    V.tensor_tensor(wrow[:, NP_TOK:NT].rearrange("p (b l) -> p b l", b=NB), ars,
                                    r1s[:, :, LB - 1:LB].to_broadcast([H, NB, LB]), ALU.add).then_inc(row_ready, 1)
            a_n = [0]

            def alink(ins):
                a_n[0] += 1
                ins.then_inc(att_d, 1)
                dve.wait_ge(att_d, a_n[0])

            def n0h(h):
                return n0T[:, 0:32].rearrange("p (b h) -> p b h", b=NB)[:, :, h:h + 1]

            def front(h):
                dve.wait_ge(E_done, h + 1)
                if h >= 2:
                    dve.wait_ge(N_done, h - 1)
                V.tensor_tensor(et2[h % 2], bank[2][:, 0:448], c("amask"), ALU.add).then_inc(em_ready, 1)
                if h == 0:
                    dve.wait_ge(kv_ready, 3 * 2 * H)
                V.tensor_tensor(vx2[h % 2], v_tok[:, 2, h * P:h * P + P].unsqueeze(1).to_broadcast([P, NB, P]),
                                c("seqm").unsqueeze(2).to_broadcast([P, NB, P]), ALU.mult).then_inc(vx_ready, 1)
                dve.wait_ge(bc_ready, h + 1)
                qw, qn = qw2[h % 2], qn2[h % 2]
                V.tensor_tensor(qw, Z(ZQ + h)[:, NP_TOK:NT], bc2[h % 2][:, NT:NT + 64], ALU.mult).then_inc(qw_ready, 1)
                dve.wait_ge(qw_ready, h + 1)
                V.tensor_tensor(qn.rearrange("p (b l) -> p b l", b=NB), qw.rearrange("p (b l) -> p b l", b=NB),
                                n0h(h).to_broadcast([P, NB, LB]), ALU.mult).then_inc(qn_ready, 1)

            def weigh_scores(h):
                dve.wait_ge(ex_ready, 3 * (h + 1))
                dve.wait_ge(S_done, h + 1)
                V.scalar_tensor_tensor(et2[h % 2], bank[3][:, 0:448], KSCALE, et2[h % 2], ALU.mult, ALU.mult).then_inc(P_ready, 1)

            dve.wait_ge(zeroed, 6)
            front(0)
            dve.wait_ge(y_done, NJ)
            V.scalar_tensor_tensor(Z(ZU + 3), Z(ZU + 3), v(V_D + 3, 1), bank[7][:, 0:NT], ALU.mult, ALU.add).then_inc(yd_ready, 1)
            weigh_scores(0)
            for n in range(4):
                dve.wait_ge(sgl_ready, 4 if n == 0 else n + 1)
                V.tensor_tensor(Z(ZU + n), Z(ZU + n), sgl[:, n * NT:n * NT + NT], ALU.mult).then_inc(ys_ready, 1)

            def gate_ssm(n):
                if n == 0:
                    dve.wait_ge(g_sig, 2)
                dve.wait_ge(up_done, n + 1)
                V.tensor_tensor(Z(ZGS + n), Z(ZGS + n), bank[1][:, 0:NT], ALU.mult).then_inc(up_dve, 1)

            for h in range(H):
                bc, bN = bc2[h % 2], bank[5]
                if h < H - 1:
                    front(h + 1)
                dve.wait_ge(abs_ready, h + 1)
                alink(V.tensor_tensor(den_a, den_a, bc[:, 0:NT], ALU.max))
                alink(V.reciprocal(den_a, den_a))
                if h < H - 1:
                    weigh_scores(h + 1)
                dve.wait_ge(N_done, h + 1)
                alink(V.tensor_tensor(den_a, bN[:, 0:NT], den_a, ALU.mult))
                if h == 0:
                    dve.wait_ge(g_sig, 1)
                V.tensor_tensor(Z(ZQ + h), den_a, Z(ZO + h), ALU.mult).then_inc(ym_ready, 1)
                dec = bc[:, NT:NT + 64].rearrange("p (b l) -> p b l", b=NB)[:, :, LB - 1:LB]
                dve.wait_ge(qn_ready, h + 1)
                alink(V.tensor_tensor(n0h(h), n0h(h), dec, ALU.mult))
                alink(V.tensor_tensor(n0h(h), n0h(h), bN[:, 448:456].unsqueeze(2), ALU.add))
                alink(V.tensor_copy(n0T[:, 32 + h:33 + h], bN[:, 456:457]))
                if h == 0:
                    dve.wait_ge(ys_ready, 4)
                V.tensor_copy(cp_rows[:, h * P:h * P + P], bN[:, NT:NT + P]).then_inc(cp_ready, 1)
                alink(V.tensor_tensor(C0[:, h], C0[:, h], dec.to_broadcast([P, NB, P]), ALU.mult))
                dve.wait_ge(C_done, 2 * h + 1)
                V.tensor_tensor(C0[:, h, 0:4], C0[:, h, 0:4], bank[7][:, :].rearrange("p (b e) -> p b e", b=4), ALU.add).then_inc(C_half, 1)
                gate_ssm(2 * h)
                dve.wait_ge(C_done, 2 * h + 2)
                V.tensor_tensor(C0[:, h, 4:8], C0[:, h, 4:8], bank[6][:, :].rearrange("p (b e) -> p b e", b=4), ALU.add).then_inc(C_ready, 1)
                gate_ssm(2 * h + 1)

            dve.wait_ge(g_sig, 3)
            dve.wait_ge(up_dve, KD)
            for n in range(KD):
                dve.wait_ge(up_done, KD + n + 1)
                V.tensor_tensor(Z(ZGM + n), Z(ZGM + n), bank[n % 4][:, 0:NT], ALU.mult).then_inc(up_dve, 1)
                dve.wait_ge(up_dve, KD + n + 1)
                V.tensor_tensor(Z(ZGS + n), Z(ZGS + n), Z(ZGM + n), ALU.add).then_inc(merged, 1)
            dve.wait_ge(res_full, 32)
            dve.wait_ge(zeroed, 12)
            for n in range(6):
                tt, hf = n // 2, n % 2
                w = TW[tt]
                dve.wait_ge(out_done, n + 1)
                A = acc[0:w, tt, 512 * hf:512 * hf + 512]
                V.tensor_tensor(A, A, bank[4 + n % 4][0:w, :], ALU.add).then_inc(h_ready, 1)
            rms(1, acc, x3)
            hnT_evac(1, V_GFFN, (0, 1, 2, 3))

            dve.wait_ge(rl_done, TT)
            for tt in range(TT):
                w = TW[tt]
                link(V.tensor_tensor(lg[0:w, tt, :], bank[4][0:w, 32 * tt:32 * tt + 32], brb[0:w, :], ALU.add))
            for tt in range(TT):
                link(V.max(mtop[:, tt, :], lg[:, tt, :]))

            def bce(x_):
                return x_.to_broadcast([P, TT, NE])

            link(V.tensor_tensor(gtm, lg, bce(mtop[:, :, 3:4]), ALU.is_gt))
            link(V.tensor_tensor(eqm, lg, bce(mtop[:, :, 3:4]), ALU.is_equal))
            link(V.reduce_sum(mcol[:, 0:3].unsqueeze(2), gtm, AX.X))
            link(V.tensor_scalar(mcol[:, 0:3], mcol[:, 0:3], -1.0, 4.5, ALU.mult, ALU.add))
            for tt in range(TT):
                link(V.tensor_tensor_scan(msk[:, tt, :], ones[:, 0:NE], eqm[:, tt, :], 0.0, ALU.mult, ALU.add))
            link(V.tensor_tensor(msk, msk, bce(mcol[:, 0:3].unsqueeze(2)), ALU.is_lt))
            link(V.tensor_tensor(msk, msk, eqm, ALU.mult))
            link(V.tensor_tensor(msk, msk, gtm, ALU.add))
            link(V.memset(msk[64:128, 2, :], 0.0))
            V.tensor_tensor(exw, lg, bce(mtop[:, :, 0:1]), ALU.subtract).then_inc(rl_ready, 1)
            dve.sem_inc(mask_ready, 1)
            dve.wait_ge(rl_ready, 2)
            link(V.tensor_tensor(exw, exw, msk, ALU.mult))
            link(V.reduce_sum(mcol[:, 4:7].unsqueeze(2), exw, AX.X))
            link(V.tensor_scalar(mcol[:, 4:7], mcol[:, 4:7], 1e-30, None, ALU.max))
            link(V.reciprocal(mcol[:, 4:7], mcol[:, 4:7]))
            link(V.memset(wt[:, :, NE:NE + 1], 0.0))
            link(V.tensor_tensor(wt[:, :, 0:NE], exw, bce(mcol[:, 4:7].unsqueeze(2)), ALU.mult))
            dve.sem_inc(mask_ready, 1)
            dve.wait_ge(rank_done, 1)
            link(V.memset(rk[:, :, NE:NE + 1], -1.0))
            link(V.tensor_scalar(rk[:, :, 0:NE], bank[5][:, 0:96].rearrange("p (t e) -> p t e", t=TT), 1.0, None, ALU.add))
            link(V.tensor_tensor(rk[:, :, 0:NE], rk[:, :, 0:NE], msk, ALU.mult))
            link(V.tensor_scalar(rk[:, :, 0:NE], rk[:, :, 0:NE], -1.0, None, ALU.add))
            cntb = bank[5][:, 96:128]
            link(V.tensor_scalar(nov, cntb, float(SLOTS), None, ALU.is_gt))
            for r in range(2, 5):
                link(V.tensor_scalar(ind, cntb, float(SLOTS * r), None, ALU.is_gt))
                link(V.tensor_tensor(nov, nov, ind, ALU.add))
            link(V.tensor_tensor_scan(cinc, ones[:, 0:NE], nov, 0.0, ALU.mult, ALU.add))
            link(V.tensor_scalar(ind, cinc, c("pidx"), None, ALU.is_le))
            link(V.reduce_sum(opass[:, 0:1], ind, AX.X))
            link(V.tensor_scalar(opass[:, 0:1], opass[:, 0:1], float(NE - 1), None, ALU.min))
            link(V.tensor_tensor(ind, ind, nov, ALU.mult))
            link(V.reduce_sum(opass[:, 1:2], ind, AX.X))
            link(V.tensor_tensor(opass[:, 1:2], c("pidx"), opass[:, 1:2], ALU.subtract))
            link(V.tensor_scalar(opass[:, 1:2], opass[:, 1:2], 1.0, float(SLOTS), ALU.add, ALU.mult))
            link(V.tensor_scalar(dtab[:, 0:EXTRA], ident[:, 0:EXTRA], opass[:, 0:1], None, ALU.mult))
            V.tensor_scalar(dtab[:, EXTRA:2 * EXTRA], ident[:, 0:EXTRA], opass[:, 1:2], None, ALU.mult).then_inc(tab_made, 1)
            dve.wait_ge(ob_done, 1)
            link(V.tensor_copy(cnt_i[0:1, 0:1], cinc[0:1, NE - 1:NE]))
            link(V.tensor_copy(cnt_i[0:1, 1:1 + EXTRA], bank[6][0:1, 0:EXTRA]))
            link(V.tensor_copy(obase, bank[6][:, EXTRA:2 * EXTRA]))
            dve.sem_inc(cnt_ready, 1)
            for n in range(6):
                tt, hf = n // 2, n % 2
                w = TW[tt]
                dve.wait_ge(bd_done, n + 1)
                A = acc[0:w, tt, 512 * hf:512 * hf + 512]
                V.tensor_tensor(A, A, bank[n % 2][0:w, :], ALU.add).then_inc(acc_ready, 1)
            link(V.memset(p_lo, 0.0))
            link(V.memset(yb, 0.0))
            dve.sem_inc(y_ready, 1)
            dve.sem_inc(acc_add, 2)

            gffn = v(V_GFFN, 8)

            def select(e, base=None):
                V.tensor_tensor(sel, (c("slot") if base is None else base).unsqueeze(1).to_broadcast([P, TT, SLOTS]),
                                rk[:, :, bass.ds(e, 1)].to_broadcast([P, TT, SLOTS]), ALU.is_equal).then_inc(sel_ready, 1)

            def hot(e):
                V.tensor_copy(onehot, ident[:, bass.ds(e, 1)].to_broadcast([P, SLOTS])).then_inc(oh_ready, 1)

            def weigh(e, n):
                dve.wait_ge(sel_ready, n + 1)
                V.tensor_tensor(selw, sel.unsqueeze(2).to_broadcast([P, TT, 2, SLOTS]),
                                wt[:, :, bass.ds(e, 1)].unsqueeze(3).to_broadcast([P, TT, 2, SLOTS]), ALU.mult).then_inc(selw_ready, 1)

            def x_evac(n):
                dve.wait_ge(xsT_done, n + 1)
                V.tensor_tensor(xsT.rearrange("p (j a s) -> p a j s", j=4, a=2),
                                bank[2][:, :].rearrange("p (j a s) -> p a j s", j=4, a=2),
                                gffn.rearrange("p (a j) -> p a j", a=2).unsqueeze(3).to_broadcast([P, 2, 4, SLOTS]),
                                ALU.mult).then_inc(xsT_ready, 1)

            def swiglu(n):
                dve.wait_ge(g_done, n + 1)
                V.tensor_scalar(mg, bank[0][:, :], LIMIT, None, ALU.min).then_inc(g_ready, 1)
                dve.wait_ge(u_done, n + 1)
                V.tensor_scalar(mu, bank[1][:, :], LIMIT, -LIMIT, ALU.min, ALU.max).then_inc(u_ready, 1)
                dve.wait_ge(u_ready, n + 1)
                V.scalar_tensor_tensor(mu, mu, 1.0, mg, ALU.add, ALU.mult).then_inc(gu_ready, 1)
                dve.wait_ge(gu_ready, n + 1)
                dve.wait_ge(s_ready, n + 1)
                V.tensor_tensor(hb, mu, ms, ALU.mult).then_inc(hb_ready, 1)

            def accumulate(n):
                for m in range(6):
                    tt, hf = m // 2, m % 2
                    w = TW[tt]
                    dve.wait_ge(sc_done, n * 6 + m + 1)
                    A = acc[0:w, tt, 512 * hf:512 * hf + 512]
                    V.tensor_tensor(A, A, bank[6 + m % 2][0:w, :], ALU.add).then_inc(acc_add, 1)

            def p_evac(n):
                dve.wait_ge(pw_done, n + 1)
                V.tensor_copy(p_lo[0:64, :], bank[4][0:64, 0:384]).then_inc(pw_ready, 1)
                V.tensor_copy(p_hi[64:128, :], bank[4][64:128, 0:384]).then_inc(pw_ready, 1)

            dve.wait_ge(acc_ready, 6)
            select(0)
            hot(0)
            x_evac(0)
            with dve.Fori(0, NE) as p:
                dve.wait_ge(gath_done, p + 1)
                weigh(p, p)
                dve.wait_ge(selw_ready, p + 1)
                select(p + 1)
                swiglu(p)
                hot(p + 1)
                accumulate(p)
                p_evac(p)
                x_evac(p + 1)
            accumulate(NE)
            extra = dve.value_load(cnt_i[0:1, 0:1], min_val=0, max_val=EXTRA)
            with dve.If(extra > 0):
                with dve.Fori(0, extra) as q:
                    e = dve.value_load(cnt_i[0:1, bass.ds(q + 1, 1)], min_val=0, max_val=NE - 1)
                    V.tensor_scalar(islot, c("slot"), obase[:, bass.ds(q, 1)], None, ALU.add).then_inc(tab_made, 1)
                    dve.wait_ge(tab_made, q + 2)
                    select(e, islot)
                    hot(e)
                    weigh(e, q + (NE + 1))
                    x_evac(q + (NE + 1))
                    swiglu(q + NE)
                    p_evac(q + NE)
                    accumulate(q + (NE + 1))

            dve.wait_ge(acc_add, extra * 6 + (6 * (NE + 1) + 2))
            rms(2, acc, x3)
            hnT_evac(2, V_GPLE, (0, 1, 2, 3))
            dve.wait_ge(pj_ready, 6)
            for n in range(6):
                tt, hf = n // 2, n % 2
                cs = slice(512 * hf, 512 * hf + 512)
                dve.wait_ge(gt_sig, n + 1)
                link(V.tensor_tensor(x3[:, tt, cs], x3[:, tt, cs], pproj[:, tt, cs], ALU.mult))
                V.tensor_tensor(acc[:, tt, cs], acc[:, tt, cs], x3[:, tt, cs], ALU.add).then_inc(fin_h, 1)
            dve.wait_ge(ssq_ready, 12)
            V.tensor_scalar(rstd[:, 0:3], rstd[:, 0:3], 1.0 / D, EPS, ALU.mult, ALU.add).then_inc(sd_ready, 1)
            dve.wait_ge(sd_ready, 8)
            link(V.reciprocal(rstd[:, 0:3], rstd[:, 0:3]))
            dve.wait_ge(gfin_full, 16)
            for tt in range(TT):
                V.scalar_tensor_tensor(acc[:, tt, :], acc[:, tt, :], rstd[:, tt:tt + 1], gfin, ALU.mult, ALU.mult).then_inc(out_ready, 1)

        @block.tensor
        def _(pe):
            mm_, tr = nc.tensor.matmul, nc.tensor.transpose

            def transposes(r, src):
                pe.wait_ge(xn_ready, TT * (r + 1))
                for k in range(KD):
                    if k >= 4:
                        pe.wait_ge(hnT_ready, KD * r + k - 3)
                    for tt in range(TT):
                        last = tr(bank[k % 4][:, tt * P:tt * P + P], src[:, tt, k * P:k * P + P], ident)
                    last.then_inc(xT_done, 1)

            pe.wait_ge(cst_full, 16)
            pe.wait_ge(ldt_ready, 1)
            tr(bank[4][:, 0:80], vec_rows[0:80, :], ident[0:80, 0:80]).then_inc(vecT_done, 1)
            transposes(0, x3)

            def z_tile(n):
                (s, use), half = z_slot(n // 2), n % 2
                if half == 0:
                    pe.wait_ge(slot_full[s], 16 * (use + 1))
                if n > ZGM:
                    pe.wait_ge(z_ready, n)
                elif n >= 4:
                    pe.wait_ge(z_ready, n - 3)
                wz = w3(s, KD, 256)
                for k in range(KD):
                    last = mm_(bank[z_bank(n)][:, 0:NT], wz[:, k, half * P:half * P + P], hn3[:, k, :], start=k == 0, stop=k == KD - 1)
                last.then_inc(z_done, 1)
                if half:
                    pe.wait_ge(z_done, n + 1)
                    pe.sem_inc(slot_free[s], 1)

            pe.wait_ge(hnT_ready, KD)
            for n in range(8):
                z_tile(n)
            for n in range(4):
                pe.wait_ge(bx_ready, n + 1)
                if n == 0:
                    pe.wait_ge(vec_ready, 1)
                src = (Bx, Cx)[n // 2][:, 512 * (n % 2):512 * (n % 2) + 512]
                for j in range(NJ):
                    last = tr(bank[4 + n][:, j * P:j * P + P], src[:, j * P:j * P + P], ident)
                last.then_inc(bxT_done, 1)
            pe.wait_ge(bct_ready, 4)
            pe.wait_ge(st_full, 48)
            tr(bank[4][:, 0:P], h0_rows_r, ident)
            tr(bank[4][:, P:2 * P], h0_rows_i, ident)
            tr(bank[4][:, 256:288], n_rows[0:32, :], ident[0:32, 0:32]).then_inc(stT_done, 1)
            for n in range(8, 10):
                z_tile(n)
            pe.wait_ge(stT_ready, 2)

            def bu(j):
                for q in range(8):
                    m = 8 * j + q
                    if q % 2 == 0:
                        pe.wait_ge(um_ready, 4 * j + q // 2 + 1)
                    if m >= 3:
                        pe.wait_ge(bu_ready, 8 * j + q - 2 if q >= 3 else 8 * j)
                    mm_(bank[4 + q % 3][:, 0:NT], BT[:, q % 2, j, :], um[:, (q // 2) * NT:(q // 2 + 1) * NT],
                        start=True, stop=True).then_inc(bu_done, 1)

            def y(j):
                pe.wait_ge(rotout_done, 2 * j + 2)
                if j:
                    pe.wait_ge(yd_ready, j)
                for i in range(NI):
                    out = bank[7][32 * i:32 * i + 32, 0:NT]
                    mm_(out, CT[:, 0, j, 32 * i:32 * i + 32], XR[:, i * NT:(i + 1) * NT], start=True, stop=False)
                    last = mm_(out, CT[:, 1, j, 32 * i:32 * i + 32], XI[:, i * NT:(i + 1) * NT], start=False, stop=True)
                last.then_inc(y_done, 1)

            bu(0)
            pe.wait_ge(wif_full, 32)
            wif = att[:, 0:KD * 36].rearrange("p (k n) -> p k n", k=KD)
            for k in range(KD):
                last = mm_(bank[7][0:36, 0:NT], wif[:, k, :], hn3[:, k, :], start=k == 0, stop=k == KD - 1)
            last.then_inc(gate_done, 1)
            for j in range(NJ):
                if j == 1:
                    pe.wait_ge(gate_rows, 3)
                if j:
                    y(j - 1)
                for n in ZSTAGE[j][:2]:
                    z_tile(n)
                if j == 2:
                    pe.wait_ge(R_ready, 3)
                    pe.wait_ge(bu_ready, 24)
                    for n, src in enumerate((arow, wrow)):
                        for tt in range(TT):
                            last = tr(bank[4][:, 12 * n + H * tt:12 * n + H * tt + H], src[:, tt * P:tt * P + P], ident[0:H, 0:H])
                    last.then_inc(asT_done, 1)
                if j == NJ - 1:
                    pe.wait_ge(bu_ready, 8 * NJ)
                    for g in range(2 * H):
                        if g >= 3:
                            pe.wait_ge(kv_ready, TT * (g - 2))
                        for tt in range(TT):
                            w = TW[tt]
                            src = Z((ZK if g < H else ZV) + g % H)
                            last = tr(bank[4 + g % 3][0:w, tt * P:tt * P + P], src[:, tt * P:tt * P + w], ident)
                        last.then_inc(kvT_done, 1)
                for n in ZSTAGE[j][2:]:
                    z_tile(n)
                if j < NJ - 1:
                    if j == 2:
                        pe.wait_ge(asT_ready, 2)
                    bu(j + 1)
            selh = c("sel")
            blocks = ((0, 256, 0, 256), (256, 384, 128, 256), (384, 448, 256, 320))

            def front(h):
                sh = selh[:, h * P:h * P + P]
                if h == 0:
                    pe.wait_ge(z_ready, ZGM)
                    pe.wait_ge(kv_ready, TT * 2 * H)
                else:
                    pe.wait_ge(em_ready, h)
                    pe.wait_ge(bc_ready, h)
                    pe.wait_ge(P_ready, h)
                for c0, c1, a0, a1 in blocks:
                    last = mm_(bank[2][:, c0:c1], sh, rows[:, a0:a1], start=True, stop=True)
                last.then_inc(E_done, 1)
                mm_(bank[4][:, 0:384], sh, rows[:, NT:2 * NT + 64], start=True, stop=True).then_inc(bc_done, 1)
                qT_, kT_ = Z(ZQ + h), Z(ZK + h)
                mm_(bank[3][:, 0:256], kT_[:, 0:128], qT_[:, 0:256], start=True, stop=True)
                mm_(bank[3][:, 256:384], kT_[:, 128:256], qT_[:, 128:256], start=True, stop=True)
                mm_(bank[3][:, 384:448], zT[:, (ZK + h) * NT + 256:(ZK + h) * NT + 384], qT_[:, 256:320], start=True, stop=True).then_inc(S_done, 1)

            def up(n, s, src, bank_):
                for k in range(4):
                    last = mm_(bank_[:, 0:NT], w3(s[k // 2], 2, D)[:, k % 2, n * P:n * P + P], Z(src + k), start=k == 0, stop=k == 3)
                last.then_inc(up_done, 1)

            front(0)
            y(NJ - 1)
            z_tile(ZGM)
            pe.wait_ge(fin_ready, 4 * NJ)
            pe.wait_ge(yd_ready, NJ)
            for n in range(2):
                tr(bank[7][:, n * P:n * P + P], fin_s[:, n * P:n * P + P], ident).then_inc(finT_done, 1)
            tr(bank[7][0:32, 2 * P:3 * P], fin_p, ident).then_inc(finT_done, 1)
            pe.wait_ge(gelu_ready, 4)
            pe.wait_ge(slot_full[3], 16 * 3)
            wg = w3(3, 4, 512)
            for n in range(4):
                if n == 3:
                    pe.wait_ge(z_ready, ZGM + 1)
                for k in range(4):
                    last = mm_(bank[GLU_BANK[n]][:, 0:NT], wg[:, k, n * P:n * P + P], Z(ZU + k), start=k == 0, stop=k == 3)
                last.then_inc(glu_done, 1)
            pe.wait_ge(glu_done, 4)
            pe.sem_inc(slot_free[3], 1)
            pe.wait_ge(sgl_ready, 4)

            for h in range(H):
                et, qw, qn = et2[h % 2], qw2[h % 2], qn2[h % 2]
                pe.wait_ge(P_ready, h + 1)
                pe.wait_ge(qn_ready, h + 1)
                if h:
                    pe.wait_ge(C_ready, h)
                bD = bank[6]
                mm_(bD[:, 0:256], ones, et[:, 0:256], start=True, stop=False)
                mm_(bD[:, 128:256], ones, et[:, 256:384], start=False, stop=True)
                mm_(bD[:, 256:320], ones, et[:, 384:448], start=True, stop=False)
                mm_(bD[:, 256:320], ones, qn, start=False, stop=True).then_inc(den_done, 1)
                if h < H - 1:
                    front(h + 1)
                vh = [v_tok[:, tt, h * P:h * P + P] for tt in range(TT)]
                k2 = [kw_all[:, h * 384 + tt * P:h * 384 + tt * P + P] for tt in range(TT)]
                bN = bank[5]
                if h == 0:
                    pe.wait_ge(c0_full, 16 * H)
                else:
                    pe.wait_ge(cp_ready, h)
                    pe.wait_ge(C_half, h)
                mm_(bN[:, NT:NT + P], k2[0], vh[0], start=True, stop=False)
                mm_(bN[:, NT:NT + P], k2[1], vh[1], start=False, stop=True)
                mm_(bN[:, 448:456], k2[2], c("seqm"), start=True, stop=True)
                mm_(bN[:, 456:457], k2[0], ones[:, 0:1], start=True, stop=False)
                mm_(bN[:, 456:457], k2[1], ones[:, 0:1], start=False, stop=True)
                mm_(bN[:, 0:256], vh[0], et[:, 0:256], start=True, stop=False)
                mm_(bN[:, 128:256], vh[1], et[:, 256:384], start=False, stop=True)
                mm_(bN[:, 256:320], vh[2], et[:, 384:448], start=True, stop=False)
                for b in range(NB):
                    last = mm_(bN[:, 256 + LB * b:264 + LB * b], C0[:, h, b], qw[:, LB * b:LB * b + LB], start=False, stop=b == NB - 1)
                last.then_inc(N_done, 1)
                if ZHEAD[h]:
                    z_tile(ZHEAD[h][0])
                pe.wait_ge(vx_ready, h + 1)
                if h == 0:
                    pe.wait_ge(finT_ready, 3)
                mm_(bank[7][:, :], k2[2], vx2[h % 2][:, 0:4].rearrange("p b e -> p (b e)"), start=True, stop=True).then_inc(C_done, 1)
                if h == 0:
                    pe.wait_ge(ys_ready, 4)
                    for s in (4, 5):
                        pe.wait_ge(slot_full[s], 16 * 3)
                else:
                    pe.wait_ge(up_dve, 2 * h)
                up(2 * h, (4, 5), ZU, bank[1])
                pe.wait_ge(abs_ready, h + 1)
                mm_(bank[6][:, :], k2[2], vx2[h % 2][:, 4:8].rearrange("p b e -> p (b e)"), start=True, stop=True).then_inc(C_done, 1)
                for n in ZHEAD[h][1:]:
                    z_tile(n)
                pe.wait_ge(up_dve, 2 * h + 1)
                up(2 * h + 1, (4, 5), ZU, bank[1])
            pe.wait_ge(up_done, KD)
            for s in (4, 5):
                pe.sem_inc(slot_free[s], 1)

            pe.wait_ge(ym_ready, H)
            pe.wait_ge(P_ready, H)
            pe.wait_ge(z_ready, ZT)
            pe.wait_ge(up_dve, KD)
            pe.wait_ge(slot_full[3], 16 * 4)
            pe.wait_ge(slot_full[0], 16 * 5)
            for n in range(KD):
                if n >= 4:
                    pe.wait_ge(up_dve, KD + n - 3)
                up(n, (3, 0), ZQ, bank[n % 4])
                if n == 3:
                    pe.wait_ge(C_ready, H)
                    tr(bank[4][0:36, 0:P], n0T, ident).then_inc(nT_done, 1)
            pe.wait_ge(up_done, 2 * KD)
            for s in (3, 0):
                pe.sem_inc(slot_free[s], 1)
            pe.wait_ge(merged, KD)
            pe.wait_ge(nT_ready, 1)
            pe.wait_ge(cp_ready, H)
            for n in range(6):
                tt, hf = n // 2, n % 2
                w = TW[tt]
                if n >= 4:
                    pe.wait_ge(h_ready, n - 3)
                for k in range(KD):
                    if n == 0 and k % 2 == 0:
                        pe.wait_ge(slot_full[WOUT[k // 2]], 16)
                    last = mm_(bank[4 + n % 4][0:w, :], Z(ZGS + k)[:, tt * P:tt * P + w],
                               w3(WOUT[k // 2], 2, D)[:, k % 2, 512 * hf:512 * hf + 512], start=k == 0, stop=k == KD - 1)
                last.then_inc(out_done, 1)
            pe.wait_ge(out_done, 6)
            for s in WOUT:
                pe.sem_inc(slot_free[s], 1)

            transposes(1, x3)
            pe.wait_ge(hnT_ready, 2 * KD)
            pe.wait_ge(wr_full, 16)
            pe.wait_ge(h_ready, 6)
            wr3 = wr_sb.rearrange("p (k e) -> p k e", k=KD)
            for tt in range(TT):
                w = TW[tt]
                for k in range(KD):
                    last = mm_(bank[4][0:w, 32 * tt:32 * tt + 32], hn3[:, k, tt * P:tt * P + w], wr3[:, k, :], start=k == 0, stop=k == KD - 1)
                last.then_inc(rl_done, 1)
            pe.wait_ge(mask_ready, 1)
            tri = c("triu")
            for tt in range(TT):
                for s in range(tt + 1):
                    mm_(bank[5][:, 32 * tt:32 * tt + 32], tri if s == tt else ones, msk[:, s, :], start=s == 0, stop=s == tt)
            for s in range(TT):
                last = mm_(bank[5][:, 96:128], ones, msk[:, s, :], start=s == 0, stop=s == TT - 1)
            last.then_inc(rank_done, 1)
            pe.wait_ge(mask_ready, 2)
            for tt in range(TT):
                last = tr(bank[4][0:NE, tt * P:tt * P + P], wt[:, tt, 0:NE], ident)
            last.then_inc(wtT_done, 1)
            pe.wait_ge(tab_made, 1)
            mm_(bank[6][:, 0:2 * EXTRA], ones, dtab, start=True, stop=True).then_inc(ob_done, 1)
            pe.wait_ge(wtT_ready, 1)
            pe.wait_ge(bt_full, 48)
            for n in range(6):
                tt, hf = n // 2, n % 2
                w = TW[tt]
                if n >= 2:
                    pe.wait_ge(acc_ready, n - 1)
                mm_(bank[n % 2][0:w, :], p_lo[:, tt * P:tt * P + w], btab[2][:, 512 * hf:512 * hf + 512],
                    start=True, stop=True).then_inc(bd_done, 1)
            pe.wait_ge(y_ready, 1)

            def gather(n):
                pe.wait_ge(sel_ready, n + 1)
                for tt in range(TT):
                    for hf in range(2):
                        last = mm_(bank[2][64 * hf:64 * hf + 64, :], sel[:, tt, :], x3[:, tt, 512 * hf:512 * hf + 512],
                                   start=tt == 0, stop=tt == TT - 1)
                last.then_inc(gath_done, 1)

            def gather_T(n):
                pe.wait_ge(xs_ready, n + 1)
                for j in range(4):
                    last = tr(bank[2][:, j * P:j * P + P], xs[:, j * P:j * P + P], ident)
                last.then_inc(xsT_done, 1)

            def project(n, s0, srcT, dst, done, bias=None):
                for hf in range(2 if bias is not None else 0):
                    mm_(dst[64 * hf:64 * hf + 64, :], onehot, btab[bias][:, 512 * hf:512 * hf + 512], start=True, stop=False)
                for k in range(KD):
                    s = s0 + k // 2
                    if k % 2 == 0:
                        pe.wait_ge(slot_full[s], n * 16 + 16 * (USED0[s] + 1))
                    for hf in range(2):
                        last = mm_(dst[64 * hf:64 * hf + 64, :], srcT[:, (k % 4) * P + 64 * (k // 4):(k % 4) * P + 64 * (k // 4) + 64],
                                   w3(s, 2, D)[:, k % 2, 512 * hf:512 * hf + 512], start=bias is None and k == 0, stop=k == KD - 1)
                    if k % 2:
                        last.then_inc(slot_free[s] if k < KD - 1 else done, 1)
                pe.wait_ge(done, n + 1)
                pe.sem_inc(slot_free[s0 + 3], 1)

            def scatter(n):
                pe.wait_ge(y_ready, n + 1)
                for m in range(6):
                    tt, hf = m // 2, m % 2
                    w = TW[tt]
                    pe.wait_ge(acc_add, n * 6 + (m + 1))
                    mm_(bank[6 + m % 2][0:w, :], (p_lo, p_hi)[hf][:, tt * P:tt * P + w], yb, start=True, stop=True).then_inc(sc_done, 1)

            def weights_T(n):
                pe.wait_ge(selw_ready, n + 1)
                for tt in range(TT):
                    last = tr(bank[4][:, tt * P:tt * P + P], selw[:, tt].rearrange("p a s -> p (a s)"), ident)
                last.then_inc(pw_done, 1)

            def gate_up(n, picked):
                pe.wait_ge(xsT_ready, picked)
                pe.wait_ge(oh_ready, picked)
                project(n, 0, xsT, bank[0], g_done, bias=0)
                project(n, 4, xsT, bank[1], u_done, bias=1)

            def hidden_T(n):
                pe.wait_ge(hb_ready, n + 1)
                for j in range(4):
                    last = tr(bank[3][:, j * P:j * P + P], hb[:, j * P:j * P + P], ident)
                last.then_inc(hTt_done, 1)

            def down(n):
                pe.wait_ge(hT_ready, n + 1)
                project(n, 8, hT, bank[5], dn_done)

            pe.wait_ge(cnt_ready, 1)
            gather(0)
            gather_T(0)
            with pe.Fori(0, NE) as p:
                gate_up(p, p + 1)
                gather(p + 1)
                scatter(p)
                weights_T(p)
                hidden_T(p)
                gather_T(p + 1)
                down(p)
            pe.wait_ge(pw_ready, 2 * NE)
            scatter(NE)
            extra = pe.value_load(cnt_i[0:1, 0:1], min_val=0, max_val=EXTRA)
            with pe.If(extra > 0):
                with pe.Fori(0, extra) as q:
                    gather(q + (NE + 1))
                    gather_T(q + (NE + 1))
                    gate_up(q + NE, q + (NE + 2))
                    weights_T(q + NE)
                    hidden_T(q + NE)
                    down(q + NE)
                    pe.wait_ge(pw_ready, q * 2 + 2 * (NE + 1))
                    scatter(q + (NE + 1))

            pe.wait_ge(ple_full, 32)
            pe.wait_ge(acc_add, extra * 6 + (6 * (NE + 1) + 2))
            for k in range(2):
                for tt in range(TT):
                    w = TW[tt]
                    last = tr(bank[4 + k][:, tt * P:tt * P + w], p_tok[0:w, tt, k * P:k * P + P], ident[0:w, 0:w])
                last.then_inc(pTt_done, 1)
            pe.wait_ge(pT_ready, 2)
            pe.wait_ge(slot_full[4], extra * 16 + 16 * (USED0[4] + NE + 1))
            for n in range(6):
                tt, hf = n // 2, n % 2
                if n >= 4:
                    pe.wait_ge(pj_ready, n - 3)
                for k in range(2):
                    last = mm_(bank[4 + n % 4][:, :], pT[:, k, tt * P:tt * P + P], w3(4, 2, D)[:, k, 512 * hf:512 * hf + 512], start=k == 0, stop=k == 1)
                last.then_inc(pj_done, 1)
            transposes(2, x3)
            pe.wait_ge(hnT_ready, 3 * KD)
            for n in range(6):
                tt, hf = n // 2, n % 2
                w = TW[tt]
                if n >= 2:
                    pe.wait_ge(gt_sig, n - 1)
                for k in range(KD):
                    if n == 0 and k % 2 == 0:
                        pe.wait_ge(slot_full[k // 2], extra * 16 + 16 * (USED0[k // 2] + NE + 1))
                    last = mm_(bank[n % 2][0:w, :], hn3[:, k, tt * P:tt * P + w], w3(k // 2, 2, D)[:, k % 2, 512 * hf:512 * hf + 512],
                               start=k == 0, stop=k == KD - 1)
                last.then_inc(gt_done, 1)


def constants():
    import numpy as np
    c = np.zeros((P, CONST_W), np.float32)

    def put(name, a):
        c[:, CONST[name][0]:CONST[name][1]] = a

    p = np.arange(P)
    n = np.arange(NT)
    put("ident", np.eye(P))
    put("ones", 1.0)
    put("triu", p[:, None] < p[None, :])
    put("slot", np.arange(SLOTS)[None])
    put("tloc", np.where(n < NP_TOK, n, (n - NP_TOK) % LB)[None])
    m = np.full((P, 448), -1.0e30, np.float32)
    m[:, 0:256][p[:, None] <= np.arange(256)[None]] = 0.0
    m[:, 256:384][p[:, None] <= p[None]] = 0.0
    q = np.arange(64)
    ok = (q[:, None] // LB == q[None] // LB) & (q[:, None] <= q[None])
    m[0:64, 384:448][ok] = 0.0
    put("amask", m)
    put("seqm", (p[:, None] // LB == np.arange(NB)[None]))
    put("half", (p[:, None] // 64 == np.arange(2)[None]))
    put("par", (p[:, None] // GW % 2 == np.arange(2)[None]))
    put("npar", -1.0 * (p[:, None] // GW % 2 == np.arange(2)[None]))
    put("imask", (p[:, None] // 32 == np.arange(NI)[None]))
    put("start", np.where((n == 0) | ((n >= NP_TOK) & ((n - NP_TOK) % LB == 0)), 0.0, 1.0)[None])
    put("sel", (p[:, None] == np.arange(H * P)[None] // P))
    put("pidx", p[:, None])
    put("halfpi", np.float32(1.5707963))
    put("eps", EPS)
    return c


_INS = ["x_prompt", "x_sample", "p_prompt", "p_sample", "state_ssm_re", "state_ssm_im", "state_ml_c", "state_ml_n",
        "state_ml_m", "g_mix", "w_in", "ssm_a_re", "ssm_a_im", "ssm_log_dt", "ssm_b_re", "ssm_b_im", "ssm_c_re",
        "ssm_c_im", "ssm_d", "ssm_w_glu", "ssm_b_glu", "ml_b_ig", "ml_b_fg", "w_ssm_up", "w_ml_up", "w_out", "g_ffn",
        "w_router", "b_router", "w_gate", "b_gate", "w_up", "b_up", "w_down", "b_down", "g_ple", "w_ple_gate",
        "w_ple_proj", "g_final"]
_OUTS = [("yp", (1, 256, 1024)), ("ys", (8, 8, 1024)), ("rp", (1, 1, 32, 64)), ("ip", (1, 1, 32, 64)),
         ("cp", (1, 1, 4, 128, 128)), ("np", (1, 1, 4, 128)), ("mp", (1, 1, 4)), ("rs", (1, 8, 32, 64)),
         ("is", (1, 8, 32, 64)), ("cs", (1, 8, 4, 128, 128)), ("ns", (1, 8, 4, 128)), ("ms", (1, 8, 4))]


def kernel(**inputs):
    import numpy as np
    import concourse.bacc as bacc
    from concourse.bass_utils import run_bass_kernel_spmd

    nc = bacc.Bacc("TRN2", target_bir_lowering=False, num_devices=1)
    arrays, t, o = {}, {}, {}
    for name in _INS:
        arrays[name] = np.ascontiguousarray(inputs[name])
    arrays["cst"] = constants()
    for name, a in arrays.items():
        t[name] = nc.dram_tensor("in_" + name, a.shape, mybir.dt.from_np(a.dtype), kind="ExternalInput").ap()
    for name, shape in _OUTS:
        o[name] = nc.dram_tensor("out_" + name, shape, F32, kind="ExternalOutput").ap()
    hybrid_step(nc, t, o)
    r = run_bass_kernel_spmd(nc, [{"in_" + k: a for k, a in arrays.items()}], core_ids=[0])
    return tuple(r.results[0]["out_" + name] for name, _ in _OUTS)
```

```python
from contextlib import ExitStack

import concourse.bass as bass
from concourse import mybir

F32 = mybir.dt.float32
I32 = mybir.dt.int32
ALU = mybir.AluOpType
ACT = mybir.ActivationFunctionType
AX = mybir.AxisListType

P = 128
D = 1024
KD = D // P
NP_TOK, NB, LB = 256, 8, 8
NT = NP_TOK + NB * LB
TT = 3
TW = [128, 128, 64]
G, ST, GW = 32, 64, 16
NJ, NI = 4, 4
NK = NJ * NI
H = 4
NE = 32
SLOTS = 64
EXTRA = 20
RING, SW = 12, 2048
ZT = 36
ZG = 6
ZU, ZQ, ZK, ZV, ZO, ZGS, ZGM = 0, 4, 8, 12, 16, 20, 28
EPS = 1e-6
KSCALE = float(P) ** -0.5
TWO_PI = 6.2831845
ROUND = 12582912.0
LIMIT, ALPHA = 7.0, 1.702

CONST = {}
_at = 0
for _name, _n in (("ident", P), ("ones", P), ("triu", P), ("slot", SLOTS), ("tloc", NT), ("amask", 448),
                  ("seqm", NB), ("half", 2), ("par", 2), ("npar", 2), ("imask", NI), ("start", NT),
                  ("sel", H * P), ("pidx", 1), ("halfpi", 1)):
    CONST[_name] = (_at, _at + _n)
    _at += _n
CONST_W = _at


def hybrid_step(nc, t, o):
    ctx = ExitStack()
    with ctx:
        def sb(name, shape, dt=F32):
            return ctx.enter_context(nc.sbuf_tensor(name, shape, dt))

        def sem(name):
            return ctx.enter_context(nc.semaphore(name))

        bank = [ctx.enter_context(nc.psum_tensor(f"bank{i}", [P, 512], F32)) for i in range(8)]

        ring = sb("ring", [P, RING * SW])
        zT = sb("zT", [P, ZT * NT])
        hnT = sb("hnT", [P, KD * NT])
        xkv = sb("xkv", [P, TT * D])
        cst = sb("cst", [P, CONST_W])
        BT = sb("BT", [P, 2, NJ, P])
        CT = sb("CT", [P, 2, NJ, P])
        rows = sb("rows", [P, 704])
        hrow = sb("hrow", [P, 7 * 384])
        att = sb("att", [P, 1664])
        small = sb("small", [P, 1280])
        cnt_i = sb("cnt_i", [1, 1 + EXTRA], I32)

        def slot(s, n=SW):
            return ring[:, s * SW:s * SW + n]

        def c(name, n=None):
            a, b = CONST[name]
            return cst[:, a:b]

        def Z(n, m=1):
            return zT[:, n * NT:(n + m) * NT]

        def zz(a, n):
            return zT[:, a:a + n]

        ident = c("ident")
        ones = c("ones")
        x3 = xkv[:, :].rearrange("p (t d) -> p t d", t=TT)
        hn3 = hnT[:, :].rearrange("p (k n) -> p k n", k=KD)

        s5 = 6 * SW
        JW = NI * NT

        def S(n, w=JW):
            return ring[:, s5 + n:s5 + n + w]

        bu_r, bu_i, t1, t2, XR, XI, rho4 = (S(n * JW) for n in range(7))
        vec_rows, h0_rows_r, h0_rows_i, n_rows = (S(9 * JW + n * P, P) for n in range(4))
        um = Z(32, NI)
        tab = [(xkv[:, 0:JW], xkv[:, JW:2 * JW]), (S(7 * JW), S(8 * JW))]
        pz = 24 * NT
        so = BT[:, 0].rearrange("p j q -> p (j q)")
        bn_r, bn_i, bb_r, bb_i, btmp = (zz(pz + 256 * n, 256) for n in range(5))
        Bx = zz(pz + 1280, 1024)
        cn = zz(pz + 2304, 512)
        Cx = zz(pz + 2816, 1024)

        at = [0]

        def sm(w):
            at[0] += w
            return small[:, at[0] - w:at[0]]

        vec = sm(80)
        V_LDT, V_ARE, V_AIM, V_GMIX, V_GFFN, V_GPLE, V_D, V_BGLU = 0, 16, 32, 48, 56, 64, 72, 76

        def v(off, n):
            return vec[:, off:off + n]

        ssq, rstd = sm(4), sm(4)
        dt_, adr, mag, fr, fr_r = sm(16), sm(16), sm(16), sm(32), sm(32)
        sc = sm(32)
        ab_r, ab_i, nr, den, co_r, co_i, tm = (sm(16) for _ in range(7))
        h0T = sm(256)
        ah = sm(256)
        n0T = sm(36)
        fin_s = sm(256)
        fin_p = sm(32)
        asT = sm(24)
        gb = sm(2)
        m09 = sm(9)
        brb = sm(32)
        assert at[0] <= 1280, at

        v_tok = xkv[:, 0:TT * 512].rearrange("p (t d) -> p t d", t=TT)
        qw2, qn2 = ([xkv[:, a:a + 64] for a in (a0, a0 + 64)] for a0 in (1536, 1664))
        sgl = xkv[:, 1792:1792 + 4 * NT]
        cp_rows, nT_rows = sgl[:, 0:512], sgl[:, 512:640]
        ig, lf, bb, mm, arow, wrow, tmpr = (hrow[0:H, 384 * n:384 * n + 384] for n in range(7))
        kw_all = att[:, 0:H * 384]
        ml = 6 * SW

        def M(a, n):
            return ring[:, ml + a:ml + a + n]

        et2, bc2 = (M(0, 448), M(448, 448)), (M(896, 384), M(1280, 384))
        den_a = M(1664, NT)
        vx2 = [M(2048 + 1024 * n, 1024).rearrange("p (b e) -> p b e", b=NB) for n in range(2)]
        C0 = ring[:, 8 * SW:10 * SW].rearrange("p (h b e) -> p h b e", h=H, b=NB)

        acc = zz(ZK * NT, TT * D).rearrange("p (t d) -> p t d", t=TT)
        btab = [zz(ZU * NT, D), zz(ZQ * NT, D)]
        bdown = att[:, 0:512]
        wr_sb = zz(ZQ * NT + D, 256)
        mg, ms, mu = (zz(6400 + 512 * n, 512) for n in range(3))
        m0_ = 28 * NT
        sel = zz(m0_, 192).rearrange("p (t s) -> p t s", t=TT)
        selw = zz(m0_ + 192, 384).rearrange("p (t a s) -> p t a s", t=TT, a=2)
        onehot = zz(m0_ + 576, 64)
        p_lo, p_hi = zz(m0_ + 640, 384), zz(m0_ + 1024, 384)
        rk = zz(m0_ + 1408, 99).rearrange("p (t e) -> p t e", t=TT)
        wt = zz(m0_ + 1507, 99).rearrange("p (t e) -> p t e", t=TT)
        lg, msk, gtm, eqm, exw = (zz(m0_ + 1606 + 96 * n, 96).rearrange("p (t e) -> p t e", t=TT)
                                  for n in range(5))
        mtop = zz(m0_ + 2086, 24).rearrange("p (t e) -> p t e", t=TT)
        mcol = zz(m0_ + 2110, 12)
        nov, cinc, ind = (zz(m0_ + 2122 + 32 * n, 32) for n in range(3))
        opass = zz(m0_ + 2218, 4)
        dtab = zz(m0_ + 2222, 2 * EXTRA)
        obase = zz(m0_ + 2262, EXTRA)
        islot = zz(m0_ + 2282, SLOTS)
        xs, xsT, hT, yb, hb = (hnT[:, 512 * n:512 * n + 512] for n in range(5))
        pproj = [CT[:, :].rearrange("p a j q -> p (a j q)"), zz(6400 + 1536, D), BT[:, :].rearrange("p a j q -> p (a j q)")]
        gfin = ring[:, 8 * SW:8 * SW + D]
        p_tok = zz(5632, TT * 256).rearrange("p (t d) -> p t d", t=TT)
        pT = hrow[:, 0:2 * 384].rearrange("p (k n) -> p k n", k=2)

        slot_full = [sem(f"slot_full{s}") for s in range(RING)]
        slot_free = [sem(f"slot_free{s}") for s in range(RING) if s % 4 < 3]
        x_full = [sem(f"x_full{tt}") for tt in range(TT)]
        ident_full, cst_full, vec_full, wif_full = (sem(n) for n in ("ident_full", "cst_full", "vec_full", "wif_full"))
        bn_full, st_full, gb_full, c0_full = sem("bn_full"), sem("st_full"), sem("gb_full"), sem("c0_full")
        bt_full, wr_full, res_full, ple_full, gfin_full = (sem(n) for n in (
            "bt_full", "wr_full", "res_full", "ple_full", "gfin_full"))
        stored, stored_pool = sem("stored"), sem("stored_pool")
        zeroed = sem("zeroed")
        ssq_ready, sd_ready = sem("ssq_ready"), sem("sd_ready")
        xn_ready, xT_done, hnT_ready = sem("xn_ready"), sem("xT_done"), sem("hnT_ready")
        vecT_done, vec_ready = sem("vecT_done"), sem("vec_ready")
        ldt_ready = sem("ldt_ready")
        par_act, par_dve = sem("par_act"), sem("par_dve")
        bx_ready, bxT_done, bct_ready = sem("bx_ready"), sem("bxT_done"), sem("bct_ready")
        stT_done, stT_ready = sem("stT_done"), sem("stT_ready")
        z_done, z_ready = sem("z_done"), sem("z_ready")
        gate_done, gate_rows, gate_act, row_ready, R_ready = (sem(n) for n in (
            "gate_done", "gate_rows", "gate_act", "row_ready", "R_ready"))
        asT_done, asT_ready = sem("asT_done"), sem("asT_ready")
        fb_ready, fb_red, tab_ready, um_ready = (sem(n) for n in (
            "fb_ready", "fb_red", "tab_ready", "um_ready"))
        bu_done, bu_ready, rotin_done, rotout_done, s5d = (sem(n) for n in (
            "bu_done", "bu_ready", "rotin_done", "rotout_done", "s5d"))
        fin_ready, finT_done, finT_ready = sem("fin_ready"), sem("finT_done"), sem("finT_ready")
        y_done, yd_ready, gelu_ready, glu_done, sgl_ready, ys_ready = (sem(n) for n in (
            "y_done", "yd_ready", "gelu_ready", "glu_done", "sgl_ready", "ys_ready"))
        g_sig = sem("g_sig")
        kvT_done, kv_ready, rho_ready = sem("kvT_done"), sem("kv_ready"), sem("rho_ready")
        E_done, bc_done, bc_ready, em_ready, ex_ready, S_done, P_ready = (sem(n) for n in (
            "E_done", "bc_done", "bc_ready", "em_ready", "ex_ready", "S_done", "P_ready"))
        qw_ready, qn_ready, N_done, den_done, ym_ready = (sem(n) for n in (
            "qw_ready", "qn_ready", "N_done", "den_done", "ym_ready"))
        vx_ready, C_done, C_half, C_ready, att_d = (sem(n) for n in (
            "vx_ready", "C_done", "C_half", "C_ready", "att_d"))
        abs_ready = sem("abs_ready")
        cp_ready, nT_done, nT_ready = sem("cp_ready"), sem("nT_done"), sem("nT_ready")
        up_done, up_dve, merged = sem("up_done"), sem("up_dve"), sem("merged")
        out_done, h_ready = sem("out_done"), sem("h_ready")
        ch = sem("dve_chain")
        ach = sem("act_chain")
        rl_done, rl_ready, mask_ready, rank_done, tab_made = (sem(n) for n in (
            "rl_done", "rl_ready", "mask_ready", "rank_done", "tab_made"))
        ob_done, cnt_ready = sem("ob_done"), sem("cnt_ready")
        sel_ready, selw_ready, oh_ready = sem("sel_ready"), sem("selw_ready"), sem("oh_ready")
        gath_done, xs_ready, xsT_done, xsT_ready = (sem(n) for n in (
            "gath_done", "xs_ready", "xsT_done", "xsT_ready"))
        g_done, u_done, g_ready, s_ready, u_ready, gu_ready, hb_ready = (sem(n) for n in (
            "g_done", "u_done", "g_ready", "s_ready", "u_ready", "gu_ready", "hb_ready"))
        hTt_done, hT_ready, pw_done, pw_ready, dn_done, y_ready, sc_done, acc_add = (sem(n) for n in (
            "hTt_done", "hT_ready", "pw_done", "pw_ready", "dn_done", "y_ready", "sc_done", "acc_add"))
        pj_done, pj_ready, pTt_done, pT_ready = (sem(n) for n in (
            "pj_done", "pj_ready", "pTt_done", "pT_ready"))
        shifted = sem("shifted")
        gt_done, gt_sig, fin_h, out_ready = sem("gt_done"), sem("gt_sig"), sem("fin_h"), sem("out_ready")

        block = ctx.enter_context(nc.Block())

        w_in = t["w_in"][0].rearrange("(k p) n -> p k n", p=P)

        def zcol(ch_):
            return 256 * ch_ if ch_ < 10 else 2568 + 256 * (ch_ - 10)

        def z_slot(ch_):
            i = ch_ if ch_ < 15 else ch_ + 3
            return i % ZG, i // ZG

        def wait_read(engine, s, n):
            if s % 4 == 3:
                engine.wait_ge((g_done, u_done, dn_done)[s // 4], n)
            else:
                engine.wait_ge(slot_free[3 * (s // 4) + s % 4], n)

        def w3(s, k, n):
            return ring[:, s * SW:s * SW + k * n].rearrange("p (k n) -> p k n", k=k)

        wexp = [t[n][0].rearrange("e (k p) n -> e p k n", p=P) for n in ("w_gate", "w_up", "w_down")]
        USED0 = [5, 4, 4, 4, 3, 3, 0, 0, 1, 1, 1, 2]
        ZSTAGE = [range(6, 12), range(12, 18), range(18, 23), range(23, 28)]
        ZHEAD = [(29, 30), (31, 32), (33, 34), (35,)]
        GLU_BANK = [1, 5, 6, 0]
        PJ_BANK = [0, 1, 3, 7]

        def z_bank(n):
            return n % 4 if n < ZGM else 0

        WOUT = [10, 11, 8, 9]

        def rows256(name, i):
            return t[name][0, 256 * i:256 * i + 256].rearrange("(k p) n -> p k n", p=P)

        @block.sync
        def _(sp):
            xp = t["x_prompt"][0].rearrange("(t p) d -> p t d", p=P)
            xd = t["x_sample"].rearrange("b l d -> (b l) d")
            for tt in range(2):
                sp.dma_start(x3[:, tt, :], xp[:, tt, :]).then_inc(x_full[tt], 16)
            sp.dma_start(x3[0:64, 2, :], xd).then_inc(x_full[2], 16)
            sp.dma_start(cst[:, 0:P], t["cst"][:, 0:P]).then_inc(ident_full, 16)
            fl = "(a b) -> a b"
            for r0, name, n in ((V_ARE, "ssm_a_re", 16), (V_AIM, "ssm_a_im", 16)):
                sp.dma_start(vec_rows[r0:r0 + n, :], t[name][0].rearrange("(k g) s -> k (g s)", g=2)).then_inc(vec_full, 16)
            for r0, name in ((V_GMIX, "g_mix"), (V_GFFN, "g_ffn"), (V_GPLE, "g_ple")):
                sp.dma_start(vec_rows[r0:r0 + 8, :], t[name][0].rearrange(fl, b=P)).then_inc(vec_full, 16)
            sp.dma_start(vec_rows[V_D:V_D + 4, :], t["ssm_d"][0].rearrange("(j g) h -> j (g h)", g=8)).then_inc(vec_full, 16)
            sp.dma_start(vec_rows[V_BGLU:V_BGLU + 4, :], t["ssm_b_glu"][0].rearrange(fl, b=P)).then_inc(vec_full, 16)
            sp.dma_start(ssq[0:16, 0:2], t["ssm_log_dt"][0].rearrange("(k g) -> k g", g=2)).then_inc(vec_full, 16)

            def load(s, src, k=2, n=D):
                sp.dma_start(w3(s, k, n), src).then_inc(slot_full[s], 16)

            def load_z(ch_):
                s, use = z_slot(ch_)
                if use:
                    sp.wait_ge(z_done, 2 * (ch_ - (ZG if ch_ < 15 else 3)) + 2)
                load(s, w_in[:, :, zcol(ch_):zcol(ch_) + 256], KD, 256)

            load_z(0)
            sp.dma_start(cst[:, P:], t["cst"][:, P:]).then_inc(cst_full, 16)
            for ch_ in range(1, 15):
                load_z(ch_)
            sp.wait_ge(z_done, 20)
            load(3, t["ssm_w_glu"][0].rearrange("(k p) n -> p k n", p=P), 4, 512)
            for i in range(2):
                sp.wait_ge(z_done, 22 + 2 * i)
                load(4 + i, rows256("w_ssm_up", i))
            load_z(15)
            load_z(16)
            sp.wait_ge(y_done, NJ)
            sp.wait_ge(fin_ready, 4 * NJ)
            for h in range(H):
                sp.dma_start(C0[:, h], t["state_ml_c"][0, :, h].rearrange("b d e -> d b e")).then_inc(c0_full, 16)
            sp.wait_ge(glu_done, 4)
            load(3, rows256("w_ml_up", 0))
            load_z(17)
            for i in range(2):
                load(WOUT[i], rows256("w_out", i))
            sp.wait_ge(z_done, 32)
            load(0, rows256("w_ml_up", 1))

            def load_first(s):
                load(s, wexp[s // 4][0, :, 2 * (s % 4):2 * (s % 4) + 2, :])

            for h in range(H):
                sp.wait_ge(C_ready, h + 1)
                sp.dma_start(o["cs"][0, :, h].rearrange("b d e -> d b e"), C0[:, h]).then_inc(stored, 16)
            sp.wait_ge(ym_ready, H)
            sp.dma_start(acc[:, 0:2, :], xp).then_inc(res_full, 16)
            sp.dma_start(acc[0:64, 2, :], xd).then_inc(res_full, 16)
            sp.dma_start(p_tok[:, 0:2, :], t["p_prompt"][0, 0].rearrange("(t p) d -> p t d", p=P)).then_inc(ple_full, 16)
            sp.dma_start(p_tok[0:64, 2, :], t["p_sample"][0].rearrange("b l d -> (b l) d")).then_inc(ple_full, 16)
            sp.wait_ge(stored, 16 * H)
            for i in range(2, 4):
                load(WOUT[i], rows256("w_out", i))
            sp.wait_ge(zeroed, 7)
            for hf in range(2):
                sp.dma_start(bdown[64 * hf:64 * hf + NE, :], t["b_down"][0, :, 512 * hf:512 * hf + 512]).then_inc(bt_full, 16)
            sp.wait_ge(z_done, ZT)
            sp.wait_ge(up_done, KD)
            for s in (1, 2, 4, 5, 6, 7):
                load_first(s)
            sp.wait_ge(zeroed, 8)
            sp.dma_start(btab[0][0:NE, :], t["b_gate"][0]).then_inc(bt_full, 16)
            sp.wait_ge(up_done, 2 * KD)
            for s in (0, 3):
                load_first(s)
            sp.wait_ge(zeroed, 10)
            sp.dma_start(btab[1][0:NE, :], t["b_up"][0]).then_inc(bt_full, 16)
            sp.dma_start(wr_sb.rearrange("p (k e) -> p k e", k=KD), t["w_router"][0].rearrange("(k p) e -> p k e", p=P)).then_inc(wr_full, 16)
            sp.wait_ge(out_done, 5)
            load(11, rows256("w_ple_proj", 0))
            for s in range(8, RING):
                if s == 11:
                    sp.wait_ge(pj_done, 6)
                load_first(s)

            def load_pass(e, n):
                for s in range(RING):
                    wait_read(sp, s, n)
                    k = 2 * (s % 4)
                    sp.dma_start(w3(s, 2, D), wexp[s // 4][bass.ds(e, 1), :, k:k + 2, :].rearrange("a p k n -> (a p) k n")).then_inc(slot_full[s], 16)

            with sp.Fori(1, NE) as p:
                load_pass(p, p)
            sp.wait_ge(cnt_ready, 1)
            extra = sp.value_load(cnt_i[0:1, 0:1], min_val=0, max_val=EXTRA)
            with sp.If(extra > 0):
                with sp.Fori(0, extra) as q:
                    e = sp.value_load(cnt_i[0:1, bass.ds(q + 1, 1)], min_val=0, max_val=NE - 1)
                    load_pass(e, q + NE)
            for s in range(4):
                wait_read(sp, s, extra + NE)
                sp.dma_start(w3(s, 2, D), t["w_ple_gate"][0, 256 * s:256 * s + 256].rearrange("(k p) n -> p k n", p=P)).then_inc(slot_full[s], 16)
            wait_read(sp, 8, extra + NE)
            sp.dma_start(gfin, t["g_final"].rearrange("(a n) -> a n", a=1).to_broadcast([P, D])).then_inc(gfin_full, 16)
            yp = o["yp"][0].rearrange("(t p) d -> t p d", p=P)
            for tt in range(TT):
                sp.wait_ge(out_ready, tt + 1)
                if tt < 2:
                    sp.dma_start(yp[tt], acc[:, tt, :]).then_inc(stored, 16)
                else:
                    sp.dma_start(o["ys"].rearrange("b l d -> (b l) d"), acc[0:64, 2, :]).then_inc(stored, 16)
            sp.wait_ge(stored, 16 * (H + TT))
            sp.wait_ge(stored_pool, 16 * 9)

        @block.gpsimd
        def _(pool):
            ms_ = nc.gpsimd.memset
            ms_(xkv[64:128, 2 * D:3 * D], 0.0).then_inc(zeroed, 1)
            pool.wait_ge(zeroed, 1)
            ms_(rows[:, :], 0.0).then_inc(zeroed, 1)
            pool.wait_ge(zeroed, 2)
            ms_(hrow[0:H, 4 * 384:6 * 384], 0.0).then_inc(zeroed, 1)
            pool.wait_ge(zeroed, 3)
            pool.wait_ge(slot_full[1], 16)
            for n, name in enumerate(("ssm_b_re", "ssm_b_im")):
                src = t[name][0].rearrange("g s h -> (g s) h").rearrange("(k q) h -> q k h", q=P)
                pool.dma_start((bn_r, bn_i)[n].rearrange("p (k h) -> p k h", k=NK), src).then_inc(bn_full, 16)
            for n, name in enumerate(("ssm_c_re", "ssm_c_im")):
                src = t[name][0].rearrange("g h s -> (g h) s").rearrange("(j q) s -> q j s", q=P)
                pool.dma_start(cn[:, 256 * n:256 * n + 256].rearrange("p (j s) -> p j s", j=NJ), src).then_inc(bn_full, 16)
            pool.dma_start(h0_rows_r, t["state_ssm_re"][0].rearrange("b g s -> b (g s)").rearrange("b (k q) -> b k q", q=P).rearrange("b k q -> (b k) q")).then_inc(st_full, 16)
            pool.dma_start(h0_rows_i, t["state_ssm_im"][0].rearrange("b g s -> b (g s)").rearrange("b (k q) -> b k q", q=P).rearrange("b k q -> (b k) q")).then_inc(st_full, 16)
            pool.dma_start(n_rows[0:32, :], t["state_ml_n"][0].rearrange("b h d -> (b h) d")).then_inc(st_full, 16)
            pool.dma_start(gb[0:H, 0:1], t["ml_b_ig"][0].rearrange("(a b) -> a b", b=1)).then_inc(gb_full, 16)
            pool.dma_start(gb[0:H, 1:2], t["ml_b_fg"][0].rearrange("(a b) -> a b", b=1)).then_inc(gb_full, 16)
            pool.dma_start(m09[0:H, 1:9], t["state_ml_m"][0].rearrange("b h -> h b"), allow_slow_non_contiguous=True).then_inc(gb_full, 16)
            pool.dma_start(brb, t["b_router"].to_broadcast([P, NE])).then_inc(gb_full, 16)
            wif = att[:, 0:KD * 36].rearrange("p (k n) -> p k n", k=KD)
            ms_(att[:, 0:KD * 36], 0.0).then_inc(zeroed, 1)
            pool.wait_ge(zeroed, 4)
            pool.dma_start(wif[:, :, 0:4], w_in[:, :, 2560:2564]).then_inc(wif_full, 16)
            pool.dma_start(wif[:, :, 32:36], w_in[:, :, 2564:2568]).then_inc(wif_full, 16)

            pool.wait_ge(gate_done, 1)
            ms_(kw_all.rearrange("p (h t) -> p h t", h=H)[64:128, :, 256:384], 0.0).then_inc(zeroed, 1)
            pool.wait_ge(zeroed, 5)

            for j in range(NJ):
                if j == NJ - 1:
                    pool.wait_ge(rotout_done, 2 * j)
                    ms_(v_tok[64:128, 2, :], 0.0).then_inc(zeroed, 1)
                    pool.wait_ge(zeroed, 6)
                for n, X in enumerate((XR, XI)):
                    X3 = X.rearrange("p (i n) -> p i n", i=NI)
                    pool.wait_ge(rotout_done, 2 * j + n + 1)
                    f4 = fin_s[:, 128 * n:128 * n + 128].rearrange("p (b k) -> p k b", b=NB)
                    nc.gpsimd.tensor_copy(f4[:, NI * j:NI * j + NI, :],
                                          X3[:, :, NP_TOK + LB - 1:NT:LB]).then_inc(fin_ready, 1)
                    pool.wait_ge(fin_ready, 4 * j + 2 * n + 1)
                    nc.gpsimd.tensor_copy(fin_p[:, 16 * n + NI * j:16 * n + NI * j + NI],
                                          X3[:, :, NP_TOK - 1:NP_TOK].rearrange("p i a -> p (i a)")).then_inc(fin_ready, 1)
                    pool.wait_ge(fin_ready, 4 * j + 2 * n + 2)
            pool.wait_ge(finT_ready, 3)
            pool.dma_start(o["rs"][0].rearrange("b g s -> b (g s)").rearrange("b (k q) -> (b k) q", q=P), so[:, 0:128]).then_inc(stored_pool, 16)
            pool.dma_start(o["is"][0].rearrange("b g s -> b (g s)").rearrange("b (k q) -> (b k) q", q=P), so[:, 128:256]).then_inc(stored_pool, 16)
            pool.dma_start(o["rp"][0, 0].rearrange("(k g) s -> k (g s)", g=2), so[0:16, 256:384]).then_inc(stored_pool, 16)
            pool.dma_start(o["ip"][0, 0].rearrange("(k g) s -> k (g s)", g=2), so[16:32, 256:384]).then_inc(stored_pool, 16)
            pool.wait_ge(row_ready, 1)
            pool.dma_start(o["mp"][0].rearrange("b h -> h b"), mm[:, NP_TOK - 1:NP_TOK], allow_slow_non_contiguous=True).then_inc(stored_pool, 16)
            pool.dma_start(o["ms"][0].rearrange("b h -> h b"), mm[:, NP_TOK + LB - 1:NT:LB], allow_slow_non_contiguous=True).then_inc(stored_pool, 16)
            pool.wait_ge(cp_ready, H)
            pool.dma_start(o["cp"][0, 0].rearrange("h d e -> d h e"), cp_rows.rearrange("p (h e) -> p h e", h=H)).then_inc(stored_pool, 16)
            pool.wait_ge(nT_ready, 1)
            pool.dma_start(o["ns"][0].rearrange("b h d -> (b h) d"), nT_rows[0:32, :]).then_inc(stored_pool, 16)
            pool.dma_start(o["np"][0, 0], nT_rows[32:36, :]).then_inc(stored_pool, 16)
            pool.wait_ge(C_ready, H)
            pool.wait_ge(ym_ready, H)
            ms_(bdown, 0.0).then_inc(zeroed, 1)
            pool.wait_ge(up_done, KD)
            pool.wait_ge(zeroed, 7)
            ms_(btab[0], 0.0).then_inc(zeroed, 1)
            pool.wait_ge(zeroed, 8)
            ms_(acc[64:128, 2, :], 0.0).then_inc(zeroed, 1)
            pool.wait_ge(up_done, 2 * KD)
            pool.wait_ge(zeroed, 9)
            ms_(btab[1], 0.0).then_inc(zeroed, 1)
            pool.wait_ge(merged, KD)
            pool.wait_ge(zeroed, 10)
            ms_(zz(m0_ + 640, 768), 0.0).then_inc(zeroed, 1)
            pool.wait_ge(zeroed, 11)
            ms_(lg.rearrange("p t e -> p (t e)"), 0.0).then_inc(zeroed, 1)
            pool.wait_ge(zeroed, 12)
            ms_(selw.rearrange("p t a s -> p (t a s)"), 0.0).then_inc(zeroed, 1)

        @block.scalar
        def _(act):
            a = nc.scalar.activation
            cnt = [0]

            def link(ins):
                cnt[0] += 1
                ins.then_inc(ach, 1)
                act.wait_ge(ach, cnt[0])

            def square(tt, src, scratch):
                a(scratch, src, ACT.Square, accum_out=rstd[:, tt:tt + 1]).then_inc(ssq_ready, 1)

            def sqrt(r, tt):
                act.wait_ge(sd_ready, 6 * r + 2 * tt + 1)
                a(rstd[:, tt:tt + 1], rstd[:, tt:tt + 1], ACT.Sqrt).then_inc(sd_ready, 1)

            def norm(r, tt, src, scratch):
                square(tt, src, scratch)
                sqrt(r, tt)

            act.wait_ge(zeroed, 1)
            link(a(xkv[64:128, 2 * D:2 * D + 1], xkv[64:128, 2 * D:2 * D + 1], ACT.Sqrt))
            for tt in range(TT):
                act.wait_ge(x_full[tt], 16)
                square(tt, x3[:, tt, :], S(tt * D, D))
                if tt:
                    sqrt(0, tt - 1)
            sqrt(0, TT - 1)
            act.wait_ge(vec_ready, 1)
            a(dt_, v(V_LDT, 16), ACT.Exp).then_inc(par_act, 1)
            act.wait_ge(par_dve, 1)
            a(mag, adr, ACT.Exp).then_inc(par_act, 1)
            act.wait_ge(par_dve, 2)
            act.wait_ge(cst_full, 16)
            a(sc, fr_r, ACT.Sin, scale=TWO_PI).then_inc(par_act, 1)
            def z_evac(n):
                act.wait_ge(z_done, n + 1)
                a(Z(n), bank[z_bank(n)][:, 0:NT], ACT.Copy).then_inc(z_ready, 1)

            for n in range(4):
                z_evac(n)
            for n in range(4):
                act.wait_ge(bxT_done, n + 1)
                dst = (BT, CT)[n // 2][:, n % 2]
                a(dst.rearrange("p j q -> p (j q)"), bank[4 + n][:, :], ACT.Copy).then_inc(bct_ready, 1)
            z_evac(4)
            act.wait_ge(stT_done, 1)
            a(h0T, bank[4][:, 0:256], ACT.Copy).then_inc(stT_ready, 1)
            a(n0T[:, 0:32], bank[4][:, 256:288], ACT.Copy).then_inc(stT_ready, 1)

            def masked_u(j):
                for i in range(NI):
                    a(um[:, i * NT:i * NT + NT], Z(ZU + j), ACT.Copy, scale=c("imask")[:, i:i + 1]).then_inc(um_ready, 1)

            def turns(j):
                F = tab[j % 2][1]
                for i in range(NI):
                    a(F[:, i * NT:i * NT + NT], c("tloc"), ACT.Copy, scale=fr[:, NI * j + i:NI * j + i + 1]).then_inc(fb_ready, 1)

            def sines(j):
                cos_, sin_ = tab[j % 2]
                act.wait_ge(fb_red, j + 1)
                a(cos_, sin_, ACT.Abs).then_inc(tab_ready, 1)
                a(sin_, sin_, ACT.Sin, scale=TWO_PI).then_inc(tab_ready, 1)
                act.wait_ge(tab_ready, 3 * j + 1)
                a(cos_, cos_, ACT.Sin, scale=-TWO_PI, bias=c("halfpi")).then_inc(tab_ready, 1)

            def gelu(j):
                act.wait_ge(yd_ready, j + 1)
                a(Z(ZU + j), Z(ZU + j), ACT.Gelu_apprx_tanh).then_inc(gelu_ready, 1)

            masked_u(0)
            act.wait_ge(xT_done, 2 * TT)
            turns(0)
            z_evac(5)
            for j in range(NJ):
                if j:
                    act.wait_ge(rotin_done, j)
                for q in range(8):
                    act.wait_ge(bu_done, 8 * j + q + 1)
                    dst = (bu_r, bu_i)[q % 2][:, (q // 2) * NT:(q // 2 + 1) * NT]
                    a(dst, bank[4 + q % 3][:, 0:NT], ACT.Copy).then_inc(bu_ready, 1)
                if j == 0:
                    sines(0)
                if j:
                    act.wait_ge(rotout_done, 2 * j)
                for i in range(NI):
                    a(rho4[:, i * NT:i * NT + NT], c("start"), ACT.Copy, scale=mag[:, NI * j + i:NI * j + i + 1]).then_inc(rho_ready, 1)
                if j < NJ - 1:
                    turns(j + 1)
                    masked_u(j + 1)
                if j == 1:
                    act.wait_ge(gate_rows, 3)
                    link(a(tmpr[:, 0:NT], tmpr[:, 0:NT], ACT.Abs))
                    link(a(tmpr[:, 0:NT], tmpr[:, 0:NT], ACT.Exp, scale=-1.0))
                    a(tmpr[:, 0:NT], tmpr[:, 0:NT], ACT.Ln, bias=1.0).then_inc(gate_act, 1)
                if j == 2:
                    act.wait_ge(row_ready, 1)
                    a(rows[0:H, NT:2 * NT], mm[:, 0:NT], ACT.Exp, scale=-1.0).then_inc(R_ready, 1)
                    a(rows[0:H, 2 * NT:2 * NT + 64], rows[0:H, 2 * NT:2 * NT + 64], ACT.Exp).then_inc(R_ready, 1)
                    a(wrow[:, 0:NT], wrow[:, 0:NT], ACT.Exp).then_inc(R_ready, 1)
                zn = ZSTAGE[j]
                for n in zn[:2]:
                    z_evac(n)
                if j == 2:
                    act.wait_ge(asT_done, 1)
                    a(asT[:, 0:12], bank[4][:, 0:12], ACT.Copy).then_inc(asT_ready, 1)
                    a(asT[:, 12:24], bank[4][:, 12:24], ACT.Copy, scale=KSCALE).then_inc(asT_ready, 1)
                if j < NJ - 1:
                    sines(j + 1)
                else:
                    act.wait_ge(asT_ready, 2)
                    act.wait_ge(zeroed, 6)
                    for g in range(2 * H):
                        h = g % H
                        act.wait_ge(kvT_done, g + 1)
                        for tt in range(TT):
                            w = TW[tt]
                            src = bank[4 + g % 3][0:w, tt * P:tt * P + P]
                            if g < H:
                                a(kw_all[0:w, h * 384 + tt * P:h * 384 + tt * P + P], src, ACT.Copy,
                                  scale=asT[0:w, 12 + tt * H + h:13 + tt * H + h]).then_inc(kv_ready, 1)
                            else:
                                a(v_tok[0:w, tt, h * P:h * P + P], src, ACT.Copy).then_inc(kv_ready, 1)
                for n in zn[2:]:
                    z_evac(n)
                if j:
                    gelu(j - 1)

            def bc_copy(h):
                act.wait_ge(bc_done, h + 1)
                if h >= 2:
                    act.wait_ge(C_ready, h - 1)
                a(bc2[h % 2], bank[4][:, 0:384], ACT.Copy).then_inc(bc_ready, 1)

            def decay_exp(h):
                act.wait_ge(em_ready, h + 1)
                et = et2[h % 2]
                for n, (c0, c1) in enumerate(((0, 256), (256, 384), (384, 448))):
                    a(et[:, c0:c1], et[:, c0:c1], ACT.Exp, bias=asT[:, n * H + h:n * H + h + 1]).then_inc(ex_ready, 1)

            act.wait_ge(rotout_done, 2 * NJ)
            bc_copy(0)
            decay_exp(0)
            gelu(NJ - 1)
            z_evac(ZGM)
            act.wait_ge(finT_done, 3)
            for n in range(3):
                rr = 128 if n < 2 else 32
                a(so[0:rr, 128 * n:128 * n + 128], bank[7][0:rr, 128 * n:128 * n + 128], ACT.Copy).then_inc(finT_ready, 1)
            for n in range(4):
                act.wait_ge(glu_done, n + 1)
                a(sgl[:, n * NT:n * NT + NT], bank[GLU_BANK[n]][:, 0:NT], ACT.Sigmoid, bias=v(V_BGLU + n, 1)).then_inc(sgl_ready, 1)
            act.wait_ge(z_ready, ZGM)
            a(Z(ZO, 4), Z(ZO, 4), ACT.Sigmoid).then_inc(g_sig, 1)
            a(Z(ZGS, 8), Z(ZGS, 8), ACT.Sigmoid).then_inc(g_sig, 1)
            for h in range(H):
                act.wait_ge(den_done, h + 1)
                if h:
                    act.wait_ge(ym_ready, h)
                a(den_a, bank[6][:, 0:NT], ACT.Abs).then_inc(abs_ready, 1)
                if h < H - 1:
                    bc_copy(h + 1)
                    decay_exp(h + 1)
                for n in ZHEAD[h]:
                    z_evac(n)
            act.wait_ge(z_ready, ZT)
            a(Z(ZGM, 8), Z(ZGM, 8), ACT.Sigmoid).then_inc(g_sig, 1)
            act.wait_ge(nT_done, 1)
            a(nT_rows[0:36, :], bank[4][0:36, 0:P], ACT.Copy).then_inc(nT_ready, 1)

            act.wait_ge(stored_pool, 16 * 9)
            for tt in range(TT):
                if tt == 2:
                    act.wait_ge(out_done, 5)
                    a(x3[0:64, 2, 512:1024], bank[4][64:128, :], ACT.Copy).then_inc(shifted, 1)
                act.wait_ge(h_ready, 2 * tt + 2)
                norm(1, tt, acc[:, tt, :], x3[:, tt, :])
            def gather_act(n):
                act.wait_ge(gath_done, n + 1)
                a(xs, bank[2][:, :], ACT.Copy).then_inc(xs_ready, 1)

            for k in range(2):
                act.wait_ge(pTt_done, k + 1)
                a(pT[:, k, :], bank[k][:, 0:384], ACT.Copy).then_inc(pT_ready, 1)
            for n in range(6):
                act.wait_ge(pj_done, n + 1)
                a(pproj[n // 2][:, (n % 2) * 512:(n % 2) * 512 + 512], bank[PJ_BANK[n % 4]][:, :], ACT.Copy).then_inc(pj_ready, 1)
                if n == 1:
                    act.wait_ge(rl_ready, 1)
                    a(exw.rearrange("p t e -> p (t e)"), exw.rearrange("p t e -> p (t e)"), ACT.Exp).then_inc(rl_ready, 1)
                if n == 2:
                    gather_act(0)
            act.wait_ge(rl_done, TT)
            act.wait_ge(bt_full, 64)
            a(yb, bdown, ACT.Copy).then_inc(y_ready, 1)

            def experts_act(n):
                act.wait_ge(g_ready, n + 1)
                a(ms, mg, ACT.Sigmoid, scale=ALPHA).then_inc(s_ready, 1)

            def down_act(n):
                act.wait_ge(hTt_done, n + 1)
                a(hT, bank[3][:, :], ACT.Copy).then_inc(hT_ready, 1)

            def y_act(n):
                act.wait_ge(dn_done, n + 1)
                a(yb, bank[5][:, :], ACT.Copy).then_inc(y_ready, 1)

            with act.Fori(0, NE) as p:
                experts_act(p)
                gather_act(p + 1)
                down_act(p)
                y_act(p)
            act.wait_ge(cnt_ready, 1)
            extra = act.value_load(cnt_i[0:1, 0:1], min_val=0, max_val=EXTRA)
            with act.If(extra > 0):
                with act.Fori(0, extra) as q:
                    gather_act(q + (NE + 1))
                    experts_act(q + NE)
                    down_act(q + NE)
                    y_act(q + NE)

            for tt in range(TT):
                act.wait_ge(acc_add, extra * 6 + (6 * NE + 2 + 2 * (tt + 1)))
                norm(2, tt, acc[:, tt, :], x3[:, tt, :])
            for tt in range(TT):
                for n in (2 * tt, 2 * tt + 1):
                    act.wait_ge(gt_done, min(n + 1, 5))
                    cs = slice((n % 2) * 512, (n % 2) * 512 + 512)
                    if tt < 2:
                        a(x3[:, tt, cs], bank[4 + n % 4][:, :], ACT.Sigmoid).then_inc(gt_sig, 1)
                    else:
                        a(x3[0:64, tt, cs], bank[4][64 * (n % 2):64 * (n % 2) + 64, :], ACT.Sigmoid).then_inc(gt_sig, 1)
                if tt:
                    act.wait_ge(fin_h, 2 * tt)
                    norm(3, tt - 1, acc[:, tt - 1, :], x3[:, tt - 1, :])
            act.wait_ge(fin_h, 2 * TT)
            norm(3, TT - 1, acc[:, TT - 1, :], x3[:, TT - 1, :])

        @block.vector
        def _(dve):
            V = nc.vector
            cnt = [0]

            def link(ins):
                cnt[0] += 1
                ins.then_inc(ch, 1)
                dve.wait_ge(ch, cnt[0])

            def root(r, tt):
                dve.wait_ge(ssq_ready, 3 * r + tt + 1)
                V.tensor_scalar(rstd[:, tt:tt + 1], rstd[:, tt:tt + 1], 1.0 / D, EPS, ALU.mult, ALU.add).then_inc(sd_ready, 1)
                dve.wait_ge(sd_ready, 6 * r + 2 * tt + 2)
                link(V.reciprocal(rstd[:, tt:tt + 1], rstd[:, tt:tt + 1]))

            def rms(r, tt, src):
                root(r, tt)
                V.tensor_scalar(x3[:, tt, :], src[:, tt, :], rstd[:, tt:tt + 1], None, ALU.mult).then_inc(xn_ready, 1)

            def hnT_evac(r, tt, g):
                w = TW[tt]
                for b in range(2):
                    dve.wait_ge(xT_done, 6 * r + 2 * tt + b + 1)
                    V.tensor_tensor(hn3[:, 4 * b:4 * b + 4, tt * P:tt * P + w],
                                    bank[(2 * tt + b) % 4][:, :].rearrange("p (k n) -> p k n", k=4)[:, :, 0:w],
                                    v(g + 4 * b, 4).unsqueeze(2).to_broadcast([P, 4, w]), ALU.mult).then_inc(hnT_ready, 1)

            for tt in range(TT):
                rms(0, tt, x3)
            dve.wait_ge(vec_full, 16 * 8)
            V.tensor_copy(vec_rows[0:16, :].rearrange("p (g s) -> p g s", g=2),
                          ssq[0:16, 0:2].unsqueeze(2).to_broadcast([16, 2, ST])).then_inc(ldt_ready, 1)
            dve.wait_ge(vecT_done, 1)
            V.tensor_copy(vec, bank[4][:, 0:80]).then_inc(vec_ready, 1)
            dve.wait_ge(vec_ready, 1)
            for tt in range(TT):
                hnT_evac(0, tt, V_GMIX)

            dve.wait_ge(par_act, 1)
            V.tensor_tensor(adr, v(V_ARE, 16), dt_, ALU.mult).then_inc(par_dve, 1)
            link(V.tensor_tensor(fr[:, 0:16], v(V_AIM, 16), dt_, ALU.mult))
            link(V.tensor_scalar(fr[:, 0:16], fr[:, 0:16], 1.0 / 6.283185307179586, None, ALU.mult))
            link(V.tensor_scalar(fr_r[:, 0:16], fr[:, 0:16], ROUND, ROUND, ALU.add, ALU.subtract))
            link(V.tensor_tensor(fr[:, 0:16], fr[:, 0:16], fr_r[:, 0:16], ALU.subtract))
            link(V.tensor_scalar(fr[:, 16:32], fr[:, 0:16], 0.25, None, ALU.add))
            link(V.tensor_scalar(fr_r, fr, ROUND, ROUND, ALU.add, ALU.subtract))
            V.tensor_tensor(fr_r, fr, fr_r, ALU.subtract).then_inc(par_dve, 1)
            dve.wait_ge(par_act, 3)
            link(V.tensor_tensor(ab_i, mag, sc[:, 0:16], ALU.mult))
            link(V.tensor_tensor(ab_r, mag, sc[:, 16:32], ALU.mult))
            ar, ai = v(V_ARE, 16), v(V_AIM, 16)
            link(V.tensor_scalar(nr, ab_r, -1.0, None, ALU.add))
            link(V.tensor_tensor(den, ar, ar, ALU.mult))
            link(V.tensor_tensor(tm, ai, ai, ALU.mult))
            link(V.tensor_tensor(den, den, tm, ALU.add))
            link(V.reciprocal(den, den))
            link(V.tensor_tensor(co_r, nr, ar, ALU.mult))
            link(V.tensor_tensor(tm, ab_i, ai, ALU.mult))
            link(V.tensor_tensor(co_r, co_r, tm, ALU.add))
            link(V.tensor_tensor(co_r, co_r, den, ALU.mult))
            link(V.tensor_tensor(co_i, ab_i, ar, ALU.mult))
            link(V.tensor_tensor(tm, nr, ai, ALU.mult))
            link(V.tensor_tensor(co_i, co_i, tm, ALU.subtract))
            link(V.tensor_tensor(co_i, co_i, den, ALU.mult))

            def k3(x_):
                return x_.rearrange("p (k h) -> p k h", k=NK)

            def bck(x_):
                return x_.unsqueeze(2).to_broadcast([P, NK, GW])

            dve.wait_ge(bn_full, 64)
            link(V.tensor_tensor(k3(bb_r), k3(bn_r), bck(co_r), ALU.mult))
            link(V.tensor_tensor(k3(btmp), k3(bn_i), bck(co_i), ALU.mult))
            link(V.tensor_tensor(bb_r, bb_r, btmp, ALU.subtract))
            link(V.tensor_tensor(k3(bb_i), k3(bn_i), bck(co_r), ALU.mult))
            link(V.tensor_tensor(k3(btmp), k3(bn_r), bck(co_i), ALU.mult))
            link(V.tensor_tensor(bb_i, bb_i, btmp, ALU.add))
            for n, src in enumerate((bb_r, bb_i)):
                V.tensor_tensor(Bx[:, 512 * n:512 * n + 512].rearrange("p (k a h) -> p k a h", k=NK, a=2),
                                k3(src).unsqueeze(2).to_broadcast([P, NK, 2, GW]),
                                c("half").unsqueeze(1).unsqueeze(3).to_broadcast([P, NK, 2, GW]), ALU.mult).then_inc(bx_ready, 1)
            for n, m_ in enumerate(("par", "npar")):
                V.tensor_tensor(Cx[:, 512 * n:512 * n + 512].rearrange("p (j a s) -> p j a s", j=NJ, a=2),
                                cn[:, 256 * n:256 * n + 256].rearrange("p (j s) -> p j s", j=NJ).unsqueeze(2).to_broadcast([P, NJ, 2, ST]),
                                c(m_).unsqueeze(1).unsqueeze(3).to_broadcast([P, NJ, 2, ST]), ALU.mult).then_inc(bx_ready, 1)
            dve.wait_ge(stT_ready, 2)
            h0v = h0T.rearrange("p (n b k) -> p n b k", n=2, b=NB)
            ahv = ah.rearrange("p (n b k) -> p n b k", n=2, b=NB)
            tv = bn_r[:, 0:128].rearrange("p (b k) -> p b k", b=NB)

            def bcb(x_):
                return x_.unsqueeze(1).to_broadcast([P, NB, NK])

            link(V.tensor_tensor(ahv[:, 0], h0v[:, 0], bcb(ab_r), ALU.mult))
            link(V.tensor_tensor(tv, h0v[:, 1], bcb(ab_i), ALU.mult))
            link(V.tensor_tensor(ahv[:, 0], ahv[:, 0], tv, ALU.subtract))
            link(V.tensor_tensor(ahv[:, 1], h0v[:, 1], bcb(ab_r), ALU.mult))
            link(V.tensor_tensor(tv, h0v[:, 0], bcb(ab_i), ALU.mult))
            link(V.tensor_tensor(ahv[:, 1], ahv[:, 1], tv, ALU.add))

            def i3(x_):
                return x_.rearrange("p (i n) -> p i n", i=NI)

            s5n = [0]

            def s5link(ins):
                s5n[0] += 1
                ins.then_inc(s5d, 1)
                dve.wait_ge(s5d, s5n[0])

            def reduce_turns(j):
                tmp, F = tab[j % 2]
                dve.wait_ge(fb_ready, 4 * (j + 1))
                s5link(V.tensor_scalar(tmp, F, ROUND, ROUND, ALU.add, ALU.subtract))
                V.tensor_tensor(F, F, tmp, ALU.subtract).then_inc(fb_red, 1)

            reduce_turns(0)
            for j in range(NJ):
                tabc, tabs = tab[j % 2]
                dve.wait_ge(bu_ready, 8 * (j + 1))
                dve.wait_ge(tab_ready, 3 * (j + 1))
                for n, b_ in enumerate((bu_r, bu_i)):
                    first = i3(b_)[:, :, NP_TOK:NT:LB]
                    s5link(V.tensor_tensor(first, first, ahv[:, n, :, NI * j:NI * j + NI].rearrange("p b i -> p i b"), ALU.add))
                s5link(V.tensor_tensor(t1, bu_r, tabc, ALU.mult))
                s5link(V.tensor_tensor(t2, bu_i, tabs, ALU.mult))
                s5link(V.tensor_tensor(t1, t1, t2, ALU.add))
                s5link(V.tensor_tensor(t2, bu_i, tabc, ALU.mult))
                s5link(V.tensor_tensor(bu_r, bu_r, tabs, ALU.mult))
                V.tensor_tensor(t2, t2, bu_r, ALU.subtract).then_inc(rotin_done, 1)
                if j < NJ - 1:
                    reduce_turns(j + 1)
                dve.wait_ge(rotin_done, j + 1)
                dve.wait_ge(rho_ready, 4 * (j + 1))
                s5link(V.tensor_tensor_scan(t1, rho4, t1, 0.0, ALU.mult, ALU.add))
                s5link(V.tensor_tensor_scan(t2, rho4, t2, 0.0, ALU.mult, ALU.add))
                if j:
                    dve.wait_ge(y_done, j)
                    dve.wait_ge(fin_ready, 4 * j)
                s5link(V.tensor_tensor(rho4, t2, tabs, ALU.mult))
                s5link(V.tensor_tensor(XR, t1, tabc, ALU.mult))
                V.tensor_tensor(XR, XR, rho4, ALU.subtract).then_inc(rotout_done, 1)
                dve.wait_ge(rotout_done, 2 * j + 1)
                s5link(V.tensor_tensor(rho4, t2, tabc, ALU.mult))
                s5link(V.tensor_tensor(XI, t1, tabs, ALU.mult))
                V.tensor_tensor(XI, XI, rho4, ALU.add).then_inc(rotout_done, 1)
                dve.wait_ge(rotout_done, 2 * j + 2)
                if j:
                    V.scalar_tensor_tensor(Z(ZU + j - 1), Z(ZU + j - 1), v(V_D + j - 1, 1), bank[7][:, 0:NT], ALU.mult, ALU.add).then_inc(yd_ready, 1)
                if j == 0:
                    dve.wait_ge(gate_done, 1)
                    dve.wait_ge(gb_full, 64)
                    V.tensor_scalar(ig[:, 0:NT], bank[7][0:H, 0:NT], gb[0:H, 0:1], None, ALU.add).then_inc(gate_rows, 1)
                    V.tensor_scalar(lf[:, 0:NT], bank[7][32:32 + H, 0:NT], gb[0:H, 1:2], 0.0, ALU.add, ALU.min).then_inc(gate_rows, 1)
                    V.tensor_scalar(tmpr[:, 0:NT], bank[7][32:32 + H, 0:NT], gb[0:H, 1:2], None, ALU.add).then_inc(gate_rows, 1)
                    dve.wait_ge(gate_rows, 3)
                    link(V.memset(m09[0:H, 0:1], 0.0))
                if j == 1:
                    dve.wait_ge(gate_act, 1)
                    st = c("start")[0:H, :]
                    link(V.tensor_tensor(lf[:, 0:NT], lf[:, 0:NT], tmpr[:, 0:NT], ALU.subtract))
                    link(V.tensor_tensor_scan(bb[:, 0:NT], st, lf[:, 0:NT], 0.0, ALU.mult, ALU.add))
                    link(V.tensor_copy(arow[:, 0:NT], ig[:, 0:NT]))
                    f0 = wrow[:, 0:9]
                    link(V.tensor_copy(f0[:, 0:1], lf[:, 0:1]))
                    link(V.tensor_copy(f0[:, 1:9], lf[:, NP_TOK:NT:LB]))
                    link(V.tensor_tensor(f0, f0, m09[0:H, :], ALU.add))
                    link(V.tensor_tensor(arow[:, 0:1], arow[:, 0:1], f0[:, 0:1], ALU.max))
                    link(V.tensor_tensor(arow[:, NP_TOK:NT:LB], arow[:, NP_TOK:NT:LB], f0[:, 1:9], ALU.max))
                    link(V.tensor_scalar(tmpr[:, 0:NT], st, -1.0, 3.0e38, ALU.add, ALU.mult))
                    link(V.tensor_tensor(lf[:, 0:NT], lf[:, 0:NT], tmpr[:, 0:NT], ALU.add))
                    link(V.tensor_tensor_scan(mm[:, 0:NT], lf[:, 0:NT], arow[:, 0:NT], 0.0, ALU.add, ALU.max))
                    link(V.tensor_tensor(rows[0:H, 0:NT], bb[:, 0:NT], mm[:, 0:NT], ALU.subtract))
                    link(V.tensor_tensor(arow[:, 0:NT], ig[:, 0:NT], bb[:, 0:NT], ALU.subtract))
                    r1 = rows[0:H, 0:NT]
                    r1s = r1[:, NP_TOK:NT].rearrange("p (b l) -> p b l", b=NB)
                    ars = arow[:, NP_TOK:NT].rearrange("p (b l) -> p b l", b=NB)
                    link(V.tensor_tensor(rows[0:H, 2 * NT:2 * NT + 64].rearrange("p (b l) -> p b l", b=NB), r1s,
                                         m09[0:H, 1:9].unsqueeze(2).to_broadcast([H, NB, LB]), ALU.add))
                    link(V.tensor_scalar(wrow[:, 0:NP_TOK], arow[:, 0:NP_TOK], r1[:, NP_TOK - 1:NP_TOK], None, ALU.add))
                    V.tensor_tensor(wrow[:, NP_TOK:NT].rearrange("p (b l) -> p b l", b=NB), ars,
                                    r1s[:, :, LB - 1:LB].to_broadcast([H, NB, LB]), ALU.add).then_inc(row_ready, 1)
            a_n = [0]

            def alink(ins):
                a_n[0] += 1
                ins.then_inc(att_d, 1)
                dve.wait_ge(att_d, a_n[0])

            def n0h(h):
                return n0T[:, 0:32].rearrange("p (b h) -> p b h", b=NB)[:, :, h:h + 1]

            def front(h):
                dve.wait_ge(E_done, h + 1)
                if h >= 2:
                    dve.wait_ge(N_done, h - 1)
                V.tensor_tensor(et2[h % 2], bank[2][:, 0:448], c("amask"), ALU.add).then_inc(em_ready, 1)
                if h == 0:
                    dve.wait_ge(kv_ready, 3 * 2 * H)
                V.tensor_tensor(vx2[h % 2], v_tok[:, 2, h * P:h * P + P].unsqueeze(1).to_broadcast([P, NB, P]),
                                c("seqm").unsqueeze(2).to_broadcast([P, NB, P]), ALU.mult).then_inc(vx_ready, 1)
                dve.wait_ge(bc_ready, h + 1)
                qw, qn = qw2[h % 2], qn2[h % 2]
                V.tensor_tensor(qw, Z(ZQ + h)[:, NP_TOK:NT], bc2[h % 2][:, NT:NT + 64], ALU.mult).then_inc(qw_ready, 1)
                dve.wait_ge(qw_ready, h + 1)
                V.tensor_tensor(qn.rearrange("p (b l) -> p b l", b=NB), qw.rearrange("p (b l) -> p b l", b=NB),
                                n0h(h).to_broadcast([P, NB, LB]), ALU.mult).then_inc(qn_ready, 1)

            def weigh_scores(h):
                dve.wait_ge(ex_ready, 3 * (h + 1))
                dve.wait_ge(S_done, h + 1)
                V.scalar_tensor_tensor(et2[h % 2], bank[3][:, 0:448], KSCALE, et2[h % 2], ALU.mult, ALU.mult).then_inc(P_ready, 1)

            dve.wait_ge(zeroed, 6)
            front(0)
            dve.wait_ge(y_done, NJ)
            V.scalar_tensor_tensor(Z(ZU + 3), Z(ZU + 3), v(V_D + 3, 1), bank[7][:, 0:NT], ALU.mult, ALU.add).then_inc(yd_ready, 1)
            weigh_scores(0)
            for n in range(4):
                dve.wait_ge(sgl_ready, 4 if n == 0 else n + 1)
                V.tensor_tensor(Z(ZU + n), Z(ZU + n), sgl[:, n * NT:n * NT + NT], ALU.mult).then_inc(ys_ready, 1)

            def gate_ssm(n):
                if n == 0:
                    dve.wait_ge(g_sig, 2)
                dve.wait_ge(up_done, n + 1)
                V.tensor_tensor(Z(ZGS + n), Z(ZGS + n), bank[1][:, 0:NT], ALU.mult).then_inc(up_dve, 1)

            for h in range(H):
                bc, bN = bc2[h % 2], bank[5]
                if h < H - 1:
                    front(h + 1)
                dve.wait_ge(abs_ready, h + 1)
                alink(V.tensor_tensor(den_a, den_a, bc[:, 0:NT], ALU.max))
                alink(V.reciprocal(den_a, den_a))
                if h < H - 1:
                    weigh_scores(h + 1)
                dve.wait_ge(N_done, h + 1)
                alink(V.tensor_tensor(den_a, bN[:, 0:NT], den_a, ALU.mult))
                if h == 0:
                    dve.wait_ge(g_sig, 1)
                V.tensor_tensor(Z(ZQ + h), den_a, Z(ZO + h), ALU.mult).then_inc(ym_ready, 1)
                dec = bc[:, NT:NT + 64].rearrange("p (b l) -> p b l", b=NB)[:, :, LB - 1:LB]
                dve.wait_ge(qn_ready, h + 1)
                alink(V.tensor_tensor(n0h(h), n0h(h), dec, ALU.mult))
                alink(V.tensor_tensor(n0h(h), n0h(h), bN[:, 448:456].unsqueeze(2), ALU.add))
                alink(V.tensor_copy(n0T[:, 32 + h:33 + h], bN[:, 456:457]))
                if h == 0:
                    dve.wait_ge(ys_ready, 4)
                V.tensor_copy(cp_rows[:, h * P:h * P + P], bN[:, NT:NT + P]).then_inc(cp_ready, 1)
                alink(V.tensor_tensor(C0[:, h], C0[:, h], dec.to_broadcast([P, NB, P]), ALU.mult))
                dve.wait_ge(C_done, 2 * h + 1)
                V.tensor_tensor(C0[:, h, 0:4], C0[:, h, 0:4], bank[7][:, :].rearrange("p (b e) -> p b e", b=4), ALU.add).then_inc(C_half, 1)
                gate_ssm(2 * h)
                dve.wait_ge(C_done, 2 * h + 2)
                V.tensor_tensor(C0[:, h, 4:8], C0[:, h, 4:8], bank[6][:, :].rearrange("p (b e) -> p b e", b=4), ALU.add).then_inc(C_ready, 1)
                gate_ssm(2 * h + 1)

            dve.wait_ge(g_sig, 3)
            dve.wait_ge(up_dve, KD)
            for n in range(KD):
                dve.wait_ge(up_done, KD + n + 1)
                V.tensor_tensor(Z(ZGM + n), Z(ZGM + n), bank[n % 4][:, 0:NT], ALU.mult).then_inc(up_dve, 1)
                dve.wait_ge(up_dve, KD + n + 1)
                V.tensor_tensor(Z(ZGS + n), Z(ZGS + n), Z(ZGM + n), ALU.add).then_inc(merged, 1)
            dve.wait_ge(res_full, 32)
            dve.wait_ge(zeroed, 13)
            for tt in range(TT):
                w = TW[tt]
                if tt == 2:
                    hnT_evac(1, 0, V_GFFN)
                for hf in range(2):
                    dve.wait_ge(out_done, min(2 * tt + hf + 1, 5))
                    A = acc[0:w, tt, 512 * hf:512 * hf + 512]
                    if tt == 2 and hf == 1:
                        dve.wait_ge(shifted, 1)
                        V.tensor_tensor(A, A, x3[0:64, 2, 512:1024], ALU.add).then_inc(h_ready, 1)
                    else:
                        if tt == 2:
                            dve.wait_ge(shifted, 1)
                        V.tensor_tensor(A, A, bank[4 + (2 * tt + hf) % 4][0:w, :], ALU.add).then_inc(h_ready, 1)
                if tt == 2:
                    hnT_evac(1, 1, V_GFFN)
                rms(1, tt, acc)
            hnT_evac(1, 2, V_GFFN)

            dve.wait_ge(rl_done, TT)
            for tt in range(TT):
                w = TW[tt]
                link(V.tensor_tensor(lg[0:w, tt, :], bank[6][0:w, 32 * tt:32 * tt + 32], brb[0:w, :], ALU.add))
            for tt in range(TT):
                link(V.max(mtop[:, tt, :], lg[:, tt, :]))

            def bce(x_):
                return x_.to_broadcast([P, TT, NE])

            link(V.tensor_tensor(gtm, lg, bce(mtop[:, :, 3:4]), ALU.is_gt))
            link(V.tensor_tensor(eqm, lg, bce(mtop[:, :, 3:4]), ALU.is_equal))
            link(V.reduce_sum(mcol[:, 0:3].unsqueeze(2), gtm, AX.X))
            link(V.tensor_scalar(mcol[:, 0:3], mcol[:, 0:3], -1.0, 4.5, ALU.mult, ALU.add))
            for tt in range(TT):
                link(V.tensor_tensor_scan(msk[:, tt, :], ones[:, 0:NE], eqm[:, tt, :], 0.0, ALU.mult, ALU.add))
            link(V.tensor_tensor(msk, msk, bce(mcol[:, 0:3].unsqueeze(2)), ALU.is_lt))
            link(V.tensor_tensor(msk, msk, eqm, ALU.mult))
            link(V.tensor_tensor(msk, msk, gtm, ALU.add))
            link(V.memset(msk[64:128, 2, :], 0.0))
            V.tensor_tensor(exw, lg, bce(mtop[:, :, 0:1]), ALU.subtract).then_inc(rl_ready, 1)
            dve.sem_inc(mask_ready, 1)
            def p_evac(n):
                dve.wait_ge(pw_done, n + 1)
                V.tensor_copy(p_lo[0:64, :], bank[4][0:64, 0:384]).then_inc(pw_ready, 1)
                V.tensor_copy(p_hi[64:128, :], bank[4][64:128, 0:384]).then_inc(pw_ready, 1)

            gffn = v(V_GFFN, 8)

            def select(e, base=None):
                V.tensor_tensor(sel, (c("slot") if base is None else base).unsqueeze(1).to_broadcast([P, TT, SLOTS]),
                                rk[:, :, bass.ds(e, 1)].to_broadcast([P, TT, SLOTS]), ALU.is_equal).then_inc(sel_ready, 1)

            def hot(e):
                V.tensor_copy(onehot, ident[:, bass.ds(e, 1)].to_broadcast([P, SLOTS])).then_inc(oh_ready, 1)

            def weigh(e, n):
                dve.wait_ge(sel_ready, n + 1)
                V.tensor_tensor(selw, sel.unsqueeze(2).to_broadcast([P, TT, 2, SLOTS]),
                                wt[:, :, bass.ds(e, 1)].unsqueeze(3).to_broadcast([P, TT, 2, SLOTS]), ALU.mult).then_inc(selw_ready, 1)

            def x_evac(n):
                dve.wait_ge(xsT_done, n + 1)
                V.tensor_tensor(xsT.rearrange("p (j a s) -> p a j s", j=4, a=2),
                                bank[2][:, :].rearrange("p (j a s) -> p a j s", j=4, a=2),
                                gffn.rearrange("p (a j) -> p a j", a=2).unsqueeze(3).to_broadcast([P, 2, 4, SLOTS]),
                                ALU.mult).then_inc(xsT_ready, 1)

            dve.wait_ge(rank_done, 1)
            link(V.memset(rk[:, :, NE:NE + 1], -1.0))
            link(V.tensor_scalar(rk[:, :, 0:NE], bank[5][:, 0:96].rearrange("p (t e) -> p t e", t=TT), 1.0, None, ALU.add))
            link(V.tensor_tensor(rk[:, :, 0:NE], rk[:, :, 0:NE], msk, ALU.mult))
            link(V.tensor_scalar(rk[:, :, 0:NE], rk[:, :, 0:NE], -1.0, None, ALU.add))
            select(0)
            hot(0)
            cntb = bank[5][:, 96:128]
            link(V.tensor_scalar(nov, cntb, float(SLOTS), None, ALU.is_gt))
            for r in range(2, 5):
                link(V.tensor_scalar(ind, cntb, float(SLOTS * r), None, ALU.is_gt))
                link(V.tensor_tensor(nov, nov, ind, ALU.add))
            link(V.tensor_tensor_scan(cinc, ones[:, 0:NE], nov, 0.0, ALU.mult, ALU.add))
            link(V.tensor_scalar(ind, cinc, c("pidx"), None, ALU.is_le))
            link(V.reduce_sum(opass[:, 0:1], ind, AX.X))
            link(V.tensor_scalar(opass[:, 0:1], opass[:, 0:1], float(NE - 1), None, ALU.min))
            link(V.tensor_tensor(ind, ind, nov, ALU.mult))
            link(V.reduce_sum(opass[:, 1:2], ind, AX.X))
            link(V.tensor_tensor(opass[:, 1:2], c("pidx"), opass[:, 1:2], ALU.subtract))
            link(V.tensor_scalar(opass[:, 1:2], opass[:, 1:2], 1.0, float(SLOTS), ALU.add, ALU.mult))
            link(V.tensor_scalar(dtab[:, 0:EXTRA], ident[:, 0:EXTRA], opass[:, 0:1], None, ALU.mult))
            V.tensor_scalar(dtab[:, EXTRA:2 * EXTRA], ident[:, 0:EXTRA], opass[:, 1:2], None, ALU.mult).then_inc(tab_made, 1)
            dve.wait_ge(rl_ready, 2)
            link(V.tensor_tensor(exw, exw, msk, ALU.mult))
            link(V.reduce_sum(mcol[:, 4:7].unsqueeze(2), exw, AX.X))
            link(V.tensor_scalar(mcol[:, 4:7], mcol[:, 4:7], 1e-30, None, ALU.max))
            link(V.reciprocal(mcol[:, 4:7], mcol[:, 4:7]))
            link(V.memset(wt[:, :, NE:NE + 1], 0.0))
            link(V.tensor_tensor(wt[:, :, 0:NE], exw, bce(mcol[:, 4:7].unsqueeze(2)), ALU.mult))
            V.tensor_copy(selw[:, :, :, 0:NE], wt[:, :, 0:NE].unsqueeze(2).to_broadcast([P, TT, 2, NE])).then_inc(selw_ready, 1)
            x_evac(0)
            p_evac(0)
            dve.wait_ge(ob_done, 1)
            link(V.tensor_copy(cnt_i[0:1, 0:1], cinc[0:1, NE - 1:NE]))
            link(V.tensor_copy(cnt_i[0:1, 1:1 + EXTRA], bank[6][0:1, 0:EXTRA]))
            link(V.tensor_copy(obase, bank[6][:, EXTRA:2 * EXTRA]))
            dve.sem_inc(cnt_ready, 1)
            dve.sem_inc(acc_add, 2)

            def swiglu(n):
                dve.wait_ge(g_done, n + 1)
                V.tensor_scalar(mg, bank[0][:, :], LIMIT, None, ALU.min).then_inc(g_ready, 1)
                dve.wait_ge(u_done, n + 1)
                V.tensor_scalar(mu, bank[1][:, :], LIMIT, -LIMIT, ALU.min, ALU.max).then_inc(u_ready, 1)
                dve.wait_ge(u_ready, n + 1)
                V.scalar_tensor_tensor(mu, mu, 1.0, mg, ALU.add, ALU.mult).then_inc(gu_ready, 1)
                dve.wait_ge(gu_ready, n + 1)
                dve.wait_ge(s_ready, n + 1)
                V.tensor_tensor(hb, mu, ms, ALU.mult).then_inc(hb_ready, 1)

            def accumulate(n):
                for m in range(6):
                    tt, hf = m // 2, m % 2
                    w = TW[tt]
                    dve.wait_ge(sc_done, n * 6 + m + 1)
                    A = acc[0:w, tt, 512 * hf:512 * hf + 512]
                    V.tensor_tensor(A, A, bank[6 + m % 2][0:w, :], ALU.add).then_inc(acc_add, 1)


            with dve.Fori(0, NE) as p:
                dve.wait_ge(gath_done, p + 1)
                weigh(p, p)
                dve.wait_ge(selw_ready, p + 2)
                select(p + 1)
                swiglu(p)
                hot(p + 1)
                accumulate(p)
                p_evac(p + 1)
                x_evac(p + 1)
            accumulate(NE)
            extra = dve.value_load(cnt_i[0:1, 0:1], min_val=0, max_val=EXTRA)
            with dve.If(extra > 0):
                with dve.Fori(0, extra) as q:
                    e = dve.value_load(cnt_i[0:1, bass.ds(q + 1, 1)], min_val=0, max_val=NE - 1)
                    V.tensor_scalar(islot, c("slot"), obase[:, bass.ds(q, 1)], None, ALU.add).then_inc(tab_made, 1)
                    dve.wait_ge(tab_made, q + 2)
                    select(e, islot)
                    hot(e)
                    weigh(e, q + (NE + 1))
                    x_evac(q + (NE + 1))
                    swiglu(q + NE)
                    p_evac(q + (NE + 1))
                    accumulate(q + (NE + 1))

            for tt in range(TT):
                dve.wait_ge(acc_add, extra * 6 + (6 * NE + 2 + 2 * (tt + 1)))
                rms(2, tt, acc)
            for tt in range(TT):
                hnT_evac(2, tt, V_GPLE)

            def final(tt):
                root(3, tt)
                if tt == 0:
                    dve.wait_ge(gfin_full, 16)
                V.scalar_tensor_tensor(acc[:, tt, :], acc[:, tt, :], rstd[:, tt:tt + 1], gfin, ALU.mult, ALU.mult).then_inc(out_ready, 1)

            for tt in range(TT):
                for hf in range(2):
                    cs = slice(512 * hf, 512 * hf + 512)
                    dve.wait_ge(gt_sig, 2 * tt + hf + 1)
                    link(V.tensor_tensor(x3[:, tt, cs], x3[:, tt, cs], pproj[tt][:, cs], ALU.mult))
                    V.tensor_tensor(acc[:, tt, cs], acc[:, tt, cs], x3[:, tt, cs], ALU.add).then_inc(fin_h, 1)
                if tt:
                    final(tt - 1)
            final(TT - 1)

        @block.tensor
        def _(pe):
            mm_, tr = nc.tensor.matmul, nc.tensor.transpose

            def transposes(r, tt):
                pe.wait_ge(xn_ready, TT * r + tt + 1)
                for b in range(2):
                    if tt == 2:
                        pe.wait_ge(hnT_ready, 6 * r + b + 1)
                    for k in range(4):
                        kk = 4 * b + k
                        last = tr(bank[(2 * tt + b) % 4][:, k * P:k * P + P], x3[:, tt, kk * P:kk * P + P], ident)
                    last.then_inc(xT_done, 1)

            pe.wait_ge(ident_full, 16)
            for tt in range(2):
                transposes(0, tt)
            pe.wait_ge(ldt_ready, 1)
            tr(bank[4][:, 0:80], vec_rows[0:80, :], ident[0:80, 0:80]).then_inc(vecT_done, 1)
            transposes(0, 2)

            def z_tile(n, beside=None):
                (s, use), half = z_slot(n // 2), n % 2
                if half == 0:
                    pe.wait_ge(slot_full[s], 16 * (use + 1))
                if n > ZGM:
                    pe.wait_ge(z_ready, n)
                elif n >= 4:
                    pe.wait_ge(z_ready, n - 3)
                wz = w3(s, KD, 256)
                for k in range(KD):
                    last = mm_(bank[z_bank(n)][:, 0:NT], wz[:, k, half * P:half * P + P], hn3[:, k, :], start=k == 0, stop=k == KD - 1)
                    if beside:
                        beside(k)
                last.then_inc(z_done, 1)

            pe.wait_ge(hnT_ready, 2 * TT)
            for n in range(4):
                z_tile(n)
            for n in range(4):
                pe.wait_ge(bx_ready, n + 1)
                if n == 0:
                    pe.wait_ge(vec_ready, 1)
                src = (Bx, Cx)[n // 2][:, 512 * (n % 2):512 * (n % 2) + 512]
                for j in range(NJ):
                    last = tr(bank[4 + n][:, j * P:j * P + P], src[:, j * P:j * P + P], ident)
                last.then_inc(bxT_done, 1)
            z_tile(4)
            pe.wait_ge(bct_ready, 4)
            pe.wait_ge(st_full, 48)
            tr(bank[4][:, 0:P], h0_rows_r, ident)
            tr(bank[4][:, P:2 * P], h0_rows_i, ident)
            tr(bank[4][:, 256:288], n_rows[0:32, :], ident[0:32, 0:32]).then_inc(stT_done, 1)
            z_tile(5)
            pe.wait_ge(stT_ready, 2)

            def bu(j):
                for q in range(8):
                    m = 8 * j + q
                    if q % 2 == 0:
                        pe.wait_ge(um_ready, 4 * j + q // 2 + 1)
                    if m >= 3:
                        pe.wait_ge(bu_ready, 8 * j + q - 2 if q >= 3 else 8 * j)
                    mm_(bank[4 + q % 3][:, 0:NT], BT[:, q % 2, j, :], um[:, (q // 2) * NT:(q // 2 + 1) * NT],
                        start=True, stop=True).then_inc(bu_done, 1)

            def y(j):
                pe.wait_ge(rotout_done, 2 * j + 2)
                if j:
                    pe.wait_ge(yd_ready, j)
                for n, X in enumerate((XR, XI)):
                    for i in range(NI):
                        last = mm_(bank[7][32 * i:32 * i + 32, 0:NT], CT[:, n, j, 32 * i:32 * i + 32],
                                   X[:, i * NT:(i + 1) * NT], start=n == 0, stop=n == 1)
                last.then_inc(y_done, 1)

            bu(0)
            pe.wait_ge(wif_full, 32)
            wif = att[:, 0:KD * 36].rearrange("p (k n) -> p k n", k=KD)
            for k in range(KD):
                last = mm_(bank[7][0:36, 0:NT], wif[:, k, :], hn3[:, k, :], start=k == 0, stop=k == KD - 1)
            last.then_inc(gate_done, 1)
            for j in range(NJ):
                if j == 1:
                    pe.wait_ge(gate_rows, 3)
                if j:
                    y(j - 1)
                for n in ZSTAGE[j][:2]:
                    z_tile(n)
                if j == 2:
                    pe.wait_ge(R_ready, 3)
                    pe.wait_ge(bu_ready, 24)
                    for n, src in enumerate((arow, wrow)):
                        for tt in range(TT):
                            last = tr(bank[4][:, 12 * n + H * tt:12 * n + H * tt + H], src[:, tt * P:tt * P + P], ident[0:H, 0:H])
                    last.then_inc(asT_done, 1)
                if j == NJ - 1:
                    pe.wait_ge(bu_ready, 8 * NJ)
                    for g in range(2 * H):
                        if g >= 3:
                            pe.wait_ge(kv_ready, TT * (g - 2))
                        for tt in range(TT):
                            w = TW[tt]
                            src = Z((ZK if g < H else ZV) + g % H)
                            last = tr(bank[4 + g % 3][0:w, tt * P:tt * P + P], src[:, tt * P:tt * P + w], ident)
                        last.then_inc(kvT_done, 1)
                for n in ZSTAGE[j][2:]:
                    z_tile(n)
                if j < NJ - 1:
                    if j == 2:
                        pe.wait_ge(asT_ready, 2)
                    bu(j + 1)
            selh = c("sel")
            blocks = ((0, 256, 0, 256), (256, 384, 128, 256), (384, 448, 256, 320))

            def front(h):
                sh = selh[:, h * P:h * P + P]
                if h == 0:
                    pe.wait_ge(z_ready, ZGM)
                    pe.wait_ge(kv_ready, TT * 2 * H)
                else:
                    pe.wait_ge(em_ready, h)
                    pe.wait_ge(bc_ready, h)
                    pe.wait_ge(P_ready, h)
                for c0, c1, a0, a1 in blocks:
                    last = mm_(bank[2][:, c0:c1], sh, rows[:, a0:a1], start=True, stop=True)
                last.then_inc(E_done, 1)
                mm_(bank[4][:, 0:384], sh, rows[:, NT:2 * NT + 64], start=True, stop=True).then_inc(bc_done, 1)
                qT_, kT_ = Z(ZQ + h), Z(ZK + h)
                mm_(bank[3][:, 0:256], kT_[:, 0:128], qT_[:, 0:256], start=True, stop=True)
                mm_(bank[3][:, 256:384], kT_[:, 128:256], qT_[:, 128:256], start=True, stop=True)
                mm_(bank[3][:, 384:448], zT[:, (ZK + h) * NT + 256:(ZK + h) * NT + 384], qT_[:, 256:320], start=True, stop=True).then_inc(S_done, 1)

            def up(n, s, src, bank_):
                for k in range(4):
                    last = mm_(bank_[:, 0:NT], w3(s[k // 2], 2, D)[:, k % 2, n * P:n * P + P], Z(src + k), start=k == 0, stop=k == 3)
                last.then_inc(up_done, 1)

            front(0)
            y(NJ - 1)
            z_tile(ZGM)
            pe.wait_ge(fin_ready, 4 * NJ)
            pe.wait_ge(yd_ready, NJ)
            for n in range(2):
                tr(bank[7][:, n * P:n * P + P], fin_s[:, n * P:n * P + P], ident).then_inc(finT_done, 1)
            tr(bank[7][0:32, 2 * P:3 * P], fin_p, ident).then_inc(finT_done, 1)
            pe.wait_ge(gelu_ready, 4)
            pe.wait_ge(slot_full[3], 16 * 3)
            wg = w3(3, 4, 512)
            for n in range(4):
                if n == 3:
                    pe.wait_ge(z_ready, ZGM + 1)
                for k in range(4):
                    last = mm_(bank[GLU_BANK[n]][:, 0:NT], wg[:, k, n * P:n * P + P], Z(ZU + k), start=k == 0, stop=k == 3)
                last.then_inc(glu_done, 1)
            pe.wait_ge(sgl_ready, 4)

            for h in range(H):
                et, qw, qn = et2[h % 2], qw2[h % 2], qn2[h % 2]
                pe.wait_ge(P_ready, h + 1)
                pe.wait_ge(qn_ready, h + 1)
                if h:
                    pe.wait_ge(C_ready, h)
                bD = bank[6]
                mm_(bD[:, 0:256], ones, et[:, 0:256], start=True, stop=False)
                mm_(bD[:, 128:256], ones, et[:, 256:384], start=False, stop=True)
                mm_(bD[:, 256:320], ones, et[:, 384:448], start=True, stop=False)
                mm_(bD[:, 256:320], ones, qn, start=False, stop=True).then_inc(den_done, 1)
                if h < H - 1:
                    front(h + 1)
                vh = [v_tok[:, tt, h * P:h * P + P] for tt in range(TT)]
                k2 = [kw_all[:, h * 384 + tt * P:h * 384 + tt * P + P] for tt in range(TT)]
                bN = bank[5]
                if h == 0:
                    pe.wait_ge(c0_full, 16 * H)
                else:
                    pe.wait_ge(cp_ready, h)
                    pe.wait_ge(C_half, h)
                mm_(bN[:, NT:NT + P], k2[0], vh[0], start=True, stop=False)
                mm_(bN[:, NT:NT + P], k2[1], vh[1], start=False, stop=True)
                mm_(bN[:, 448:456], k2[2], c("seqm"), start=True, stop=True)
                mm_(bN[:, 456:457], k2[0], ones[:, 0:1], start=True, stop=False)
                mm_(bN[:, 456:457], k2[1], ones[:, 0:1], start=False, stop=True)
                mm_(bN[:, 0:256], vh[0], et[:, 0:256], start=True, stop=False)
                mm_(bN[:, 128:256], vh[1], et[:, 256:384], start=False, stop=True)
                mm_(bN[:, 256:320], vh[2], et[:, 384:448], start=True, stop=False)

                def old_state(b):
                    ins = mm_(bN[:, 256 + LB * b:264 + LB * b], C0[:, h, b], qw[:, LB * b:LB * b + LB], start=False, stop=b == NB - 1)
                    if b == NB - 1:
                        ins.then_inc(N_done, 1)

                z_tile(ZHEAD[h][0], old_state)
                pe.wait_ge(vx_ready, h + 1)
                if h == 0:
                    pe.wait_ge(finT_ready, 3)
                mm_(bank[7][:, :], k2[2], vx2[h % 2][:, 0:4].rearrange("p b e -> p (b e)"), start=True, stop=True).then_inc(C_done, 1)
                if h == 0:
                    pe.wait_ge(ys_ready, 4)
                    for s in (4, 5):
                        pe.wait_ge(slot_full[s], 16 * 3)
                else:
                    pe.wait_ge(up_dve, 2 * h)
                up(2 * h, (4, 5), ZU, bank[1])
                pe.wait_ge(abs_ready, h + 1)
                mm_(bank[6][:, :], k2[2], vx2[h % 2][:, 4:8].rearrange("p b e -> p (b e)"), start=True, stop=True).then_inc(C_done, 1)
                for n in ZHEAD[h][1:]:
                    z_tile(n)
                pe.wait_ge(up_dve, 2 * h + 1)
                up(2 * h + 1, (4, 5), ZU, bank[1])

            pe.wait_ge(ym_ready, H)
            pe.wait_ge(P_ready, H)
            pe.wait_ge(z_ready, ZT)
            pe.wait_ge(up_dve, KD)
            pe.wait_ge(slot_full[3], 16 * 4)
            pe.wait_ge(slot_full[0], 16 * 5)
            for n in range(KD):
                if n >= 4:
                    pe.wait_ge(up_dve, KD + n - 3)
                up(n, (3, 0), ZQ, bank[n % 4])
                if n == 3:
                    pe.wait_ge(C_ready, H)
                    tr(bank[4][0:36, 0:P], n0T, ident).then_inc(nT_done, 1)
            pe.wait_ge(merged, KD)
            pe.wait_ge(nT_ready, 1)
            pe.wait_ge(cp_ready, H)
            wr3 = wr_sb.rearrange("p (k e) -> p k e", k=KD)

            def token_halves(n):
                return (n % 2,) if n < 4 else (0, 1)

            def half_bank(n, hf):
                return bank[4 + n % 4][:, :] if n < 4 else bank[4][64 * hf:64 * hf + 64, :]

            def out_tile(tt):
                for n in (2 * tt, 2 * tt + 1)[:2 if tt < 2 else 1]:
                    if n == 4:
                        pe.wait_ge(h_ready, 1)
                    for k in range(KD):
                        if n == 0 and k % 2 == 0:
                            pe.wait_ge(slot_full[WOUT[k // 2]], 16)
                        for hf in token_halves(n):
                            last = mm_(half_bank(n, hf), Z(ZGS + k)[:, tt * P:tt * P + TW[tt]],
                                       w3(WOUT[k // 2], 2, D)[:, k % 2, 512 * hf:512 * hf + 512], start=k == 0, stop=k == KD - 1)
                    last.then_inc(out_done, 1)

            def logits(tt):
                w = TW[tt]
                pe.wait_ge(hnT_ready, 6 + 2 * tt + 2)
                if tt == 0:
                    pe.wait_ge(wr_full, 16)
                    pe.wait_ge(h_ready, 3)
                for k in range(KD):
                    last = mm_(bank[6][0:w, 32 * tt:32 * tt + 32], hn3[:, k, tt * P:tt * P + w], wr3[:, k, :], start=k == 0, stop=k == KD - 1)
                last.then_inc(rl_done, 1)

            out_tile(0)
            out_tile(1)
            transposes(1, 0)
            out_tile(2)
            transposes(1, 1)
            logits(0)
            logits(1)
            transposes(1, 2)
            pe.wait_ge(ple_full, 32)
            pe.wait_ge(hnT_ready, 6 + 4)
            pe.wait_ge(stored_pool, 16 * 9)
            for k in range(2):
                if k == 0:
                    pe.wait_ge(hnT_ready, 6 + 5)
                else:
                    logits(2)
                for tt in range(TT):
                    w = TW[tt]
                    last = tr(bank[k][:, tt * P:tt * P + w], p_tok[0:w, tt, k * P:k * P + P], ident[0:w, 0:w])
                last.then_inc(pTt_done, 1)
            pe.wait_ge(pT_ready, 2)
            pe.wait_ge(slot_full[11], 16 * 2)

            def ple_proj(n):
                tt, hf = n // 2, n % 2
                if n >= 4:
                    pe.wait_ge(pj_ready, n - 3)
                for k in range(2):
                    last = mm_(bank[PJ_BANK[n % 4]][:, :], pT[:, k, tt * P:tt * P + P], w3(11, 2, D)[:, k, 512 * hf:512 * hf + 512], start=k == 0, stop=k == 1)
                last.then_inc(pj_done, 1)

            ple_proj(0)
            ple_proj(1)
            pe.wait_ge(mask_ready, 1)
            tri = c("triu")
            for tt in range(TT):
                for s in range(tt + 1):
                    mm_(bank[5][:, 32 * tt:32 * tt + 32], tri if s == tt else ones, msk[:, s, :], start=s == 0, stop=s == tt)
            for s in range(TT):
                last = mm_(bank[5][:, 96:128], ones, msk[:, s, :], start=s == 0, stop=s == TT - 1)
            last.then_inc(rank_done, 1)
            def gather(n):
                pe.wait_ge(sel_ready, n + 1)
                for tt in range(TT):
                    for hf in range(2):
                        last = mm_(bank[2][64 * hf:64 * hf + 64, :], sel[:, tt, :], x3[:, tt, 512 * hf:512 * hf + 512],
                                   start=tt == 0, stop=tt == TT - 1)
                last.then_inc(gath_done, 1)

            def gather_T(n):
                pe.wait_ge(xs_ready, n + 1)
                for j in range(4):
                    last = tr(bank[2][:, j * P:j * P + P], xs[:, j * P:j * P + P], ident)
                last.then_inc(xsT_done, 1)

            def weights_T(n):
                pe.wait_ge(selw_ready, n + 1)
                for tt in range(TT):
                    last = tr(bank[4][:, tt * P:tt * P + P], selw[:, tt].rearrange("p a s -> p (a s)"), ident)
                last.then_inc(pw_done, 1)

            ple_proj(2)
            gather(0)
            ple_proj(3)
            ple_proj(4)
            gather_T(0)
            pe.wait_ge(tab_made, 1)
            mm_(bank[6][:, 0:2 * EXTRA], ones, dtab, start=True, stop=True).then_inc(ob_done, 1)
            ple_proj(5)
            weights_T(0)
            pe.wait_ge(pw_ready, 2)
            pe.wait_ge(bt_full, 64)
            pe.wait_ge(pj_ready, 6)

            def project(n, s0, srcT, dst, done, bias=None):
                for hf in range(2 if bias is not None else 0):
                    mm_(dst[64 * hf:64 * hf + 64, :], onehot, btab[bias][:, 512 * hf:512 * hf + 512], start=True, stop=False)
                for k in range(KD):
                    s = s0 + k // 2
                    if k % 2 == 0:
                        pe.wait_ge(slot_full[s], n * 16 + 16 * (USED0[s] + 1))
                    for hf in range(2):
                        last = mm_(dst[64 * hf:64 * hf + 64, :], srcT[:, (k % 4) * P + 64 * (k // 4):(k % 4) * P + 64 * (k // 4) + 64],
                                   w3(s, 2, D)[:, k % 2, 512 * hf:512 * hf + 512], start=bias is None and k == 0, stop=k == KD - 1)
                    if k % 2:
                        last.then_inc(slot_free[3 * (s // 4) + s % 4] if k < KD - 1 else done, 1)
            def scatter(n):
                pe.wait_ge(y_ready, n + 1)
                for m in range(6):
                    tt, hf = m // 2, m % 2
                    w = TW[tt]
                    pe.wait_ge(acc_add, n * 6 + (m + 1))
                    mm_(bank[6 + m % 2][0:w, :], (p_lo, p_hi)[hf][:, tt * P:tt * P + w], yb, start=True, stop=True).then_inc(sc_done, 1)

            def gate_up(n, picked):
                pe.wait_ge(xsT_ready, picked)
                pe.wait_ge(oh_ready, picked)
                project(n, 0, xsT, bank[0], g_done, bias=0)
                project(n, 4, xsT, bank[1], u_done, bias=1)

            def hidden_T(n):
                pe.wait_ge(hb_ready, n + 1)
                for j in range(4):
                    last = tr(bank[3][:, j * P:j * P + P], hb[:, j * P:j * P + P], ident)
                last.then_inc(hTt_done, 1)

            def down(n):
                pe.wait_ge(hT_ready, n + 1)
                project(n, 8, hT, bank[5], dn_done)

            with pe.Fori(0, NE) as p:
                gate_up(p, p + 1)
                gather(p + 1)
                scatter(p)
                weights_T(p + 1)
                hidden_T(p)
                gather_T(p + 1)
                down(p)
            pe.wait_ge(pw_ready, 2 * (NE + 1))
            scatter(NE)
            pe.wait_ge(cnt_ready, 1)
            extra = pe.value_load(cnt_i[0:1, 0:1], min_val=0, max_val=EXTRA)
            with pe.If(extra > 0):
                with pe.Fori(0, extra) as q:
                    gather(q + (NE + 1))
                    gather_T(q + (NE + 1))
                    gate_up(q + NE, q + (NE + 2))
                    weights_T(q + (NE + 1))
                    hidden_T(q + NE)
                    down(q + NE)
                    pe.wait_ge(pw_ready, q * 2 + 2 * (NE + 2))
                    scatter(q + (NE + 1))

            def ple_gate(tt):
                w = TW[tt]
                pe.wait_ge(hnT_ready, 6 * 2 + 2 * tt + 2)
                if tt == 1:
                    pe.wait_ge(acc_add, extra * 6 + (6 * (NE + 1) + 2))
                for n in (2 * tt, 2 * tt + 1)[:2 if tt < 2 else 1]:
                    if n == 4:
                        pe.wait_ge(gt_sig, 1)
                    for k in range(KD):
                        if n == 0 and k % 2 == 0:
                            pe.wait_ge(slot_full[k // 2], extra * 16 + 16 * (USED0[k // 2] + NE + 1))
                        for hf in token_halves(n):
                            last = mm_(half_bank(n, hf), hn3[:, k, tt * P:tt * P + TW[tt]],
                                       w3(k // 2, 2, D)[:, k % 2, 512 * hf:512 * hf + 512], start=k == 0, stop=k == KD - 1)
                    last.then_inc(gt_done, 1)

            transposes(2, 0)
            transposes(2, 1)
            ple_gate(0)
            transposes(2, 2)
            ple_gate(1)
            ple_gate(2)


def constants():
    import numpy as np
    c = np.zeros((P, CONST_W), np.float32)

    def put(name, a):
        c[:, CONST[name][0]:CONST[name][1]] = a

    p = np.arange(P)
    n = np.arange(NT)
    put("ident", np.eye(P))
    put("ones", 1.0)
    put("triu", p[:, None] < p[None, :])
    put("slot", np.arange(SLOTS)[None])
    put("tloc", np.where(n < NP_TOK, n, (n - NP_TOK) % LB)[None])
    m = np.full((P, 448), -1.0e30, np.float32)
    m[:, 0:256][p[:, None] <= np.arange(256)[None]] = 0.0
    m[:, 256:384][p[:, None] <= p[None]] = 0.0
    q = np.arange(64)
    ok = (q[:, None] // LB == q[None] // LB) & (q[:, None] <= q[None])
    m[0:64, 384:448][ok] = 0.0
    put("amask", m)
    put("seqm", (p[:, None] // LB == np.arange(NB)[None]))
    put("half", (p[:, None] // 64 == np.arange(2)[None]))
    put("par", (p[:, None] // GW % 2 == np.arange(2)[None]))
    put("npar", -1.0 * (p[:, None] // GW % 2 == np.arange(2)[None]))
    put("imask", (p[:, None] // 32 == np.arange(NI)[None]))
    put("start", np.where((n == 0) | ((n >= NP_TOK) & ((n - NP_TOK) % LB == 0)), 0.0, 1.0)[None])
    put("sel", (p[:, None] == np.arange(H * P)[None] // P))
    put("pidx", p[:, None])
    put("halfpi", np.float32(1.5707963))
    return c


_INS = ["x_prompt", "x_sample", "p_prompt", "p_sample", "state_ssm_re", "state_ssm_im", "state_ml_c", "state_ml_n",
        "state_ml_m", "g_mix", "w_in", "ssm_a_re", "ssm_a_im", "ssm_log_dt", "ssm_b_re", "ssm_b_im", "ssm_c_re",
        "ssm_c_im", "ssm_d", "ssm_w_glu", "ssm_b_glu", "ml_b_ig", "ml_b_fg", "w_ssm_up", "w_ml_up", "w_out", "g_ffn",
        "w_router", "b_router", "w_gate", "b_gate", "w_up", "b_up", "w_down", "b_down", "g_ple", "w_ple_gate",
        "w_ple_proj", "g_final"]
_OUTS = [("yp", (1, 256, 1024)), ("ys", (8, 8, 1024)), ("rp", (1, 1, 32, 64)), ("ip", (1, 1, 32, 64)),
         ("cp", (1, 1, 4, 128, 128)), ("np", (1, 1, 4, 128)), ("mp", (1, 1, 4)), ("rs", (1, 8, 32, 64)),
         ("is", (1, 8, 32, 64)), ("cs", (1, 8, 4, 128, 128)), ("ns", (1, 8, 4, 128)), ("ms", (1, 8, 4))]


def kernel(**inputs):
    import numpy as np
    import concourse.bacc as bacc
    from concourse.bass_utils import run_bass_kernel_spmd

    nc = bacc.Bacc("TRN2", target_bir_lowering=False, num_devices=1)
    arrays, t, o = {}, {}, {}
    for name in _INS:
        arrays[name] = np.ascontiguousarray(inputs[name])
    arrays["cst"] = constants()
    for name, a in arrays.items():
        t[name] = nc.dram_tensor("in_" + name, a.shape, mybir.dt.from_np(a.dtype), kind="ExternalInput").ap()
    for name, shape in _OUTS:
        o[name] = nc.dram_tensor("out_" + name, shape, F32, kind="ExternalOutput").ap()
    hybrid_step(nc, t, o)
    r = run_bass_kernel_spmd(nc, [{"in_" + k: a for k, a in arrays.items()}], core_ids=[0])
    return tuple(r.results[0]["out_" + name] for name, _ in _OUTS)
```
